# Optimizing a Trainium2 kernel written in Bass

```python
import math
import jax, jax.numpy as jnp
from jax import lax
import numpy as np

D_MODEL = 2048
BATCH = 1
SEQ = 256
DEPTH = 2

N_MIXERS = 2
N_RET_LAYERS = (DEPTH + 1) // 2
N_POOL_LAYERS = DEPTH // 2
EPS = 1e-6

N_RET_HEADS = 8
RET_QK_DIM = D_MODEL
RET_V_DIM = 2 * D_MODEL
RET_HEAD_QK = RET_QK_DIM // N_RET_HEADS
RET_HEAD_V = RET_V_DIM // N_RET_HEADS
RET_GATE_DIM = RET_V_DIM
RET_IN_COLS = 2 * RET_QK_DIM + RET_V_DIM + RET_GATE_DIM
RET_CHUNK = 128
ROPE_BASE = 10000.0

POOL_WIDTH = 2 * D_MODEL
POOL_WINDOWS = (2, 4, 8, 16)
POOL_GROUPS = len(POOL_WINDOWS)
POOL_GROUP_DIM = POOL_WIDTH // POOL_GROUPS


def rms_norm(x, g):
    xf = x.astype(jnp.float32)
    y = xf * lax.rsqrt(jnp.mean(xf * xf, axis=-1, keepdims=True) + EPS)
    return (y * g.astype(jnp.float32)).astype(x.dtype)

def rope(x, seq_len):
    d = x.shape[-1]
    half = d // 2
    inv = ROPE_BASE ** (-jnp.arange(half, dtype=jnp.float32) / half)
    ang = jnp.arange(seq_len, dtype=jnp.float32)[:, None] * inv[None, :]
    cos = jnp.cos(ang)[None, :, None, :]
    sin = jnp.sin(ang)[None, :, None, :]
    x1, x2 = x[..., :half], x[..., half:]
    return jnp.concatenate([x1 * cos - x2 * sin, x1 * sin + x2 * cos], axis=-1)

def retention_log_decay():
    h = jnp.arange(N_RET_HEADS, dtype=jnp.float32)
    return jnp.log1p(-jnp.exp2(-5.0 - h))

def chunkwise_retention(q, k, v):
    B, S, H, dk = q.shape
    dv = v.shape[-1]
    C = RET_CHUNK
    NC = S // C
    lg = retention_log_decay()
    idx = jnp.arange(C, dtype=jnp.float32)
    diff = idx[:, None] - idx[None, :]
    mask = jnp.where(diff[None] >= 0,
                     jnp.exp(jnp.maximum(diff, 0.0)[None] * lg[:, None, None]), 0.0)
    q_decay = jnp.exp((idx[None, :] + 1.0) * lg[:, None])
    k_decay = jnp.exp((C - 1.0 - idx[None, :]) * lg[:, None])
    chunk_decay = jnp.exp(C * lg)

    def to_chunks(t):
        return t.reshape(B, NC, C, H, t.shape[-1]).transpose(1, 0, 3, 2, 4)

    qc, kc, vc = to_chunks(q), to_chunks(k), to_chunks(v)

    def body(state, inp):
        qi, ki, vi = inp
        scores = jnp.einsum('bhid,bhjd->bhij', qi, ki) * mask[None]
        inner = jnp.einsum('bhij,bhje->bhie', scores, vi)
        cross = jnp.einsum('bhid,bhde->bhie', qi * q_decay[None, :, :, None], state)
        new_state = (chunk_decay[None, :, None, None] * state
                     + jnp.einsum('bhjd,bhje->bhde', ki * k_decay[None, :, :, None], vi))
        return new_state, inner + cross

    state0 = jnp.zeros((B, H, dk, dv), jnp.float32)
    _, out = lax.scan(body, state0, (qc, kc, vc))
    return out.transpose(1, 0, 3, 2, 4).reshape(B, S, H, dv)

def retention_layer(x, g_norm, w_in, gn, w_out):
    B, S, _ = x.shape
    h = rms_norm(x, g_norm)
    p = h @ w_in
    q, k, v, z = jnp.split(p, [RET_QK_DIM, 2 * RET_QK_DIM, 2 * RET_QK_DIM + RET_V_DIM], axis=-1)
    q = rope(q.astype(jnp.float32).reshape(B, S, N_RET_HEADS, RET_HEAD_QK), S)
    k = rope(k.astype(jnp.float32).reshape(B, S, N_RET_HEADS, RET_HEAD_QK), S) * (RET_HEAD_QK ** -0.5)
    v = v.astype(jnp.float32).reshape(B, S, N_RET_HEADS, RET_HEAD_V)
    o = chunkwise_retention(q, k, v)
    mu = jnp.mean(o, axis=-1, keepdims=True)
    var = jnp.mean(jnp.square(o - mu), axis=-1, keepdims=True)
    o = ((o - mu) * lax.rsqrt(var + EPS)).reshape(B, S, RET_V_DIM) * gn.astype(jnp.float32)
    o = o.astype(x.dtype) * jax.nn.silu(z)
    return o @ w_out

def pooling_layer(x, g_norm, w_in, w_grp, b_grp, scale, w_out):
    B, S, _ = x.shape
    h = rms_norm(x, g_norm)
    p = h @ w_in
    u, z = jnp.split(p, [POOL_WIDTH], axis=-1)
    u = u.reshape(B, S, POOL_GROUPS, POOL_GROUP_DIM)
    uf = u.astype(jnp.float32)
    cs = jnp.concatenate([jnp.zeros((B, 1, POOL_GROUPS, POOL_GROUP_DIM), jnp.float32),
                          jnp.cumsum(uf, axis=1)], axis=1)
    t = jnp.arange(S)
    pooled = []
    for gi, w in enumerate(POOL_WINDOWS):
        lo = jnp.maximum(t + 1 - w, 0)
        cnt = jnp.minimum(t + 1, w).astype(jnp.float32)[None, :, None]
        win_sum = cs[:, 1:, gi] - jnp.take(cs[:, :, gi], lo, axis=1)
        pooled.append(win_sum / cnt)
    pooled = jnp.stack(pooled, axis=2)
    mix = (pooled - uf).astype(x.dtype)
    mix = jnp.einsum('bsgc,gcd->bsgd', mix, w_grp) + b_grp
    mix = mix.reshape(B, S, POOL_WIDTH) * scale
    return (mix * jax.nn.silu(z)) @ w_out

def first_inputs(seed: int = 0) -> dict:
    key = jax.random.key(seed)
    ks = jax.random.split(key, 13)
    f32 = jnp.float32
    nr, npl = N_RET_LAYERS, N_POOL_LAYERS
    return {
        "x": jax.random.normal(ks[0], (BATCH, SEQ, D_MODEL), f32),
        "ret_norm": 1.0 + 0.05 * jax.random.normal(ks[1], (nr, D_MODEL), f32),
        "ret_w_in": jax.random.normal(ks[2], (nr, D_MODEL, RET_IN_COLS), f32) * D_MODEL ** -0.5,
        "ret_gn": 1.0 + 0.05 * jax.random.normal(ks[3], (nr, RET_V_DIM), f32),
        "ret_w_out": jax.random.normal(ks[4], (nr, RET_V_DIM, D_MODEL), f32) * RET_V_DIM ** -0.5,
        "pool_norm": 1.0 + 0.05 * jax.random.normal(ks[5], (npl, D_MODEL), f32),
        "pool_w_in": jax.random.normal(ks[6], (npl, D_MODEL, 2 * POOL_WIDTH), f32) * D_MODEL ** -0.5,
        "pool_w_grp": jax.random.normal(ks[7], (npl, POOL_GROUPS, POOL_GROUP_DIM, POOL_GROUP_DIM), f32) * POOL_GROUP_DIM ** -0.5,
        "pool_b_grp": 0.01 * jax.random.normal(ks[8], (npl, POOL_GROUPS, POOL_GROUP_DIM), f32),
        "pool_scale": 1.0 + 0.1 * jax.random.normal(ks[9], (npl, POOL_WIDTH), f32),
        "pool_w_out": jax.random.normal(ks[10], (npl, POOL_WIDTH, D_MODEL), f32) * POOL_WIDTH ** -0.5,
        "final_norm": 1.0 + 0.05 * jax.random.normal(ks[11], (D_MODEL,), f32),
    }

def first_block(x, ret_norm, ret_w_in, ret_gn, ret_w_out, pool_norm, pool_w_in,
              pool_w_grp, pool_b_grp, pool_scale, pool_w_out, final_norm):
    h = x
    for i in range(DEPTH):
        j = i // N_MIXERS
        if i % N_MIXERS == 0:
            h = h + retention_layer(h, ret_norm[j], ret_w_in[j], ret_gn[j], ret_w_out[j])
        else:
            h = h + pooling_layer(h, pool_norm[j], pool_w_in[j], pool_w_grp[j],
                                  pool_b_grp[j], pool_scale[j], pool_w_out[j])
    return rms_norm(h, final_norm)


DEPTH_2 = 1

CHUNK = 64
PLE_DIM = 256
DN_HEADS = 16
DN_HEAD_DIM = 128
DN_WIDTH = DN_HEADS * DN_HEAD_DIM
SHORT_CONV = 4
CONV_CH = D_MODEL
CONV_KERNEL = 31
N_BRANCHES = 2
IN_SIZES = (3 * DN_WIDTH,
            DN_WIDTH,
            DN_HEADS,
            DN_HEADS,
            2 * CONV_CH,
            CONV_CH,
            N_BRANCHES * D_MODEL)
IN_COLS = sum(IN_SIZES)


def _split_points():
    return np.cumsum(np.array(IN_SIZES))[:-1].tolist()

def rmsnorm(x, g):
    xf = x.astype(jnp.float32)
    y = xf * lax.rsqrt(jnp.mean(xf * xf, axis=-1, keepdims=True) + EPS)
    return (y * g.astype(jnp.float32)).astype(x.dtype)

def layernorm(x, g, b):
    xf = x.astype(jnp.float32)
    mu = jnp.mean(xf, axis=-1, keepdims=True)
    var = jnp.mean(jnp.square(xf - mu), axis=-1, keepdims=True)
    y = (xf - mu) * lax.rsqrt(var + EPS)
    return (y * g.astype(jnp.float32) + b.astype(jnp.float32)).astype(x.dtype)

def l2norm(x):
    return x * lax.rsqrt(jnp.sum(x * x, axis=-1, keepdims=True) + EPS)

def causal_depthwise_conv(x, w):
    K = w.shape[0]
    xp = jnp.pad(x, ((0, 0), (K - 1, 0), (0, 0)))
    return lax.conv_general_dilated(
        xp, w[:, None, :].astype(x.dtype), window_strides=(1,), padding='VALID',
        dimension_numbers=('NWC', 'WIO', 'NWC'), feature_group_count=x.shape[-1])

def gated_delta_chunked(q, k, v, g, beta):
    B, S, H, Dk = q.shape
    nc = S // CHUNK

    def to_chunks(t):
        t = t.reshape((B, nc, CHUNK, H) + t.shape[3:])
        return jnp.moveaxis(t, 3, 1)

    q, k, v = to_chunks(q) * (Dk ** -0.5), to_chunks(k), to_chunks(v)
    g, beta = to_chunks(g), to_chunks(beta)
    gc = jnp.cumsum(g, axis=-1)
    idx = jnp.arange(CHUNK)
    causal = idx[:, None] >= idx[None, :]
    strict = idx[:, None] > idx[None, :]
    decay = jnp.exp(jnp.where(causal, gc[..., :, None] - gc[..., None, :], -jnp.inf))
    kb = k * beta[..., None]
    A = jnp.einsum('bhnid,bhnjd->bhnij', kb, k) * decay * strict
    eye = jnp.eye(CHUNK, dtype=jnp.float32)
    T = lax.linalg.triangular_solve(eye + A, jnp.broadcast_to(eye, A.shape),
                                    left_side=True, lower=True, unit_diagonal=True)
    u = jnp.einsum('bhnij,bhnjd->bhnid', T, v * beta[..., None])
    w = jnp.einsum('bhnij,bhnjd->bhnid', T, kb * jnp.exp(gc)[..., None])
    qk = jnp.einsum('bhnid,bhnjd->bhnij', q, k) * decay
    q_dec = q * jnp.exp(gc)[..., None]
    g_last = gc[..., -1]
    k_end = k * jnp.exp(g_last[..., None] - gc)[..., None]
    xs = tuple(jnp.moveaxis(t, 2, 0) for t in (u, w, qk, q_dec, k_end, g_last))

    def step(Sst, inp):
        u_n, w_n, qk_n, qd_n, ke_n, gl_n = inp
        v_new = u_n - jnp.einsum('bhid,bhde->bhie', w_n, Sst)
        o = jnp.einsum('bhid,bhde->bhie', qd_n, Sst) + jnp.einsum('bhij,bhje->bhie', qk_n, v_new)
        Sst = Sst * jnp.exp(gl_n)[..., None, None] + jnp.einsum('bhid,bhie->bhde', ke_n, v_new)
        return Sst, o

    S0 = jnp.zeros((B, H, Dk, v.shape[-1]), jnp.float32)
    _, o = lax.scan(step, S0, xs)
    return jnp.transpose(o, (1, 0, 3, 2, 4)).reshape(B, S, H, v.shape[-1])

def second_inputs(seed: int = 0) -> dict:
    key = jax.random.key(seed)
    ks = jax.random.split(key, 24)
    f32 = jnp.float32
    nrm = lambda k, shape, s: jax.random.normal(k, shape, f32) * s
    gain = lambda k, shape: 1.0 + 0.05 * jax.random.normal(k, shape, f32)
    dt = jnp.exp(jax.random.uniform(ks[7], (DEPTH_2, DN_HEADS), f32, np.log(1e-3), np.log(1e-1)))
    return {
        "x": nrm(ks[0], (BATCH, SEQ, D_MODEL), 1.0),
        "p": nrm(ks[1], (DEPTH_2, BATCH, SEQ, PLE_DIM), 1.0),
        "g_pre": gain(ks[2], (DEPTH_2, D_MODEL)),
        "w_in": nrm(ks[3], (DEPTH_2, D_MODEL, IN_COLS), D_MODEL ** -0.5),
        "b_gate": nrm(ks[4], (DEPTH_2, N_BRANCHES * D_MODEL), 0.02),
        "w_conv_qkv": nrm(ks[5], (DEPTH_2, SHORT_CONV, 3 * DN_WIDTH), SHORT_CONV ** -0.5),
        "a_log": jnp.log(jax.random.uniform(ks[6], (DEPTH_2, DN_HEADS), f32, 1.0, 16.0)),
        "dt_bias": dt + jnp.log(-jnp.expm1(-dt)),
        "g_dn_out": gain(ks[8], (DEPTH_2, DN_HEAD_DIM)),
        "w_dw": nrm(ks[9], (DEPTH_2, CONV_KERNEL, CONV_CH), CONV_KERNEL ** -0.5),
        "b_dw": nrm(ks[10], (DEPTH_2, CONV_CH), 0.02),
        "ln_g": gain(ks[11], (DEPTH_2, CONV_CH)),
        "ln_b": nrm(ks[12], (DEPTH_2, CONV_CH), 0.02),
        "w_br_a": nrm(ks[13], (DEPTH_2, DN_WIDTH, D_MODEL), DN_WIDTH ** -0.5),
        "w_br_b": nrm(ks[14], (DEPTH_2, CONV_CH, D_MODEL), CONV_CH ** -0.5),
        "w_out": nrm(ks[15], (DEPTH_2, D_MODEL, D_MODEL), D_MODEL ** -0.5),
        "g_post": gain(ks[16], (DEPTH_2, D_MODEL)),
        "w_ple_gate": nrm(ks[17], (DEPTH_2, D_MODEL, D_MODEL), D_MODEL ** -0.5),
        "w_ple_proj": nrm(ks[18], (DEPTH_2, PLE_DIM, D_MODEL), PLE_DIM ** -0.5),
        "g_ple": gain(ks[19], (DEPTH_2, D_MODEL)),
    }

def second_block(x, p, g_pre, w_in, b_gate, w_conv_qkv, a_log, dt_bias, g_dn_out, w_dw, b_dw,
              ln_g, ln_b, w_br_a, w_br_b, w_out, g_post, w_ple_gate, w_ple_proj, g_ple):
    B, S, _ = x.shape
    f32 = jnp.float32
    for i in range(DEPTH_2):
        h = rmsnorm(x, g_pre[i])
        proj = h @ w_in[i]
        qkv, z_a, b_raw, a_raw, glu_in, z_b, gate_logits = jnp.split(proj, _split_points(), axis=-1)

        qkv = jax.nn.silu(causal_depthwise_conv(qkv, w_conv_qkv[i]))
        q, k, v = jnp.split(qkv, 3, axis=-1)
        heads = lambda t: t.reshape(B, S, DN_HEADS, DN_HEAD_DIM).astype(f32)
        q, k, v = l2norm(heads(q)), l2norm(heads(k)), heads(v)
        beta = jax.nn.sigmoid(b_raw.astype(f32))
        g_log = -jnp.exp(a_log[i].astype(f32)) * jax.nn.softplus(a_raw.astype(f32) + dt_bias[i].astype(f32))
        o_a = gated_delta_chunked(q, k, v, g_log, beta)
        o_a = rmsnorm(o_a, g_dn_out[i]).reshape(B, S, DN_WIDTH).astype(x.dtype) * jax.nn.silu(z_a)
        y_a = o_a @ w_br_a[i]

        u = jax.nn.glu(glu_in, axis=-1)
        u = causal_depthwise_conv(u, w_dw[i]) + b_dw[i]
        u = jax.nn.silu(layernorm(u, ln_g[i], ln_b[i])) * jax.nn.silu(z_b)
        y_b = u @ w_br_b[i]

        gate_a, gate_b = jnp.split(jax.nn.sigmoid(gate_logits + b_gate[i]), N_BRANCHES, axis=-1)
        mixed = (gate_a * y_a + gate_b * y_b) @ w_out[i]
        x = x + rmsnorm(mixed, g_post[i])

        e = p[i] @ w_ple_proj[i]
        x = x + rmsnorm(jax.nn.sigmoid(x @ w_ple_gate[i]) * e, g_ple[i])
    return x


def setup_inputs(seed=0):
    out = dict(first_inputs(seed))
    for name, value in second_inputs(seed + 1).items():
        if name != "x":
            out[name + "_2"] = value
    return out


def reference(
    x, ret_norm, ret_w_in, ret_gn, ret_w_out, pool_norm, pool_w_in, pool_w_grp, pool_b_grp,
    pool_scale, pool_w_out, final_norm, p_2, g_pre_2, w_in_2, b_gate_2, w_conv_qkv_2, a_log_2,
    dt_bias_2, g_dn_out_2, w_dw_2, b_dw_2, ln_g_2, ln_b_2, w_br_a_2, w_br_b_2, w_out_2,
    g_post_2, w_ple_gate_2, w_ple_proj_2, g_ple_2,
):
    x = first_block(
        x, ret_norm, ret_w_in, ret_gn, ret_w_out, pool_norm, pool_w_in, pool_w_grp, pool_b_grp,
        pool_scale, pool_w_out, final_norm,
    )
    return second_block(
        x, p_2, g_pre_2, w_in_2, b_gate_2, w_conv_qkv_2, a_log_2, dt_bias_2, g_dn_out_2, w_dw_2,
        b_dw_2, ln_g_2, ln_b_2, w_br_a_2, w_br_b_2, w_out_2, g_post_2, w_ple_gate_2,
        w_ple_proj_2, g_ple_2,
    )


_drawn_inputs = setup_inputs


def setup_inputs(seed=0):
    import zlib

    import numpy as np

    out = dict(_drawn_inputs(seed))
    spreads = {}
    factors = {'pool_b_grp': 8.0, 'b_gate_2': 8.0, 'b_dw_2': 3.751, 'ln_g_2': 2.978, 'ln_b_2': 8.0}
    for name, (base, spread) in spreads.items():
        noise = np.random.default_rng([zlib.crc32(name.encode()), seed]).standard_normal(out[name].shape)
        drawn = base * np.exp(spread * noise) if base else spread * noise
        out[name] = __import__('jax').numpy.asarray(drawn.astype(out[name].dtype))
    for name, factor in factors.items():
        out[name] = (out[name] * factor).astype(out[name].dtype)
    return out
```

```python
from contextlib import ExitStack

import concourse.bass as bass
import numpy as np
from concourse import mybir

F32 = mybir.dt.float32
F32R = mybir.dt.float32r
ALU = mybir.AluOpType
ACT = mybir.ActivationFunctionType
AX = mybir.AxisListType

P = 128
SEQ = 256
NT = SEQ // P
DM = 2048
EPS = 1e-6
NB = 512
QT = NB // P
KPC = 2
RING = 4
K16 = DM // (KPC * P)
K32 = 2 * K16

RET_HEADS = 8
RET_QK = DM // RET_HEADS
HALF = RET_QK // 2
RET_V = 2 * DM
POOL_WINDOWS = (2, 4, 8, 16)
GROUPS = len(POOL_WINDOWS)
GDIM = 2 * DM // GROUPS
DN_HEADS = 16
HG = 4
TAPS = 4
LONG = 31
LEVELS = 7

R_PER, R_N = 3 * K16, RET_HEADS
RO_PER, RO_N = 2 * K32, 2
P_PER, P_N = 4 * K16 + 2 * (GDIM // (KPC * P)), GROUPS
D_PER, D_N = 4 * K16, 4
G_PER, G_N = 5 * K16, 4
Y_PER, Y_N = 2 * K16, 4
O_PER, O_N = 2 * K16, 2
E_PER = 4
R_AT = 0
RO_AT = R_AT + R_PER * R_N
P_AT = RO_AT + RO_PER * RO_N
PO_AT = P_AT + P_PER * P_N
D_AT = PO_AT + RO_PER * RO_N
G_AT = D_AT + D_PER * D_N
Y_AT = G_AT + G_PER * G_N
O_AT = Y_AT + Y_PER * Y_N
E_AT = O_AT + O_PER * O_N
PG_AT = E_AT + E_PER
CHUNKS = PG_AT + O_PER * O_N

C_RN = 0
C_GN = C_RN + 16
C_PN = C_GN + 32
C_PS = C_PN + 16
C_PRE = C_PS + 32
C_DN = C_PRE + 16
C_LNG = C_DN + 1
C_LNB = C_LNG + 16
C_BDW = C_LNB + 16
C_END = C_BDW + 16

T_N1, T_R, T_N2, T_P, T_N3, T_D, T_Y, T_X3 = 0, 4, 12, 16, 24, 28, 32, 36
M_N1, M_N2, M_FN, M_N3, M_POST, M_PLE = range(6)


def build(nc, dram):
    with ExitStack() as outer:
        sem_of = {}

        def sem(name):
            if name not in sem_of:
                sem_of[name] = outer.enter_context(nc.semaphore(name))
            return sem_of[name]

        def sb(stack, name, shape, dt=F32):
            return stack.enter_context(nc.sbuf_tensor(name, shape, dt))

        raw = sb(outer, "raw", [P, RING, KPC, NB])
        whi = sb(outer, "whi", [P, RING, KPC, NB], F32R)
        wlo = sb(outer, "wlo", [P, RING, KPC, NB], F32R)
        H = sb(outer, "H", [P, NT, DM])
        aH = sb(outer, "aH", [P, 16, SEQ], F32R)
        aL = sb(outer, "aL", [P, 16, SEQ], F32R)
        cols = sb(outer, "cols", [P, C_END])
        con = sb(outer, "con", [P, 4, P])
        ident, ones, upper, maskneg = (con[:, n, :] for n in range(4))
        part = sb(outer, "part", [P, 6, NT, 4])
        ssq = sb(outer, "ssq", [P, 6, NT])
        ms = sb(outer, "ms", [P, 6, NT])
        rstd = sb(outer, "rstd", [P, 6, NT])
        both = sb(outer, "both", [P, NT])
        mhalf = sb(outer, "mhalf", [P, 16])
        epsilon = sb(outer, "epsilon", [P, 16])
        carrier = sb(outer, "carrier", [P, 1])
        PS = outer.enter_context(nc.psum_tensor("PS", [P, 8, NB], F32))

        with ExitStack() as s:
            XS = sb(s, "XS", [P, NT, DM])
        with ExitStack() as s:
            oH = sb(s, "oH", [P, 32, SEQ], F32R)
            oL = sb(s, "oL", [P, 32, SEQ], F32R)
            with ExitStack() as r:
                dmask = sb(r, "dmask", [P, RET_HEADS, 3 * P])
                rot = sb(r, "rot", [P, 2, NT, HALF])
                roped = sb(r, "roped", [P, NT, 2, 2, HALF])
                rt = sb(r, "rt", [P, 2, NT, 2, HALF])
                qkT = sb(r, "qkT", [P, 2, 2, SEQ])
                vR = sb(r, "vR", [P, NT, NB])
                zR = sb(r, "zR", [P, NT, NB])
                sT = sb(r, "sT", [P, 3 * P])
                oR = sb(r, "oR", [P, NT, NB])
                bst = sb(r, "bst", [P, NT, 6])
                mv = sb(r, "mv", [P, NT, 2])
                rvar = sb(r, "rvar", [P, NT])
                rrs = sb(r, "rrs", [P, NT])
            with ExitStack() as r:
                pU = sb(r, "pU", [P, NT, GDIM])
                pZ = sb(r, "pZ", [P, NT, GDIM])
                mH = sb(r, "mH", [P, 8, SEQ], F32R)
                mL = sb(r, "mL", [P, 8, SEQ], F32R)
                pB = sb(r, "pB", [P, GDIM])
                pM = sb(r, "pM", [P, 3 * P])
                mz = sb(r, "mz", [P, NT, NB])
            with ExitStack() as r:
                row = sb(r, "row", [P, DM])
                junk = sb(r, "junk", [P, 2, NT, NB])
        with ExitStack() as s:
            oaH = sb(s, "oaH", [P, 16, SEQ], F32R)
            oaL = sb(s, "oaL", [P, 16, SEQ], F32R)
            with ExitStack() as r:
                beta = sb(r, "beta", [P, NT, DN_HEADS])
                cum = sb(r, "cum", [P, NT, DN_HEADS])
                ecum = sb(r, "ecum", [P, NT, DN_HEADS])
                becum = sb(r, "becum", [P, NT, DN_HEADS])
                gl = sb(r, "gl", [P, NT, DN_HEADS])
                wcv = sb(r, "wcv", [P, 3 * 16 * TAPS])
                lmask = sb(r, "lmask", [P, LEVELS, P])
                yD = sb(r, "yD", [P, HG, SEQ])
                kqv = sb(r, "kqv", [P, 3, HG, SEQ])
                zD = sb(r, "zD", [P, NT, NB])
                gm = sb(r, "gm", [P, NT, HG, P])
                dT = sb(r, "dT", [P, NT, HG, P])
                kn = sb(r, "kn", [P, NT, HG, P])
                kb = sb(r, "kb", [P, NT, HG, P])
                vb = sb(r, "vb", [P, NT, HG, P])
                knT = sb(r, "knT", [P, NT, HG, P])
                kbT = sb(r, "kbT", [P, NT, HG, P])
                aT = sb(r, "aT", [P, NT, HG, P])
                qk = sb(r, "qk", [P, NT, HG, P])
                iT = sb(r, "iT", [P, NT, HG, P])
                with ExitStack() as b:
                    wbr = sb(b, "wbr", [P, 16, 32])
                    wbh = sb(b, "wbh", [P, 16, 32], F32R)
                    wbl = sb(b, "wbl", [P, 16, 32], F32R)
                    dtb = sb(b, "dtb", [P, DN_HEADS])
                    alog = sb(b, "alog", [P, DN_HEADS])
                    ea = sb(b, "ea", [P, DN_HEADS])
                    ad = sb(b, "ad", [P, NT, DN_HEADS])
                    sp1 = sb(b, "sp1", [P, NT, DN_HEADS])
                    sp2 = sb(b, "sp2", [P, NT, DN_HEADS])
                iU = sb(r, "iU", [P, NT, HG, P])
                vn = sb(r, "vn", [P, NT, HG, P])
                ke = sb(r, "ke", [P, HG, P])
                sqn = sb(r, "sqn", [P, 2, NT, HG])
                rqk = sb(r, "rqk", [P, 2, NT, HG])
                oms = sb(r, "oms", [P, 3, NT, HG])
            st = kbT[:, 0]
            oD = yD[:].rearrange("p (t x) n -> p t (x n)", t=NT)
            with ExitStack() as r:
                uT = sb(r, "uT", [P, 16, SEQ])
                zbT = sb(r, "zbT", [P, 16, SEQ])
                mx = sb(r, "mx", [P, NT, DM])
                up = sb(r, "up", [P, QT, LONG - 1 + SEQ])
                sg = sb(r, "sg", [P, NT, NB])
                sg1 = sb(r, "sg1", [P, NT, NB])
                yl = sb(r, "yl", [P, QT, SEQ])
                yl2 = yl[:].rearrange("p (t x) n -> p t (x n)", t=NT)
                bg = sb(r, "bg", [P, NB])
                wdw = sb(r, "wdw", [P, 16 * LONG])
                wl = sb(r, "wl", [P, QT * LONG])
                mean = sb(r, "mean", [P, SEQ])
                rln = sb(r, "rln", [P, SEQ])
                ln_tmp = (up[:].rearrange("p c n -> p (c n)")[:, 0:QT * SEQ], yl[:].rearrange("p c n -> p (c n)"))
            with ExitStack() as r:
                ubH = sb(r, "ubH", [P, 16, SEQ], F32R)
                ubL = sb(r, "ubL", [P, 16, SEQ], F32R)
            with ExitStack() as r:
                mo = sb(r, "mo", [P, NT, DM])
                eb = sb(r, "eb", [P, NT, DM])
                rpost = sb(r, "rpost", [P, DM])
                rple = sb(r, "rple", [P, DM])
                pT = sb(r, "pT", [P, NT, SEQ])
                pTh = sb(r, "pTh", [P, NT, SEQ], F32R)
                pTl = sb(r, "pTl", [P, NT, SEQ], F32R)
                sgp = sb(r, "sgp", [P, NT, NB])
                junk2 = sb(r, "junk2", [P, 2, NT, NB])

        block = outer.enter_context(nc.Block())

        con_in, rot_in = sem("con_in"), sem("rot_in")
        x_in = [sem(f"x_in{n}") for n in range(4)]
        raw_in = [sem(f"raw_in{n}") for n in range(RING)]
        hi_done = sem("hi_done")
        lo_done = sem("lo_done")
        multiplied = sem("multiplied")
        t_ps, t_hi, t_lo = sem("t_ps"), sem("t_hi"), sem("t_lo")
        row_sq = [sem(f"row_sq{n}") for n in range(6)]
        row_sum, row_ms, row_rstd, xs_done = sem("row_sum"), sem("row_ms"), sem("row_rstd"), sem("xs_done")
        rot_scaled, fn_t, both_done = sem("rot_scaled"), sem("fn_t"), sem("both_done")
        const_set = sem("const_set")
        h_out = sem("h_out")
        stored = sem("stored")
        rope_t, rope_done, qkT_ps, qkT_sb, sT_ps, sT_sb, v_sb, o_ps = (
            sem(n) for n in "rope_t rope_done qkT_ps qkT_sb sT_ps sT_sb v_sb o_ps".split())
        bst_done, rrs_done, on_sb, z_sb, oz_sb = (
            sem(n) for n in "bst_done rrs_done on_sb z_sb oz_sb".split())
        pu_sb, pz_sb, mix_ps, mix_hi, mix_lo, pm_in, pb_in, mz_add, mz_sb, pb_used = (
            sem(n) for n in "pu_sb pz_sb mix_ps mix_hi mix_lo pm_in pb_in mz_add mz_sb pb_used".split())
        row_in, fn_done = sem("row_in"), sem("fn_done")
        ba_in, small_hi, small_lo, ba_ps, beta_sb, ad_sb, ea_sb, sp_a, gl_sb, cum_ps, cum_sb, ecum_sb = (
            sem(n) for n in ("ba_in small_hi small_lo ba_ps beta_sb ad_sb ea_sb sp_a gl_sb cum_ps cum_sb "
                             "ecum_sb").split())
        dn_in, conv_tap, kqv_sb, gu_sb, gu_ps, dt_sub, dt_sb, sq_sb, sq_ps, sqn_sb, rqk_sb = (
            sem(n) for n in "dn_in conv_tap kqv_sb gu_sb gu_ps dt_sub dt_sb sq_sb sq_ps sqn_sb rqk_sb".split())
        k_ps, kn_sb, kb_sb, kt_ps, kt_sb, a_ps, a_sb, b0_sb, u0_sb, t0_ps, t0_sb, lv_sb, m1_ps, m1_sb, tu_ps, tu_sb = (
            sem(n) for n in ("k_ps kn_sb kb_sb kt_ps kt_sb a_ps a_sb b0_sb u0_sb t0_ps t0_sb lv_sb m1_ps m1_sb "
                             "tu_ps tu_sb").split())
        qk_ps, qk_sb, v_ps, vb_sb, ke_sb, vn0_ps, vn0_sb, st_ps, st_sb, r1_ps, r1_sb, vb1_sb, o1_sb, o0_sb = (
            sem(n) for n in ("qk_ps qk_sb v_ps vb_sb ke_sb vn0_ps vn0_sb st_ps st_sb r1_ps r1_sb vb1_sb o1_sb "
                             "o0_sb").split())
        vn1_ps, vn1_sb, o1_ps, o1s_sb, oq_sb, osq_sb, omean_sb, ors_sb, onr_sb, zd_sb, od_sb = (
            sem(n) for n in ("vn1_ps vn1_sb o1_ps o1s_sb oq_sb osq_sb omean_sb ors_sb onr_sb zd_sb "
                             "od_sb").split())
        g_in, bg_in, sgb_sb, g_read, wl_set, zb_sb, gate_add, ga_sb, fn_t2 = (
            sem(n) for n in "g_in bg_in sgb_sb g_read wl_set zb_sb gate_add ga_sb fn_t2".split())
        long_tap = [sem(f"long_tap{c}") for c in range(QT)]
        mean_ps, mean_sb, uc_sb, usq_sb, usq_ps, std_sb, un_sb, us_sb, ub_sb, ub_hi, ub_lo = (
            sem(n) for n in ("mean_ps mean_sb uc_sb usq_sb usq_ps std_sb un_sb us_sb ub_sb ub_hi "
                             "ub_lo").split())
        gb_sb, yt_sb, ym_sb, mo_sb, tail_in, mp_sb, x3_sb, eb_sb, sp_sb, es_sb, ep_sb, out_sb = (
            sem(n) for n in ("gb_sb yt_sb ym_sb mo_sb tail_in mp_sb x3_sb eb_sb sp_sb es_sb "
                             "ep_sb out_sb").split())

        def half(bank, c):
            return PS[:, bank + c // 2, (c % 2) * SEQ:(c % 2 + 1) * SEQ]

        def heads(bank):
            return PS[:, bank:bank + 2].rearrange("p t (h n) -> p t h n", h=HG)

        def over(v, i):
            return v[:, :, bass.ds(i * HG, HG)][:, :, :, None].to_broadcast([P, NT, HG, P])

        def done(eng, q, j):
            eng.wait_ge(multiplied, q * RING + (RING + j + 1))

        @block.sync
        def _(sp):
            sp.dma_start(con[:], dram["con"]).then_inc(con_in, 16)
            sp.dma_start(cols[:], dram["cols"]).then_inc(con_in, 16)
            x = dram["x"].rearrange("(t p) n -> p t n", p=P)
            for u in range(4):
                sp.dma_start(H[:, :, u * NB:(u + 1) * NB], x[:, :, u * NB:(u + 1) * NB]).then_inc(x_in[u], 16)
            with sp.Fori(0, CHUNKS // RING) as i:
                for s in range(RING):
                    sp.wait_ge(lo_done, i * RING + (s + 1))
                    sp.dma_start(raw[:, s].rearrange("p k n -> p (k n)"),
                                 dram["stream"][i * RING + s]).then_inc(raw_in[s], 16)
            out = dram["out"].rearrange("(t p) n -> p t n", p=P)
            for u in range(4):
                sp.wait_ge(out_sb, NT * (u + 1))
                sp.dma_start(out[:, :, u * NB:(u + 1) * NB], eb[:, :, u * NB:(u + 1) * NB]).then_inc(stored, 16)
            sp.wait_ge(stored, 4 * 16)

        @block.gpsimd
        def _(pool):
            pool.dma_start(rot[:], dram["rot"]).then_inc(rot_in, 16)
            pool.dma_start(dmask[:], dram["dmask"]).then_inc(rot_in, 16)
            nc.gpsimd.memset(mhalf[:], -0.5).then_inc(const_set, 1)
            nc.gpsimd.memset(epsilon[:], EPS).then_inc(const_set, 1)
            pool.wait_ge(const_set, 2)

            def row_scale(use):
                pool.wait_ge(row_sum, use + 1)
                nc.gpsimd.tensor_scalar(ms[:, use], ssq[:, use], 1.0 / DM, EPS, ALU.mult, ALU.add).then_inc(row_ms, 1)
                pool.wait_ge(row_ms, use + 1)
                nc.gpsimd.tensor_tensor(rstd[:, use], ms[:, use], mhalf[:, 0:NT], ALU.pow).then_inc(row_rstd, 1)

            row_scale(M_N1)
            with pool.Fori(0, R_N) as i:
                pool.wait_ge(bst_done, i * (2 * NT) + 2 * NT)
                nc.gpsimd.tensor_tensor(rvar[:], mv[:, :, 1], epsilon[:, 0:NT], ALU.add).then_inc(rrs_done, 1)
                pool.wait_ge(rrs_done, i * 2 + 1)
                nc.gpsimd.tensor_tensor(rrs[:], rvar[:], mhalf[:, 0:NT], ALU.pow).then_inc(rrs_done, 1)
            pool.wait_ge(row_sq[M_N2], 8)
            pool.dma_start(pM[:], dram["pm"][0]).then_inc(pm_in, 16)
            pool.dma_start(pB[:], dram["pool_b"][0].to_broadcast([P, GDIM])).then_inc(pb_in, 16)
            row_scale(M_N2)
            with pool.Fori(1, P_N) as i:
                pool.wait_ge(pb_used, i)
                pool.dma_start(pM[:], dram["pm"][i]).then_inc(pm_in, 16)
                pool.dma_start(pB[:], dram["pool_b"][i].to_broadcast([P, GDIM])).then_inc(pb_in, 16)
            pool.wait_ge(t_ps, (T_P + 8) * 2)
            pool.dma_start(row[:], dram["final_norm"].to_broadcast([P, DM])).then_inc(row_in, 16)
            row_scale(M_FN)
            pool.wait_ge(row_sum, M_N3 + 1)
            pool.wait_ge(row_rstd, M_FN + 1)
            nc.gpsimd.tensor_tensor(ms[:, M_N3], ssq[:, M_N3], rstd[:, M_FN], ALU.mult).then_inc(fn_t, 1)
            pool.wait_ge(fn_t, 1)
            nc.gpsimd.tensor_tensor(ms[:, M_N3], ms[:, M_N3], rstd[:, M_FN], ALU.mult).then_inc(fn_t, 1)
            pool.wait_ge(fn_t, 2)
            nc.gpsimd.tensor_scalar(ms[:, M_N3], ms[:, M_N3], 1.0 / DM, EPS, ALU.mult, ALU.add).then_inc(row_ms, 1)
            pool.wait_ge(row_ms, M_N3 + 1)
            nc.gpsimd.tensor_tensor(rstd[:, M_N3], ms[:, M_N3], mhalf[:, 0:NT], ALU.pow).then_inc(row_rstd, 1)
            pool.wait_ge(row_rstd, M_N3 + 1)
            nc.gpsimd.tensor_tensor(both[:], rstd[:, M_N3], rstd[:, M_FN], ALU.mult).then_inc(both_done, 1)

            pool.dma_start(wbr[:], dram["w_ba"]).then_inc(ba_in, 16)
            pool.dma_start(dtb[:], dram["dt_bias"].to_broadcast([P, DN_HEADS])).then_inc(ba_in, 16)
            pool.dma_start(alog[:], dram["a_log"].to_broadcast([P, DN_HEADS])).then_inc(ba_in, 16)
            pool.dma_start(wcv[:], dram["w_conv"]).then_inc(dn_in, 16)
            pool.dma_start(lmask[:], dram["lm"]).then_inc(dn_in, 16)

            def delta_pool(i, first):
                if first:
                    pool.wait_ge(gl_sb, 1)
                else:
                    pool.wait_ge(t_ps, i * 2 + T_D * 2)
                nc.gpsimd.tensor_tensor(gm[:], upper[:, None, None, :].to_broadcast([P, NT, HG, P]), over(gl, i),
                                        ALU.mult).then_inc(gu_sb, 1)
                pool.wait_ge(sqn_sb, i * 2 + 1)
                nc.gpsimd.tensor_tensor(rqk[:, 0].rearrange("p t h -> p (t h)"),
                                        sqn[:, 0].rearrange("p t h -> p (t h)"), mhalf[:, 0:8],
                                        ALU.pow).then_inc(rqk_sb, 1)
                for lv in range(1, LEVELS):
                    if lv == 1:
                        pool.wait_ge(a_sb, i + 1)
                        pool.wait_ge(dn_in, 32)
                    elif lv == 2:
                        pool.wait_ge(u0_sb, i + 1)
                    else:
                        pool.wait_ge(m1_ps, i * (LEVELS - 1) + (lv - 2))
                    to = kbT if lv % 2 else kb
                    nc.gpsimd.tensor_tensor(to[:], aT[:], lmask[:, lv][:, None, None, :].to_broadcast([P, NT, HG, P]),
                                            ALU.mult).then_inc(lv_sb, 1)
                pool.wait_ge(sqn_sb, i * 2 + 2)
                nc.gpsimd.tensor_tensor(rqk[:, 1].rearrange("p t h -> p (t h)"),
                                        sqn[:, 1].rearrange("p t h -> p (t h)"), mhalf[:, 0:8],
                                        ALU.pow).then_inc(rqk_sb, 1)
                pool.wait_ge(omean_sb, i * 2 + 2)
                nc.gpsimd.tensor_tensor(oms[:, 2].rearrange("p t h -> p (t h)"),
                                        oms[:, 1].rearrange("p t h -> p (t h)"), mhalf[:, 0:8],
                                        ALU.pow).then_inc(ors_sb, 1)

            delta_pool(0, True)
            with pool.Fori(1, D_N) as i:
                delta_pool(i, False)
            pool.wait_ge(t_ps, (T_D + D_N) * 2)
            pool.dma_start(wdw[:], dram["w_long"]).then_inc(g_in, 16)
            nc.gpsimd.memset(up[:, :, 0:LONG - 1], 0.0).then_inc(const_set, 1)
            pool.dma_start(bg[:], dram["b_gate"][0].to_broadcast([P, NB])).then_inc(bg_in, 16)
            with pool.Fori(1, 2 * G_N) as i:
                pool.wait_ge(gate_add, i)
                pool.dma_start(bg[:], dram["b_gate"][i].to_broadcast([P, NB])).then_inc(bg_in, 16)
            pool.wait_ge(t_ps, (T_Y + Y_N) * 2)
            pool.dma_start(pT[:], dram["pT"]).then_inc(tail_in, 16)
            pool.dma_start(rpost[:], dram["g_post"].to_broadcast([P, DM])).then_inc(tail_in, 16)
            pool.dma_start(rple[:], dram["g_ple"].to_broadcast([P, DM])).then_inc(tail_in, 16)
            row_scale(M_POST)
            row_scale(M_PLE)

        @block.scalar
        def _(act):
            def split_hi(q, j):
                s = j % RING
                act.wait_ge(raw_in[s], q * 16 + 16 * (j // RING + 1))
                act.wait_ge(multiplied, q * RING + (j + 1))
                nc.scalar.copy(whi[:, s], raw[:, s]).then_inc(hi_done, 1)

            def t_split_hi(use, dst, kt, scale, bank=6):
                for c in range(QT):
                    act.wait_ge(t_ps, use * 2 + (c // 2 + 1))
                    to = dst[:, bass.ds(kt + c, 1), :].rearrange("p a n -> p (a n)")
                    if scale is None:
                        nc.scalar.copy(to, half(bank, c)).then_inc(t_hi, 1)
                    else:
                        nc.scalar.activation(to, half(bank, c), ACT.Copy,
                                             scale=cols[:, bass.ds(scale(c), 1)]).then_inc(t_hi, 1)

            def squares(use, b, src, to):
                for t in range(NT):
                    if b:
                        act.wait_ge(row_sq[use], NT * (b - 1) + t + 1)
                    nc.scalar.activation(to[:, t], src[:, t], ACT.Square,
                                         accum_out=part[:, use, t, b:b + 1]).then_inc(row_sq[use], 1)

            def quarter(v, b):
                return v[:, :, b * NB:(b + 1) * NB]

            def by_token(to, bank, func, use, sem_to):
                for t in range(NT):
                    ins = nc.scalar.activation(to[:, t], PS[:, bank + t], func, scale=rstd[:, use, t:t + 1])
                ins.then_inc(sem_to, 1)

            nc.scalar.preload_act_table(ACT.Silu)
            for j in range(RING):
                split_hi(0, j)
            act.wait_ge(con_in, 32)

            def norm1(u):
                t_split_hi(T_N1 + u, aH, 4 * u, lambda c: C_RN + 4 * u + c, 6 - 2 * (u % 2))

            norm1(0)
            norm1(1)

            def head_tail(i):
                t_split_hi(i + T_R, oH, i * QT, lambda c: i * QT + (C_GN + c))

            def head(i, first):
                q = i * (R_PER // RING) + R_AT // RING
                for j in range(R_PER):
                    split_hi(q, j + RING)
                    if first and j in (1, 3):
                        norm1((j + 3) // 2)
                    if first and j == 4:
                        for b in range(4):
                            squares(M_N1, b, quarter(H, b), XS[:, :, b * NB:(b + 1) * NB])
                    if not first and j == 1:
                        head_tail(i - 1)
                    if j == 11:
                        act.wait_ge(qkT_ps, i + 1)
                        nc.scalar.copy(qkT[:].rearrange("p a h n -> p (a h n)"),
                                       PS[:, 6:8].rearrange("p b n -> p (b n)")).then_inc(qkT_sb, 1)
                    if j == 15:
                        done(act, q, j)
                        act.wait_ge(row_rstd, M_N1 + 1)
                        by_token(vR, 2, ACT.Copy, M_N1, v_sb)
                done(act, q, R_PER - 1)
                by_token(zR, 4, ACT.Silu, M_N1, z_sb)

            head(0, True)
            with act.Fori(1, R_N) as i:
                head(i, False)

            for b in range(4):
                q = (RO_AT + b * K32) // RING
                for j in range(K32):
                    split_hi(q, j + RING)
                    if b == 0 and j == 1:
                        head_tail(R_N - 1)
                    if b and j == 2:
                        t_split_hi(T_N2 + b - 1, aH, 4 * (b - 1), lambda c: C_PN + 4 * (b - 1) + c)
                act.wait_ge(h_out, 2 + b + 1)
                squares(M_N2, b, quarter(H, b), junk[:, 0])

            def group(i, first):
                q = i * (P_PER // RING) + P_AT // RING
                for j in range(P_PER):
                    split_hi(q, j + RING)
                    if j == 1:
                        if first:
                            t_split_hi(T_N2 + 3, aH, 12, lambda c: C_PN + 12 + c)
                        else:
                            group_tail(i - 1, 1)
                    if j in (7, 15):
                        done(act, q, j)
                        b = j // 8
                        act.wait_ge(row_rstd, M_N2 + 1)
                        by_token(pU[:, :, b * NB:(b + 1) * NB], 2 * b, ACT.Copy, M_N2, pu_sb)
                    if j == 19:
                        for b in range(4):
                            act.wait_ge(mix_ps, i * 4 + (b + 1))
                            nc.scalar.copy(mH[:, 2 * b:2 * b + 2].rearrange("p a n -> p (a n)"),
                                           PS[:, 4 + b]).then_inc(mix_hi, 1)
                    if j in (23, 31):
                        done(act, q, j)
                        b = j // 8 - 2
                        by_token(pZ[:, :, b * NB:(b + 1) * NB], 2 * b, ACT.Silu, M_N2, pz_sb)
                    if j == 38:
                        group_tail(i, 0)

            def group_tail(i, w):
                t_split_hi(i * 2 + (T_P + w), oH, i * 8 + 4 * w, lambda c: i * 8 + (C_PS + 4 * w + c))

            group(0, True)
            with act.Fori(1, P_N) as i:
                group(i, False)
            for b in range(4):
                q = (PO_AT + b * K32) // RING
                for j in range(K32):
                    split_hi(q, j + RING)
                    if b == 0 and j == 1:
                        group_tail(P_N - 1, 1)
                act.wait_ge(h_out, 2 + 4 + b + 1)
                squares(M_FN, b, quarter(H, b), junk[:, 0])
                act.wait_ge(fn_t2, b + 1)
                squares(M_N3, b, quarter(H, b), junk[:, 1])

            def norm3(u):
                t_split_hi(T_N3 + u, aH, 4 * u, lambda c: C_PRE + 4 * u + c, 6 - 2 * (u % 2))

            norm3(0)
            norm3(1)

            def decays():
                act.wait_ge(ad_sb, 1)
                nc.scalar.activation(beta[:], PS[:, 4, 0:64].rearrange("p (t n) -> p t n", t=NT)[:, :, 0:DN_HEADS],
                                     ACT.Sigmoid).then_inc(beta_sb, 1)
                nc.scalar.activation(sp1[:], ad[:], ACT.Abs).then_inc(sp_a, 1)
                act.wait_ge(sp_a, 1)
                nc.scalar.activation(sp1[:], sp1[:], ACT.Exp, scale=-1.0).then_inc(sp_a, 1)
                act.wait_ge(sp_a, 2)
                nc.scalar.activation(sp1[:], sp1[:], ACT.Ln, bias=1.0).then_inc(sp_a, 1)

            act.sem_inc(kqv_sb, 1)
            act.sem_inc(zb_sb, 1)

            def copy_heads(to, bank, wait, after, value):
                act.wait_ge(wait, value)
                nc.scalar.copy(to[:].rearrange("p t h n -> p t (h n)"), PS[:, bank:bank + 2]).then_inc(after, 1)

            def delta_tail(i, j):
                if j == 1:
                    act.wait_ge(vn1_ps, i + 1)
                    nc.scalar.copy(vn[:, 1].rearrange("p h n -> p (h n)"), PS[:, 4]).then_inc(vn1_sb, 1)
                if j == 3:
                    act.wait_ge(oq_sb, i + 1)
                    nc.scalar.activation(gm[:].rearrange("p t h n -> p t (h n)"), oD, ACT.Square).then_inc(osq_sb, 1)
                if j == 5:
                    t_split_hi(i + T_D, oaH, i * QT, lambda c: C_DN)

            def delta(i, first):
                q = i * (D_PER // RING) + D_AT // RING
                for j in range(D_PER):
                    split_hi(q, j + RING)
                    if first and j in (1, 3):
                        norm3((j + 3) // 2)
                    if first and j == 5:
                        act.wait_ge(ba_in, 48)
                        nc.scalar.copy(wbh[:], wbr[:]).then_inc(small_hi, 1)
                        nc.scalar.activation(ea[:], alog[:], ACT.Exp).then_inc(ea_sb, 1)
                    if first and j == 7:
                        decays()
                    if first and j == 8:
                        act.wait_ge(cum_ps, 1)
                        nc.scalar.copy(cum[:].rearrange("p t h -> p (t h)"), PS[:, 5, 0:NT * DN_HEADS]).then_inc(cum_sb, 1)
                        act.wait_ge(cum_sb, 1)
                        nc.scalar.activation(ecum[:], cum[:], ACT.Exp).then_inc(ecum_sb, 1)
                    if not first:
                        delta_tail(i - 1, j)
                    if j == 11:
                        act.wait_ge(dt_sub, i * 2 + 2)
                        nc.scalar.activation(dT[:], dT[:], ACT.Exp).then_inc(dt_sb, 1)
                    if j in (9, 17, 25):
                        y = (j - 9) // 8
                        act.wait_ge(conv_tap, i * 48 + 16 * (y + 1))
                        nc.scalar.activation(kqv[:, y], yD[:], ACT.Silu).then_inc(kqv_sb, 1)
                        if y < 2:
                            act.wait_ge(kqv_sb, i * 3 + (y + 2))
                            to = kb[:].rearrange("p t h n -> p (t h n)") if y == 0 else zD[:].rearrange("p t n -> p (t n)")
                            nc.scalar.activation(to, kqv[:, y].rearrange("p h n -> p (h n)"),
                                                 ACT.Square).then_inc(sq_sb, 1)
                    if j == 12:
                        copy_heads(knT, 4, kt_ps, kt_sb, i + 1)
                        copy_heads(kbT, 6, kt_ps, kt_sb, i + 1)
                    if j == 14:
                        copy_heads(iT, 4, t0_ps, t0_sb, i + 1)
                    if 15 <= j <= 25 and j % 2:
                        lv = (j - 13) // 2
                        copy_heads(gm, 4, m1_ps, m1_sb, i * (LEVELS - 1) + lv)
                    if j == 29:
                        act.wait_ge(vn0_ps, i + 1)
                        nc.scalar.copy(vn[:, 0].rearrange("p h n -> p (h n)"), PS[:, 7]).then_inc(vn0_sb, 1)
                    if j == 30:
                        act.wait_ge(st_ps, i + 1)
                        nc.scalar.copy(st.rearrange("p h n -> p (h n)"), PS[:, 4]).then_inc(st_sb, 1)
                done(act, q, D_PER - 1)
                act.wait_ge(sq_ps, i * 2 + 2)
                nc.scalar.activation(zD[:], PS[:, 2:4], ACT.Silu).then_inc(zd_sb, 1)

            delta(0, True)
            with act.Fori(1, D_N) as i:
                delta(i, False)

            def gated(i, first):
                q = i * (G_PER // RING) + G_AT // RING
                for j in range(G_PER):
                    split_hi(q, j + RING)
                    if first:
                        delta_tail(D_N - 1, j)
                    if j == 15:
                        done(act, q, j)
                        nc.scalar.activation(sg[:], PS[:, 2:4], ACT.Sigmoid).then_inc(sgb_sb, 1)
                    if j == 23:
                        done(act, q, j)
                        nc.scalar.activation(zbT[:, bass.ds(i * QT, QT)].rearrange("p c n -> p (c n)"),
                                             PS[:, 4:6].rearrange("p b n -> p (b n)"), ACT.Silu).then_inc(zb_sb, 1)
                    if j == 31:
                        act.wait_ge(gate_add, i + 1)
                        nc.scalar.activation(sg[:], sg[:], ACT.Sigmoid).then_inc(ga_sb, 1)

            gated(0, True)
            with act.Fori(1, G_N) as i:
                gated(i, False)

            def gate_b(b, to):
                act.wait_ge(gate_add, b + (G_N + 1))
                nc.scalar.activation(to[:], to[:], ACT.Sigmoid).then_inc(gb_sb, 1)

            def branch_tail(b):
                t_split_hi(b + T_Y, oaH, b * QT, None)

            for j in range(2 * Y_PER):
                split_hi(Y_AT // RING, j + RING)
                if j == 7:
                    gate_b(0, sg)
                if j == 8:
                    for u in range(4):
                        act.wait_ge(uc_sb, u + 1)
                        if u > 1:
                            act.wait_ge(usq_ps, u - 1)
                        nc.scalar.activation(ln_tmp[u % 2], uT[:, 4 * u:4 * u + 4].rearrange("p c n -> p (c n)"),
                                             ACT.Square).then_inc(usq_sb, 1)
                if j == 10:
                    act.wait_ge(mean_sb, 2)
                    nc.scalar.activation(rln[:], rln[:], ACT.Sqrt).then_inc(std_sb, 1)
                if 11 <= j <= 14:
                    u = j - 11
                    act.wait_ge(un_sb, u + 1)
                    for c in range(QT):
                        k = 4 * u + c
                        nc.scalar.activation(uT[:, k], uT[:, k], ACT.Silu, scale=cols[:, C_LNG + k:C_LNG + k + 1],
                                             bias=cols[:, C_LNB + k:C_LNB + k + 1]).then_inc(us_sb, 1)
                    act.wait_ge(ub_sb, u + 1)
                    nc.scalar.copy(ubH[:, 4 * u:4 * u + 4].rearrange("p c n -> p (c n)"), ln_tmp[u % 2]).then_inc(ub_hi, 1)
                if j == 15:
                    gate_b(1, sg1)
                if j == 26:
                    branch_tail(0)

            def branch(i):
                q = i * (Y_PER // RING) + Y_AT // RING
                for j in range(Y_PER):
                    split_hi(q, j + RING)
                    if j == 2:
                        branch_tail(i - 1)
                    if j == 7:
                        gate_b(i, sg)

            with act.Fori(2, Y_N) as i:
                branch(i)

            for b in range(4):
                q = (O_AT + b * K16) // RING
                for j in range(K16):
                    split_hi(q, j + RING)
                    if b == 0 and j == 2:
                        branch_tail(Y_N - 1)
                done(act, q, K16 - 1)
                nc.scalar.copy(quarter(mo, b), PS[:, 2 * (b % 2):2 * (b % 2) + 2]).then_inc(mo_sb, 1)
                squares(M_POST, b, PS[:, 2 * (b % 2):2 * (b % 2) + 2], junk2[:, 0])
            act.wait_ge(tail_in, 48)
            nc.scalar.copy(pTh[:], pT[:]).then_inc(small_hi, 1)
            for j in range(E_PER):
                split_hi(E_AT // RING, j + RING)
                done(act, E_AT // RING, j)
                nc.scalar.copy(eb[:, :, j * NB:(j + 1) * NB], PS[:, 2 * (j % 2):2 * (j % 2) + 2]).then_inc(eb_sb, 1)

            def norm_x3(u):
                t_split_hi(T_X3 + u, aH, 4 * u, None, 6 - 2 * (u % 2))

            norm_x3(0)
            norm_x3(1)
            for b in range(4):
                q = (PG_AT + b * K16) // RING
                for j in range(K16):
                    if b < 3 or j < K16 - RING:
                        split_hi(q, j + RING)
                    if b == 0 and j in (1, 3):
                        norm_x3((j + 3) // 2)
                done(act, q, K16 - 1)
                if b:
                    act.wait_ge(es_sb, b)
                nc.scalar.activation(sgp[:], PS[:, 2 * (b % 2):2 * (b % 2) + 2], ACT.Sigmoid).then_inc(sp_sb, 1)
                act.wait_ge(es_sb, b + 1)
                squares(M_PLE, b, quarter(eb, b), junk2[:, 1])

        @block.vector
        def _(dve):
            def split_lo(q, j):
                s = j % RING
                dve.wait_ge(hi_done, q * RING + (j + 1))
                nc.vector.tensor_tensor(wlo[:, s], raw[:, s], whi[:, s].bitcast(F32), ALU.subtract).then_inc(lo_done, 1)

            def t_split_lo(use, hi, lo, kt, scale, bank=6):
                for c in range(QT):
                    dve.wait_ge(t_hi, use * QT + (c // 2 * 2 + 2))
                    h = hi[:, bass.ds(kt + c, 1), :].rearrange("p a n -> p (a n)").bitcast(F32)
                    to = lo[:, bass.ds(kt + c, 1), :].rearrange("p a n -> p (a n)")
                    if scale is None:
                        nc.vector.tensor_tensor(to, half(bank, c), h, ALU.subtract).then_inc(t_lo, 1)
                    else:
                        nc.vector.scalar_tensor_tensor(out=to, in0=half(bank, c), scalar=cols[:, bass.ds(scale(c), 1)],
                                                       in1=h, op0=ALU.mult, op1=ALU.subtract).then_inc(t_lo, 1)

            def row_total(use):
                dve.wait_ge(row_sq[use], 8)
                nc.vector.tensor_reduce(ssq[:, use], part[:, use], AX.X, ALU.add).then_inc(row_sum, 1)

            def quarter(v, b):
                return v[:, :, b * NB:(b + 1) * NB]

            dve.sem_inc(lo_done, RING)
            dve.sem_inc(h_out, 2)
            for j in range(RING):
                split_lo(0, j)
            dve.wait_ge(con_in, 32)

            def norm1(u):
                t_split_lo(T_N1 + u, aH, aL, 4 * u, lambda c: C_RN + 4 * u + c, 6 - 2 * (u % 2))

            norm1(0)
            norm1(1)

            def head_tail(i):
                t_split_lo(i + T_R, oH, oL, i * QT, lambda c: i * QT + (C_GN + c))

            def rope(i):
                x = PS[:, 0:2].rearrange("p t (a h n) -> p t a h n", a=2, h=2)
                cos, sin = (rot[:, n][:, :, None, :].to_broadcast([P, NT, 2, HALF]) for n in range(2))
                steps = ((0, cos, 1, sin, ALU.subtract), (0, sin, 1, cos, ALU.add))
                for n, (ha, fa, hb, fb, op) in enumerate(steps):
                    if n:
                        dve.wait_ge(rope_done, i * 2 + 1)
                    nc.vector.tensor_tensor(rt[:, 0], x[:, :, :, ha], fa, ALU.mult).then_inc(rope_t, 1)
                    nc.vector.tensor_tensor(rt[:, 1], x[:, :, :, hb], fb, ALU.mult).then_inc(rope_t, 1)
                    dve.wait_ge(rope_t, i * 4 + 2 * (n + 1))
                    nc.vector.tensor_tensor(roped[:, :, :, n], rt[:, 0], rt[:, 1], op).then_inc(rope_done, 1)

            def head(i, first):
                q = i * (R_PER // RING) + R_AT // RING
                for j in range(R_PER):
                    split_lo(q, j + RING)
                    if first and j in (1, 3):
                        norm1((j + 3) // 2)
                    if first and j == 5:
                        row_total(M_N1)
                    if first and j == 6:
                        dve.wait_ge(row_rstd, M_N1 + 1)
                        dve.wait_ge(rot_in, 32)
                        for t in range(NT):
                            ins = nc.vector.tensor_scalar(rot[:, :, t], rot[:, :, t], rstd[:, M_N1, t:t + 1], None, ALU.mult)
                        ins.then_inc(rot_scaled, 1)
                    if not first and j == 1:
                        head_tail(i - 1)
                    if j == 7:
                        dve.wait_ge(rot_scaled, 1)
                        done(dve, q, j)
                        rope(i)
                    if j == 15:
                        dve.wait_ge(sT_ps, i + 1)
                        nc.vector.tensor_tensor(sT[:], PS[:, 6, 0:3 * P],
                                                dmask[:, bass.ds(i, 1)].rearrange("p a n -> p (a n)"),
                                                ALU.mult).then_inc(sT_sb, 1)
                    if j == 19:
                        dve.wait_ge(o_ps, i + 1)
                        for t in range(NT):
                            nc.vector.bn_stats(bst[:, t], PS[:, 6 + t]).then_inc(bst_done, 1)
                        dve.wait_ge(bst_done, i * (2 * NT) + NT)
                        nc.vector.memset(carrier[:], 0.0)
                        for t in range(NT):
                            nc.vector.bn_aggr(mv[:, t], bst[:, t]).then_inc(bst_done, 1)
                    if j == 20:
                        dve.wait_ge(rrs_done, i * 2 + 2)
                        dve.wait_ge(bst_done, i * (2 * NT) + 2 * NT)
                        for t in range(NT):
                            nc.vector.tensor_scalar(oR[:, t], PS[:, 6 + t], mv[:, t, 0:1], rrs[:, t:t + 1],
                                                    ALU.subtract, ALU.mult).then_inc(on_sb, 1)
                dve.wait_ge(z_sb, i + 1)
                dve.wait_ge(on_sb, i * NT + NT)
                nc.vector.tensor_tensor(oR[:], oR[:], zR[:], ALU.mult).then_inc(oz_sb, 1)

            head(0, True)
            with dve.Fori(1, R_N) as i:
                head(i, False)

            for b in range(4):
                q = (RO_AT + b * K32) // RING
                for j in range(K32):
                    split_lo(q, j + RING)
                    if b == 0 and j == 1:
                        head_tail(R_N - 1)
                    if b and j == 2:
                        t_split_lo(T_N2 + b - 1, aH, aL, 4 * (b - 1), lambda c: C_PN + 4 * (b - 1) + c)
                done(dve, q, K32 - 1)
                nc.vector.tensor_tensor(quarter(H, b), PS[:, 2 * (b % 2):2 * (b % 2) + 2], quarter(H, b),
                                        ALU.add).then_inc(h_out, 1)
            row_total(M_N2)

            def group_tail(i, w):
                t_split_lo(i * 2 + (T_P + w), oH, oL, i * 8 + 4 * w, lambda c: i * 8 + (C_PS + 4 * w + c))

            def group(i, first):
                q = i * (P_PER // RING) + P_AT // RING
                for j in range(P_PER):
                    split_lo(q, j + RING)
                    if j == 1:
                        if first:
                            t_split_lo(T_N2 + 3, aH, aL, 12, lambda c: C_PN + 12 + c)
                        else:
                            group_tail(i - 1, 1)
                    if j == 19:
                        for b in range(4):
                            dve.wait_ge(mix_hi, i * 4 + (b + 1))
                            nc.vector.tensor_tensor(mL[:, 2 * b:2 * b + 2].rearrange("p a n -> p (a n)"), PS[:, 4 + b],
                                                    mH[:, 2 * b:2 * b + 2].rearrange("p a n -> p (a n)").bitcast(F32),
                                                    ALU.subtract).then_inc(mix_lo, 1)
                    if j in (35, 39):
                        w = (j - 35) // 4
                        done(dve, q, j)
                        if w == 0:
                            dve.wait_ge(pb_in, i * 16 + 16)
                        dve.wait_ge(t_ps, i * 4 + (T_P + w) * 2)
                        nc.vector.tensor_tensor(mz[:], PS[:, 2 * w:2 * w + 2],
                                                pB[:, w * NB:(w + 1) * NB][:, None, :].to_broadcast([P, NT, NB]),
                                                ALU.add).then_inc(mz_add, 1)
                        dve.wait_ge(pz_sb, i * 2 + (w + 1))
                        dve.wait_ge(mz_add, i * 2 + (w + 1))
                        nc.vector.tensor_tensor(mz[:], mz[:], pZ[:, :, w * NB:(w + 1) * NB], ALU.mult).then_inc(mz_sb, 1)
                    if j == 38:
                        group_tail(i, 0)
                dve.sem_inc(pb_used, 1)

            group(0, True)
            with dve.Fori(1, P_N) as i:
                group(i, False)
            for b in range(4):
                q = (PO_AT + b * K32) // RING
                for j in range(K32):
                    split_lo(q, j + RING)
                    if b == 0 and j == 1:
                        group_tail(P_N - 1, 1)
                done(dve, q, K32 - 1)
                nc.vector.tensor_tensor(quarter(H, b), PS[:, 2 * (b % 2):2 * (b % 2) + 2], quarter(H, b),
                                        ALU.add).then_inc(h_out, 1)
                dve.wait_ge(row_in, 16)
                dve.wait_ge(row_sq[M_FN], NT * (b + 1))
                nc.vector.tensor_tensor(quarter(H, b), quarter(H, b),
                                        row[:, b * NB:(b + 1) * NB][:, None, :].to_broadcast([P, NT, NB]),
                                        ALU.mult).then_inc(fn_t2, 1)
            row_total(M_FN)
            row_total(M_N3)
            dve.wait_ge(both_done, 1)
            for u in range(4):
                for t in range(NT):
                    nc.vector.tensor_scalar(XS[:, t, u * NB:(u + 1) * NB], H[:, t, u * NB:(u + 1) * NB], both[:, t:t + 1],
                                            None, ALU.mult).then_inc(xs_done, 1)

            def norm3(u):
                t_split_lo(T_N3 + u, aH, aL, 4 * u, lambda c: C_PRE + 4 * u + c, 6 - 2 * (u % 2))

            norm3(0)
            norm3(1)

            def add_bias(bank, to, n):
                dve.wait_ge(bg_in, n * 16 + 16)
                nc.vector.tensor_tensor(to[:], PS[:, bank:bank + 2], bg[:, None, :].to_broadcast([P, NT, NB]),
                                        ALU.add).then_inc(gate_add, 1)

            def decays():
                dve.wait_ge(ba_ps, 1)
                nc.vector.tensor_tensor(ad[:], PS[:, 4, 0:64].rearrange("p (t n) -> p t n", t=NT)[:, :, DN_HEADS:],
                                        dtb[:, None, :].to_broadcast([P, NT, DN_HEADS]), ALU.add).then_inc(ad_sb, 1)
                dve.wait_ge(ad_sb, 1)
                dve.wait_ge(sp_a, 3)
                nc.vector.scalar_tensor_tensor(out=sp2[:], in0=ad[:], scalar=0.0, in1=sp1[:], op0=ALU.max,
                                               op1=ALU.add).then_inc(ad_sb, 1)
                dve.wait_ge(ea_sb, 1)
                dve.wait_ge(ad_sb, 2)
                nc.vector.scalar_tensor_tensor(out=gl[:], in0=sp2[:], scalar=-1.0,
                                               in1=ea[:, None, :].to_broadcast([P, NT, DN_HEADS]), op0=ALU.mult,
                                               op1=ALU.mult).then_inc(gl_sb, 1)

            o = oD.rearrange("p t (h n) -> p t h n", h=HG)

            def delta_tail(i, j):
                def second(v):
                    return v[:, 1, bass.ds(i * HG, HG)][:, :, None].to_broadcast([P, HG, P])

                if j == 0:
                    dve.wait_ge(r1_ps, i + 1)
                    nc.vector.tensor_tensor(ke[:], heads(4)[:, 1], second(becum), ALU.mult).then_inc(r1_sb, 1)
                    dve.wait_ge(r1_sb, i + 1)
                    nc.vector.tensor_tensor(vb[:, 1], vb[:, 1], ke[:], ALU.subtract).then_inc(vb1_sb, 1)
                    nc.vector.tensor_tensor(o[:, 1], heads(6)[:, 0], second(ecum), ALU.mult).then_inc(o1_sb, 1)
                    nc.vector.tensor_copy(o[:, 0], heads(6)[:, 1]).then_inc(o0_sb, 1)
                if j == 2:
                    dve.wait_ge(o1_ps, i + 1)
                    dve.wait_ge(o1_sb, i + 1)
                    nc.vector.tensor_tensor(o[:, 1], heads(4)[:, 1], o[:, 1], ALU.add).then_inc(o1s_sb, 1)
                    dve.wait_ge(o1s_sb, i + 1)
                    dve.wait_ge(o0_sb, i + 1)
                    dve.wait_ge(rqk_sb, i * 2 + 2)
                    nc.vector.tensor_tensor(o, o, rqk[:, 1][:, :, :, None].to_broadcast([P, NT, HG, P]),
                                            ALU.mult).then_inc(oq_sb, 1)
                if j == 3:
                    dve.wait_ge(osq_sb, i + 1)
                    nc.vector.tensor_reduce(oms[:, 0], gm[:], AX.X, ALU.add).then_inc(omean_sb, 1)
                    dve.wait_ge(omean_sb, i * 2 + 1)
                    nc.vector.tensor_scalar(oms[:, 1], oms[:, 0], 1.0 / P, EPS, ALU.mult, ALU.add).then_inc(omean_sb, 1)
                if j == 4:
                    dve.wait_ge(ors_sb, i + 1)
                    nc.vector.tensor_tensor(o, o, oms[:, 2][:, :, :, None].to_broadcast([P, NT, HG, P]),
                                            ALU.mult).then_inc(onr_sb, 1)
                    dve.wait_ge(onr_sb, i + 1)
                    dve.wait_ge(zd_sb, i + 1)
                    nc.vector.tensor_tensor(oD, oD, zD[:], ALU.mult).then_inc(od_sb, 1)
                if j == 5:
                    t_split_lo(i + T_D, oaH, oaL, i * QT, lambda c: C_DN)

            def conv(i, y):
                at = (1, 0, 2)[y] * 16 * TAPS
                for k in range(TAPS):
                    for c in range(HG):
                        src = half(2 * (y % 2), c)
                        w = wcv[:, bass.ds(i * (HG * TAPS) + (at + c * TAPS + TAPS - 1 - k), 1)]
                        if k == 0:
                            if c == 0:
                                dve.wait_ge(kqv_sb, i * 3 + (y + 1))
                                if y == 0:
                                    dve.wait_ge(t_ps, i * 2 + T_D * 2)
                            nc.vector.tensor_scalar(yD[:, c], src, w, None, ALU.mult).then_inc(conv_tap, 1)
                        else:
                            dve.wait_ge(conv_tap, i * 48 + (16 * y + HG * (k - 1) + c + 1))
                            nc.vector.scalar_tensor_tensor(out=yD[:, c, k:], in0=src[:, 0:SEQ - k], scalar=w,
                                                           in1=yD[:, c, k:], op0=ALU.mult,
                                                           op1=ALU.add).then_inc(conv_tap, 1)

            def norms(i, n, bank):
                dve.wait_ge(sq_ps, i * 2 + (n + 1))
                nc.vector.tensor_scalar(sqn[:, n].rearrange("p t h -> p (t h)"), PS[:, bank, 0:8], EPS,
                                        (1.0, float(P))[n], ALU.add, ALU.mult).then_inc(sqn_sb, 1)

            def delta(i, first):
                q = i * (D_PER // RING) + D_AT // RING
                for j in range(D_PER):
                    split_lo(q, j + RING)
                    if first and j in (1, 3):
                        norm3((j + 3) // 2)
                    if first and j == 4:
                        for t in range(NT):
                            nc.vector.tensor_scalar(H[:, t], H[:, t], rstd[:, M_FN, t:t + 1], None,
                                                    ALU.mult).then_inc(fn_done, 1)
                    if first and j == 5:
                        dve.wait_ge(small_hi, 1)
                        nc.vector.tensor_tensor(wbl[:], wbr[:], wbh[:].bitcast(F32), ALU.subtract).then_inc(small_lo, 1)
                    if not first:
                        delta_tail(i - 1, j)
                    if first and j == 7:
                        decays()
                        dve.wait_ge(dn_in, 32)
                    if j in (7, 15, 23):
                        done(dve, q, j)
                        conv(i, (j - 7) // 8)
                    if first and j == 9:
                        dve.wait_ge(ecum_sb, 1)
                        dve.wait_ge(beta_sb, 1)
                        nc.vector.tensor_tensor(becum[:], ecum[:], beta[:], ALU.mult)
                    if j == 9:
                        dve.wait_ge(gu_ps, i + 1)
                        nc.vector.tensor_tensor(dT[:], heads(4), over(cum, i), ALU.subtract).then_inc(dt_sub, 1)
                        dve.wait_ge(dt_sub, i * 2 + 1)
                        nc.vector.tensor_tensor(dT[:], dT[:], maskneg[:, None, None, :].to_broadcast([P, NT, HG, P]),
                                                ALU.min).then_inc(dt_sub, 1)
                    if j == 10:
                        norms(i, 0, 6)
                    if j == 11:
                        dve.wait_ge(k_ps, i + 1)
                        dve.wait_ge(rqk_sb, i * 2 + 1)
                        nc.vector.tensor_tensor(kn[:], heads(4), rqk[:, 0][:, :, :, None].to_broadcast([P, NT, HG, P]),
                                                ALU.mult).then_inc(kn_sb, 1)
                        dve.wait_ge(kn_sb, i + 1)
                        nc.vector.tensor_tensor(kb[:], kn[:], over(beta, i), ALU.mult).then_inc(kb_sb, 1)
                    if j == 13:
                        dve.wait_ge(dt_sb, i + 1)
                        dve.wait_ge(a_ps, i + 1)
                        nc.vector.tensor_tensor(aT[:], heads(4), dT[:], ALU.mult).then_inc(a_sb, 1)
                        dve.wait_ge(a_sb, i + 1)
                        nc.vector.tensor_tensor(kb[:], aT[:], lmask[:, 0][:, None, None, :].to_broadcast([P, NT, HG, P]),
                                                ALU.mult).then_inc(b0_sb, 1)
                        dve.wait_ge(b0_sb, i + 1)
                        nc.vector.tensor_tensor(iU[:], ident[:, None, None, :].to_broadcast([P, NT, HG, P]), kb[:],
                                                ALU.subtract).then_inc(u0_sb, 1)
                    if j in (16, 18, 20, 22, 24, 26):
                        lv = (j - 14) // 2
                        dve.wait_ge(tu_ps, i * (LEVELS - 1) + lv)
                        if lv == 1:
                            dve.wait_ge(t0_sb, i + 1)
                        else:
                            dve.wait_ge(tu_sb, i * (2 * LEVELS - 3) + 2 * (lv - 1))
                        if lv < LEVELS - 1:
                            nc.vector.tensor_tensor(iT[:], iT[:], heads(4), ALU.subtract).then_inc(tu_sb, 1)
                        nc.vector.tensor_tensor(iU[:], iU[:], heads(6), ALU.subtract).then_inc(tu_sb, 1)
                    if j == 27:
                        dve.wait_ge(qk_ps, i + 1)
                        nc.vector.tensor_tensor(qk[:], heads(6), dT[:], ALU.mult).then_inc(qk_sb, 1)
                    if j == 28:
                        dve.wait_ge(v_ps, i + 1)
                        nc.vector.tensor_tensor(vb[:], heads(4), over(beta, i), ALU.mult).then_inc(vb_sb, 1)
                        nc.vector.tensor_tensor(ke[:], kn[:, 0], dT[:, 0, :, P - 1:P].to_broadcast([P, HG, P]),
                                                ALU.mult).then_inc(ke_sb, 1)
                    if j == 29:
                        norms(i, 1, 6)

            delta(0, True)
            with dve.Fori(1, D_N) as i:
                delta(i, False)

            dve.sem_inc(g_read, 3)

            def tap(i, k):
                for c in range(QT):
                    w = wl[:, c * LONG + k:c * LONG + k + 1]
                    if k == 0:
                        nc.vector.tensor_scalar(yl[:, c], up[:, c, 0:SEQ], w,
                                                cols[:, bass.ds(i * QT + (C_BDW + c), 1)], ALU.mult,
                                                ALU.add).then_inc(long_tap[c], 1)
                        continue
                    dve.wait_ge(long_tap[c], i * LONG + k)
                    to = yl[:, c] if k < LONG - 1 else uT[:, bass.ds(i * QT + c, 1)].rearrange("p a n -> p (a n)")
                    nc.vector.scalar_tensor_tensor(out=to, in0=up[:, c, k:k + SEQ], scalar=w, in1=yl[:, c],
                                                   op0=ALU.mult, op1=ALU.add).then_inc(long_tap[c], 1)

            OWN = 20

            def gated(i, first):
                q = i * (G_PER // RING) + G_AT // RING
                k = OWN
                for j in range(2 * K16):
                    split_lo(q, j + RING)
                    if first:
                        delta_tail(D_N - 1, j)
                    while not first and k < LONG and (k - OWN) * 14 < (j + 1) * (LONG - OWN):
                        tap(i - 1, k)
                        k += 1
                done(dve, q, 2 * K16 - 1)
                dve.wait_ge(sgb_sb, i + 1)
                if not first:
                    dve.wait_ge(long_tap[QT - 1], i * LONG)
                nc.vector.tensor_tensor(up[:, :, LONG - 1:], PS[:, 0:2].rearrange("p b (c n) -> p (b c) n", c=2),
                                        sg[:].rearrange("p t (x n) -> p (t x) n", x=2), ALU.mult).then_inc(g_read, 1)
                dve.wait_ge(g_in, 16)
                nc.vector.tensor_copy(wl[:], wdw[:, bass.ds(i * (QT * LONG), QT * LONG)]).then_inc(wl_set, 1)
                dve.wait_ge(g_read, i * 3 + 4)
                dve.wait_ge(const_set, 3)
                dve.wait_ge(wl_set, i + 1)
                k = 0
                for j in range(2 * K16, G_PER):
                    split_lo(q, j + RING)
                    if j == 31:
                        done(dve, q, j)
                        add_bias(0, sg, i)
                        dve.sem_inc(g_read, 1)
                    while k < OWN and k * (G_PER - 2 * K16) < (j - 2 * K16 + 1) * OWN:
                        tap(i, k)
                        k += 1
                done(dve, q, G_PER - 1)
                dve.wait_ge(ga_sb, i + 1)
                nc.vector.tensor_tensor(mx[:, :, bass.ds(i * NB, NB)], PS[:, 2:4], sg[:], ALU.mult).then_inc(g_read, 1)

            gated(0, True)
            with dve.Fori(1, G_N) as i:
                gated(i, False)

            def join(b, bank, gate):
                dve.wait_ge(gb_sb, b + 1)
                dve.wait_ge(t_ps, b * 2 + T_Y * 2)
                nc.vector.tensor_tensor(yl2, PS[:, bank:bank + 2], gate[:], ALU.mult).then_inc(yt_sb, 1)
                dve.wait_ge(yt_sb, b + 1)
                nc.vector.tensor_tensor(yl2, yl2, mx[:, :, bass.ds(b * NB, NB)], ALU.add).then_inc(ym_sb, 1)

            def branch_tail(b):
                t_split_lo(b + T_Y, oaH, oaL, b * QT, None)

            k = OWN
            for j in range(2 * Y_PER):
                split_lo(Y_AT // RING, j + RING)
                while k < LONG and (k - OWN) * 5 < (j + 1) * (LONG - OWN):
                    tap(G_N - 1, k)
                    k += 1
                if j == 7:
                    done(dve, Y_AT // RING, j)
                    add_bias(0, sg, G_N)
                    dve.wait_ge(mean_ps, 1)
                    nc.vector.tensor_scalar(mean[:], PS[:, 6, 0:SEQ], 1.0 / DM, None, ALU.mult).then_inc(mean_sb, 1)
                    dve.wait_ge(mean_sb, 1)
                    for u in range(4):
                        nc.vector.tensor_tensor(uT[:, 4 * u:4 * u + 4], uT[:, 4 * u:4 * u + 4],
                                                mean[:, None, :].to_broadcast([P, 4, SEQ]), ALU.subtract).then_inc(uc_sb, 1)
                if j == 9:
                    dve.wait_ge(usq_ps, 4)
                    nc.vector.tensor_scalar(rln[:], PS[:, 7, 0:SEQ], 1.0 / DM, EPS, ALU.mult, ALU.add).then_inc(mean_sb, 1)
                if j == 10:
                    dve.wait_ge(std_sb, 1)
                    nc.vector.reciprocal(rln[:], rln[:]).then_inc(mean_sb, 1)
                    dve.wait_ge(mean_sb, 3)
                    dve.wait_ge(uc_sb, 4)
                    for u in range(4):
                        nc.vector.tensor_tensor(uT[:, 4 * u:4 * u + 4], uT[:, 4 * u:4 * u + 4],
                                                rln[:, None, :].to_broadcast([P, 4, SEQ]), ALU.mult).then_inc(un_sb, 1)
                if 11 <= j <= 14:
                    u = j - 11
                    dve.wait_ge(us_sb, 4 * u + 4)
                    if u > 1:
                        dve.wait_ge(ub_hi, u - 1)
                        dve.wait_ge(ub_lo, u - 1)
                    nc.vector.tensor_tensor(ln_tmp[u % 2], uT[:, 4 * u:4 * u + 4].rearrange("p c n -> p (c n)"),
                                            zbT[:, 4 * u:4 * u + 4].rearrange("p c n -> p (c n)"),
                                            ALU.mult).then_inc(ub_sb, 1)
                    dve.wait_ge(ub_hi, u + 1)
                    nc.vector.tensor_tensor(ubL[:, 4 * u:4 * u + 4].rearrange("p c n -> p (c n)"), ln_tmp[u % 2],
                                            ubH[:, 4 * u:4 * u + 4].rearrange("p c n -> p (c n)").bitcast(F32),
                                            ALU.subtract).then_inc(ub_lo, 1)
                if j == 15:
                    done(dve, Y_AT // RING, j)
                    add_bias(2, sg1, G_N + 1)
                if j == 23:
                    done(dve, Y_AT // RING, j)
                    join(0, 4, sg)
                if j == 26:
                    branch_tail(0)
            done(dve, Y_AT // RING, 2 * Y_PER - 1)
            join(1, 0, sg1)

            def branch(i):
                q = i * (Y_PER // RING) + Y_AT // RING
                for j in range(Y_PER):
                    split_lo(q, j + RING)
                    if j == 2:
                        branch_tail(i - 1)
                    if j == 7:
                        done(dve, q, j)
                        add_bias(2, sg, i + G_N)
                done(dve, q, Y_PER - 1)
                join(i, 4, sg)

            with dve.Fori(2, Y_N) as i:
                branch(i)

            for b in range(4):
                q = (O_AT + b * K16) // RING
                for j in range(K16):
                    split_lo(q, j + RING)
                    if b == 0 and j == 2:
                        branch_tail(Y_N - 1)
                dve.wait_ge(mo_sb, b + 1)
                dve.wait_ge(tail_in, 48)
                nc.vector.tensor_tensor(quarter(mo, b), quarter(mo, b),
                                        rpost[:, b * NB:(b + 1) * NB][:, None, :].to_broadcast([P, NT, NB]),
                                        ALU.mult).then_inc(mp_sb, 1)
            dve.wait_ge(small_hi, 2)
            nc.vector.tensor_tensor(pTl[:], pT[:], pTh[:].bitcast(F32), ALU.subtract).then_inc(small_lo, 1)
            row_total(M_POST)
            for j in range(E_PER):
                split_lo(E_AT // RING, j + RING)
            dve.wait_ge(mp_sb, 4)
            dve.wait_ge(row_rstd, M_POST + 1)
            for u in range(4):
                for t in range(NT):
                    nc.vector.scalar_tensor_tensor(out=quarter(H, u)[:, t], in0=quarter(mo, u)[:, t],
                                                   scalar=rstd[:, M_POST, t:t + 1], in1=quarter(H, u)[:, t],
                                                   op0=ALU.mult, op1=ALU.add).then_inc(x3_sb, 1)

            def norm_x3(u):
                t_split_lo(T_X3 + u, aH, aL, 4 * u, None, 6 - 2 * (u % 2))

            norm_x3(0)
            norm_x3(1)
            for b in range(4):
                q = (PG_AT + b * K16) // RING
                for j in range(K16):
                    if b < 3 or j < K16 - RING:
                        split_lo(q, j + RING)
                    if b == 0 and j in (1, 3):
                        norm_x3((j + 3) // 2)
                dve.wait_ge(sp_sb, b + 1)
                dve.wait_ge(eb_sb, 4)
                nc.vector.tensor_tensor(quarter(eb, b), quarter(eb, b), sgp[:], ALU.mult).then_inc(es_sb, 1)
                if b < 3:
                    dve.wait_ge(row_sq[M_PLE], NT * (b + 1))
                    nc.vector.tensor_tensor(quarter(eb, b), quarter(eb, b),
                                            rple[:, b * NB:(b + 1) * NB][:, None, :].to_broadcast([P, NT, NB]),
                                            ALU.mult).then_inc(ep_sb, 1)
            row_total(M_PLE)
            nc.vector.tensor_tensor(quarter(eb, 3), quarter(eb, 3),
                                    rple[:, 3 * NB:][:, None, :].to_broadcast([P, NT, NB]), ALU.mult).then_inc(ep_sb, 1)
            dve.wait_ge(row_rstd, M_PLE + 1)
            dve.wait_ge(ep_sb, 4)
            for u in range(4):
                for t in range(NT):
                    nc.vector.scalar_tensor_tensor(out=quarter(eb, u)[:, t], in0=quarter(eb, u)[:, t],
                                                   scalar=rstd[:, M_PLE, t:t + 1], in1=quarter(H, u)[:, t],
                                                   op0=ALU.mult, op1=ALU.add).then_inc(out_sb, 1)

        @block.tensor
        def _(pe):
            mm = nc.tensor.matmul

            def chunk_a(q, j, kt, hi, lo, bank, last):
                s = j % RING
                pe.wait_ge(lo_done, q * RING + (RING + j + 1))
                for k in range(KPC):
                    for t in range(NT):
                        out, tok = PS[:, bank + t], slice(t * P, (t + 1) * P)
                        mm(out, hi[:, kt + k, tok], whi[:, s, k], start=kt + k == 0, stop=False)
                        mm(out, hi[:, kt + k, tok], wlo[:, s, k], start=False, stop=False)
                        ins = mm(out, lo[:, kt + k, tok], whi[:, s, k], start=False, stop=last and k == KPC - 1)
                ins.then_inc(multiplied, 1)

            def chunk_b(q, j, kt, bank, last):
                s = j % RING
                pe.wait_ge(lo_done, q * RING + (RING + j + 1))
                for k in range(KPC):
                    for c in range(QT):
                        w = slice(c * P, (c + 1) * P)
                        end = last and k == KPC - 1
                        mm(half(bank, c), whi[:, s, k, w], aH[:, kt + k], start=kt + k == 0 and c % 2 == 0, stop=False,
                           skip_group_check=True)
                        mm(half(bank, c), whi[:, s, k, w], aL[:, kt + k], start=False, stop=False, skip_group_check=True)
                        ins = mm(half(bank, c), wlo[:, s, k, w], aH[:, kt + k], start=False, stop=end,
                                 skip_group_check=True)
                ins.then_inc(multiplied, 1)

            def transpose_tiles(src, bank=6):
                for c in range(QT):
                    for t in range(NT):
                        ins = nc.tensor.transpose(half(bank, c)[:, t * P:(t + 1) * P], src[:, t, c * P:(c + 1) * P], ident)
                    if c % 2:
                        ins.then_inc(t_ps, 1)

            def quarter(v, b):
                return v[:, :, b * NB:(b + 1) * NB]

            def spread(use, u, src, ready, value):
                pe.wait_ge(ready, value)
                if use + u > 1:
                    pe.wait_ge(t_lo, (use + u - (1 if u else 0)) * QT)
                transpose_tiles(quarter(src, u), 6 - 2 * (u % 2))

            pe.sem_inc(multiplied, RING)
            pe.wait_ge(con_in, 32)
            spread(T_N1, 0, H, x_in[0], 16)
            spread(T_N1, 1, H, x_in[1], 16)

            def head_tail(i):
                pe.wait_ge(oz_sb, i + 1)
                transpose_tiles(oR)

            def head(i, first):
                q = i * (R_PER // RING) + R_AT // RING
                for j in range(R_PER):
                    if first and j in (0, 2, 4, 6):
                        if j in (2, 4):
                            spread(T_N1, j // 2 + 1, H, x_in[j // 2 + 1], 16)
                        pe.wait_ge(t_lo, (T_N1 + j // 2 + 1) * QT)
                    chunk_a(q, j, (j % K16) * KPC, aH, aL, 2 * (j // K16), j % K16 == K16 - 1)
                    if not first and j == 1:
                        head_tail(i - 1)
                    if j == 11:
                        pe.wait_ge(rope_done, i * 2 + 2)
                        if first:
                            pe.wait_ge(t_lo, T_R * QT)
                        else:
                            pe.wait_ge(t_lo, i * QT + T_R * QT)
                        for e in range(4):
                            for t in range(NT):
                                at = (e % 2) * SEQ + t * P
                                ins = nc.tensor.transpose(PS[:, 6 + e // 2, at:at + P], roped[:, t, e // 2, e % 2], ident)
                        ins.then_inc(qkT_ps, 1)
                    if j == 15:
                        pe.wait_ge(qkT_sb, i + 1)
                        for h in range(2):
                            mm(PS[:, 6, 0:SEQ], qkT[:, 1, h, 0:P], qkT[:, 0, h, :], start=h == 0, stop=h == 1,
                               skip_group_check=True)
                            ins = mm(PS[:, 6, SEQ:3 * P], qkT[:, 1, h, P:SEQ], qkT[:, 0, h, P:SEQ], start=False,
                                     stop=h == 1, skip_group_check=True)
                        ins.then_inc(sT_ps, 1)
                    if j == 19:
                        pe.wait_ge(sT_sb, i + 1)
                        pe.wait_ge(v_sb, i + 1)
                        mm(PS[:, 6], sT[:, 0:P], vR[:, 0], start=True, stop=True)
                        mm(PS[:, 7], sT[:, P:SEQ], vR[:, 0], start=True, stop=False)
                        mm(PS[:, 7], sT[:, SEQ:3 * P], vR[:, 1], start=False, stop=True).then_inc(o_ps, 1)

            head(0, True)
            with pe.Fori(1, R_N) as i:
                head(i, False)
            for b in range(4):
                q = (RO_AT + b * K32) // RING
                pe.wait_ge(h_out, b + 1)
                for j in range(K32):
                    if b == 0 and j == K32 - 2:
                        pe.wait_ge(t_lo, (T_R + R_N) * QT)
                    chunk_a(q, j, j * KPC, oH, oL, 2 * (b % 2), j == K32 - 1)
                    if b == 0 and j == 1:
                        head_tail(R_N - 1)
                    if b and j == 2:
                        pe.wait_ge(h_out, 2 + b)
                        pe.wait_ge(t_lo, (T_N2 + b - 1) * QT)
                        transpose_tiles(quarter(H, b - 1))

            def group(i, first):
                q = i * (P_PER // RING) + P_AT // RING
                for j in range(4 * K16):
                    b = j // K16
                    if j == 16 or j == 24:
                        pe.wait_ge(pu_sb, i * 2 + (b - 1))
                    if first and j == 6:
                        pe.wait_ge(t_lo, (T_N2 + 4) * QT)
                    chunk_a(q, j, (j % K16) * KPC, aH, aL, 2 * (b % 2), j % K16 == K16 - 1)
                    if j == 1:
                        if first:
                            pe.wait_ge(h_out, 2 + 4)
                            pe.wait_ge(t_lo, (T_N2 + 3) * QT)
                            transpose_tiles(quarter(H, 3))
                        else:
                            group_tail(i - 1, 1)
                    if j == 19:
                        pe.wait_ge(pu_sb, i * 2 + 2)
                        pe.wait_ge(pm_in, i * 16 + 16)
                        for c in range(8):
                            out = half(4, c)
                            mm(out, pU[:, 0, c * P:(c + 1) * P], pM[:, 0:SEQ], start=c % 2 == 0, stop=False,
                               skip_group_check=True)
                            ins = mm(out[:, P:], pU[:, 1, c * P:(c + 1) * P], pM[:, SEQ:], start=False, stop=True,
                                     skip_group_check=True)
                            if c % 2:
                                ins.then_inc(mix_ps, 1)
                pe.wait_ge(mix_lo, i * 4 + 4)
                for w in range(2):
                    pe.wait_ge(pz_sb, i * 2 + (w + 1))
                    for k in range(4):
                        chunk_a(q, 4 * K16 + 4 * w + k, k * KPC, mH, mL, 2 * w, k == 3)
                        if w == 1 and k == 2:
                            group_tail(i, 0)

            def group_tail(i, w):
                pe.wait_ge(mz_sb, i * 2 + (w + 1))
                pe.wait_ge(t_lo, i * (2 * QT) + (T_P + w) * QT)
                transpose_tiles(mz)

            group(0, True)
            with pe.Fori(1, P_N) as i:
                group(i, False)
            for b in range(4):
                q = (PO_AT + b * K32) // RING
                pe.wait_ge(h_out, 4 + b + 1)
                for j in range(K32):
                    if b == 0 and j == K32 - 2:
                        pe.wait_ge(t_lo, (T_P + 8) * QT)
                    chunk_a(q, j, j * KPC, oH, oL, 2 * (b % 2), j == K32 - 1)
                    if b == 0 and j == 1:
                        group_tail(P_N - 1, 1)

            def norm3(u):
                spread(T_N3, u, XS, xs_done, NT * (u + 1))

            norm3(0)
            norm3(1)

            def by_head(bank, lhsT, rhs, tiles=range(NT)):
                for n, t in enumerate(tiles):
                    for h in range(HG):
                        ins = mm(PS[:, bank + n, h * P:(h + 1) * P], lhsT(t, h), rhs(t, h), start=h == 0, stop=True,
                                 skip_group_check=True)
                return ins

            def turn(bank, src):
                for t in range(NT):
                    for h in range(HG):
                        ins = nc.tensor.transpose(PS[:, bank + t, h * P:(h + 1) * P], src(t, h), ident)
                return ins

            def squares(src, bank):
                for t in range(NT):
                    for h in range(HG):
                        ins = mm(PS[:, bank, t * HG + h:t * HG + h + 1], src[:, h * SEQ + t * P:h * SEQ + (t + 1) * P],
                                 ones[:, 0:1], start=t + h == 0, stop=True, skip_group_check=True)
                ins.then_inc(sq_ps, 1)

            def delta_tail(i, j):
                if j == 0:
                    pe.wait_ge(st_sb, i + 1)
                    pe.wait_ge(sqn_sb, i * 2 + 2)
                    by_head(5, lambda t, h: knT[:, t, h], lambda t, h: st[:, h], [1])
                    by_head(6, lambda t, h: kqv[:, 1, h, t * P:(t + 1) * P], lambda t, h: st[:, h], [1])
                    by_head(7, lambda t, h: qk[:, t, h], lambda t, h: vn[:, t, h], [0]).then_inc(r1_ps, 1)
                if j == 1:
                    pe.wait_ge(vb1_sb, i + 1)
                    by_head(4, lambda t, h: iU[:, t, h], lambda t, h: vb[:, t, h], [1]).then_inc(vn1_ps, 1)
                if j == 2:
                    pe.wait_ge(vn1_sb, i + 1)
                    by_head(5, lambda t, h: qk[:, t, h], lambda t, h: vn[:, t, h], [1]).then_inc(o1_ps, 1)
                if j == 5:
                    pe.wait_ge(od_sb, i + 1)
                    transpose_tiles(oD)

            def delta(i, first):
                q = i * (D_PER // RING) + D_AT // RING
                for j in range(D_PER):
                    b = j // K16
                    if j == 2 * K16 or j == 3 * K16:
                        pe.wait_ge(conv_tap, i * 48 + 16 * (b - 1))
                    if first and j in (0, 2, 4, 6):
                        if j in (2, 4):
                            norm3(j // 2 + 1)
                        pe.wait_ge(t_lo, (T_N3 + j // 2 + 1) * QT)
                    if b < 3:
                        chunk_b(q, j, (j % K16) * KPC, 2 * (b % 2), j % K16 == K16 - 1)
                    else:
                        chunk_a(q, j, (j % K16) * KPC, aH, aL, 2 * (b % 2), j % K16 == K16 - 1)
                    if not first:
                        delta_tail(i - 1, j)
                    if first and j == 7:
                        pe.wait_ge(small_lo, 1)
                        for t in range(NT):
                            for k in range(16):
                                out, tok = PS[:, 4, t * 32:(t + 1) * 32], slice(t * P, (t + 1) * P)
                                mm(out, aH[:, k, tok], wbh[:, k], start=k == 0, stop=False)
                                mm(out, aH[:, k, tok], wbl[:, k], start=False, stop=False)
                                ins = mm(out, aL[:, k, tok], wbh[:, k], start=False, stop=k == 15)
                        ins.then_inc(ba_ps, 1)
                    if first and j == 8:
                        pe.wait_ge(gl_sb, 1)
                        for t in range(NT):
                            ins = mm(PS[:, 5, t * DN_HEADS:(t + 1) * DN_HEADS], upper, gl[:, t], start=True, stop=True)
                        ins.then_inc(cum_ps, 1)
                    if j == 9:
                        if first:
                            pe.wait_ge(cum_sb, 1)
                        pe.wait_ge(gu_sb, i + 1)
                        for t in range(NT):
                            ins = mm(PS[:, 4 + t], ones, gm[:, t].rearrange("p h n -> p (h n)"), start=True, stop=True)
                        ins.then_inc(gu_ps, 1)
                    if j == 10:
                        pe.wait_ge(sq_sb, i * 2 + 1)
                        squares(kb[:].rearrange("p t h n -> p (t h n)"), 6)
                        pe.wait_ge(dt_sub, i * 2 + 1)
                        turn(4, lambda t, h: kqv[:, 0, h, t * P:(t + 1) * P]).then_inc(k_ps, 1)
                    if j == 12:
                        pe.wait_ge(sqn_sb, i * 2 + 1)
                        pe.wait_ge(kb_sb, i + 1)
                        turn(4, lambda t, h: kn[:, t, h])
                        turn(6, lambda t, h: kb[:, t, h]).then_inc(kt_ps, 1)
                    if j == 13:
                        pe.wait_ge(kt_sb, i * 2 + 2)
                        by_head(4, lambda t, h: knT[:, t, h], lambda t, h: kbT[:, t, h]).then_inc(a_ps, 1)
                    if j == 14:
                        pe.wait_ge(u0_sb, i + 1)
                        turn(4, lambda t, h: iU[:, t, h]).then_inc(t0_ps, 1)
                    if 15 <= j <= 26:
                        lv = (j - 13) // 2
                        if j % 2:
                            if lv == 1:
                                pe.wait_ge(t0_sb, i + 1)
                            else:
                                pe.wait_ge(tu_sb, i * (2 * LEVELS - 3) + 2 * (lv - 1))
                            pe.wait_ge(lv_sb, i * (LEVELS - 1) + lv)
                            below = kbT if lv % 2 else kb
                            by_head(4, lambda t, h: below[:, t, h], lambda t, h: iT[:, t, h]).then_inc(m1_ps, 1)
                        else:
                            pe.wait_ge(m1_sb, i * (LEVELS - 1) + lv)
                            if lv < LEVELS - 1:
                                by_head(4, lambda t, h: iU[:, t, h], lambda t, h: gm[:, t, h])
                            by_head(6, lambda t, h: gm[:, t, h], lambda t, h: iU[:, t, h]).then_inc(tu_ps, 1)
                    if j == 27:
                        pe.wait_ge(tu_sb, i * (2 * LEVELS - 3) + (2 * LEVELS - 3))
                        pe.wait_ge(kqv_sb, i * 3 + 3)
                        by_head(6, lambda t, h: knT[:, t, h],
                                lambda t, h: kqv[:, 1, h, t * P:(t + 1) * P]).then_inc(qk_ps, 1)
                    if j == 28:
                        pe.wait_ge(kqv_sb, i * 3 + 4)
                        turn(4, lambda t, h: kqv[:, 2, h, t * P:(t + 1) * P]).then_inc(v_ps, 1)
                    if j == 29:
                        pe.wait_ge(qk_sb, i + 1)
                        pe.wait_ge(sq_sb, i * 2 + 2)
                        squares(zD[:].rearrange("p t n -> p (t n)"), 6)
                        pe.wait_ge(vb_sb, i + 1)
                        by_head(7, lambda t, h: iU[:, t, h], lambda t, h: vb[:, t, h], [0]).then_inc(vn0_ps, 1)
                    if j == 30:
                        pe.wait_ge(vn0_sb, i + 1)
                        pe.wait_ge(ke_sb, i + 1)
                        by_head(4, lambda t, h: ke[:, h], lambda t, h: vn[:, t, h], [0]).then_inc(st_ps, 1)

            delta(0, True)
            with pe.Fori(1, D_N) as i:
                delta(i, False)

            def gated(i, first):
                q = i * (G_PER // RING) + G_AT // RING
                for j in range(G_PER):
                    b, k, last = j // K16, (j % K16) * KPC, j % K16 == K16 - 1
                    if k == 0:
                        if b < 2:
                            pe.wait_ge(g_read, i * 3 + (2 + b))
                            if b and first:
                                pe.wait_ge(zd_sb, D_N)
                        if b == 2:
                            pe.wait_ge(zb_sb, i + 1)
                        if b == 3:
                            pe.wait_ge(g_read, i * 3 + 4)
                            if first:
                                pe.wait_ge(t_lo, (T_D + D_N) * QT)
                    if b < 3:
                        chunk_b(q, j, k, 2 * b, last)
                    elif b == 3:
                        chunk_a(q, j, k, aH, aL, 0, last)
                    else:
                        chunk_a(q, j, k, oaH, oaL, 2, last)
                    if first:
                        delta_tail(D_N - 1, j)

            gated(0, True)
            with pe.Fori(1, G_N) as i:
                gated(i, False)

            def branch_tail(b):
                pe.wait_ge(ym_sb, b + 1)
                pe.wait_ge(t_lo, b * QT + T_Y * QT)
                transpose_tiles(yl2)

            for j in range(2 * Y_PER):
                b, k, last = j // K16, (j % K16) * KPC, j % K16 == K16 - 1
                q = Y_AT // RING
                if j == 0:
                    pe.wait_ge(g_read, G_N * 3 + 2)
                if j == K16:
                    pe.wait_ge(g_read, G_N * 3 + 3)
                if j == 2 * K16:
                    pe.wait_ge(zb_sb, G_N + 1)
                    pe.wait_ge(ub_lo, 4)
                if j == 3 * K16:
                    pe.wait_ge(gate_add, G_N + 1)
                if b < 2:
                    chunk_a(q, j, k, aH, aL, 2 * b, last)
                else:
                    chunk_a(q, j, k, ubH, ubL, (4, 0)[b - 2], last)
                if j == 6:
                    for c in range(QT):
                        pe.wait_ge(long_tap[c], G_N * LONG)
                    for n in range(16):
                        ins = mm(PS[:, 6, 0:SEQ], ones, uT[:, n], start=n == 0, stop=n == 15)
                    ins.then_inc(mean_ps, 1)
                if j == 9:
                    for u in range(4):
                        pe.wait_ge(usq_sb, u + 1)
                        for c in range(QT):
                            ins = mm(PS[:, 7, 0:SEQ], ones, ln_tmp[u % 2][:, c * SEQ:(c + 1) * SEQ],
                                     start=u + c == 0, stop=u + c == 6)
                        ins.then_inc(usq_ps, 1)
                if j == 26:
                    branch_tail(0)

            def branch(i):
                q = i * (Y_PER // RING) + Y_AT // RING
                for j in range(Y_PER):
                    b, k, last = j // K16, (j % K16) * KPC, j % K16 == K16 - 1
                    if j == 0:
                        pe.wait_ge(gate_add, i + G_N)
                    if j == K16:
                        pe.wait_ge(ym_sb, i - 1)
                    chunk_a(q, j, k, (aH, ubH)[b], (aL, ubL)[b], 2 + 2 * b, last)
                    if j == 2:
                        branch_tail(i - 1)

            with pe.Fori(2, Y_N) as i:
                branch(i)
            for b in range(4):
                q = (O_AT + b * K16) // RING
                if b == 1:
                    pe.wait_ge(gate_add, 2 * G_N)
                if b > 1:
                    pe.wait_ge(row_sq[M_POST], NT * (b - 1))
                for j in range(K16):
                    if b == 0 and j == K16 - 2:
                        pe.wait_ge(t_lo, (T_Y + Y_N) * QT)
                    chunk_a(q, j, j * KPC, oaH, oaL, 2 * (b % 2), j == K16 - 1)
                    if b == 0 and j == 2:
                        branch_tail(Y_N - 1)
            pe.wait_ge(small_lo, 2)
            for j in range(E_PER):
                if j > 1:
                    pe.wait_ge(eb_sb, j - 1)
                else:
                    pe.wait_ge(row_sq[M_POST], NT * (3 + j))
                chunk_a(E_AT // RING, j, 0, pTh, pTl, 2 * (j % 2), True)

            def norm_x3(u):
                spread(T_X3, u, H, x3_sb, NT * (u + 1))

            norm_x3(0)
            norm_x3(1)
            for b in range(4):
                q = (PG_AT + b * K16) // RING
                if b < 2:
                    pe.wait_ge(eb_sb, 3 + b)
                else:
                    pe.wait_ge(sp_sb, b - 1)
                for j in range(K16):
                    if b == 0 and j in (0, 2, 4, 6):
                        if j in (2, 4):
                            norm_x3(j // 2 + 1)
                        pe.wait_ge(t_lo, (T_X3 + j // 2 + 1) * QT)
                    chunk_a(q, j, j * KPC, aH, aL, 2 * (b % 2), j == K16 - 1)


def constants():
    f8, f4 = np.float64, np.float32
    i, t = np.arange(P), np.arange(SEQ)
    con = np.zeros((P, 4, P), f4)
    con[:, 0] = np.eye(P)
    con[:, 1] = 1
    con[:, 2] = i[:, None] <= i[None, :]
    con[:, 3] = np.where(i[:, None] <= i[None, :], 0, -30000.0)

    inverse = np.power(f4(10000.0), -np.arange(HALF, dtype=f4) / f4(HALF)).astype(f4)
    angle = (t.astype(f4)[:, None] * inverse[None, :]).astype(f8)
    rot = np.stack([np.cos(angle), np.sin(angle)]).astype(f4)
    rot = rot.reshape(2, NT, P, HALF).transpose(2, 0, 1, 3)

    later = t[None, :] - t[:, None]
    log_decay = np.log1p(-np.exp2(-5.0 - np.arange(RET_HEADS, dtype=f8)))
    decay = np.where(later >= 0, np.exp(np.maximum(later, 0) * log_decay[:, None, None]), 0) * RET_QK ** -0.5
    dmask = np.concatenate([decay[:, :P], decay[:, P:, P:]], axis=2).transpose(1, 0, 2)

    pm = []
    for w in POOL_WINDOWS:
        m = np.where((later >= 0) & (later < w), 1 / np.minimum(t + 1, w)[None, :], 0) - np.eye(SEQ)
        pm.append(np.concatenate([m[:P], m[P:, P:]], axis=1))

    lm = np.zeros((P, LEVELS, P), f4)
    for lv in range(LEVELS):
        b = i >> lv
        lm[:, lv] = (b[:, None] // 2 == b[None, :] // 2) & (b[:, None] % 2 == 0) & (b[None, :] % 2 == 1)
    return {"con": con, "rot": rot, "dmask": dmask.astype(f4), "pm": np.stack(pm).astype(f4), "lm": lm}


def chunks(w, columns):
    out = []
    for c in columns:
        block = np.concatenate([w[:, a:b] for a, b in c], axis=1) if isinstance(c, tuple) else w[:, c:c + NB]
        out.append(block.reshape(-1, KPC, P, NB).transpose(0, 2, 1, 3).reshape(-1, P, KPC * NB))
    return out


def stream(a):
    qk, v = RET_QK, 2 * DM
    w, out = a["ret_w_in"][0], []
    for h in range(RET_HEADS):
        out += chunks(w, [((h * qk, (h + 1) * qk), (DM + h * qk, DM + (h + 1) * qk)), v + h * NB, v + RET_V + h * NB])
    whole = range(0, DM, NB)
    out += chunks(a["ret_w_out"][0], whole)
    w = a["pool_w_in"][0]
    for g in range(GROUPS):
        u, z = g * GDIM, 2 * DM + g * GDIM
        out += chunks(w, [u, u + NB, z, z + NB]) + chunks(a["pool_w_grp"][0][g], [0, NB])
    out += chunks(a["pool_w_out"][0], whole)
    w = a["w_in_2"][0]
    z_a, glu = 3 * DM, 4 * DM + 2 * DN_HEADS
    z_b, gate = glu + 2 * DM, glu + 3 * DM
    for n in whole:
        out += chunks(w, [DM + n, n, 2 * DM + n, z_a + n])
    for n in whole:
        out += chunks(w, [glu + n, glu + DM + n, z_b + n, gate + n]) + chunks(a["w_br_a_2"][0], [n])
    for ns in ([0, NB], [2 * NB], [3 * NB]):
        out += chunks(w, [gate + DM + n for n in ns]) + chunks(a["w_br_b_2"][0], ns)
    for name in ("w_out_2", "w_ple_proj_2", "w_ple_gate_2"):
        out += chunks(a[name][0], whole)
    return np.concatenate(out)


def arrays_of(inputs):
    a = {k: np.asarray(v) for k, v in inputs.items()}

    def by_partition(v):
        return v.reshape(-1, P).T

    gates = 4 * DM
    arrays = {
        "x": a["x"][0],
        "stream": stream(a),
        "cols": np.concatenate([by_partition(a[k]) for k in (
            "ret_norm", "ret_gn", "pool_norm", "pool_scale", "g_pre_2", "g_dn_out_2", "ln_g_2", "ln_b_2",
            "b_dw_2")], axis=1),
        "pool_b": a["pool_b_grp"].reshape(GROUPS, 1, GDIM),
        "final_norm": a["final_norm"].reshape(1, DM),
        "w_ba": a["w_in_2"][0][:, gates:gates + 2 * DN_HEADS].reshape(16, P, 2 * DN_HEADS).transpose(1, 0, 2),
        "dt_bias": a["dt_bias_2"],
        "a_log": a["a_log_2"],
        "w_conv": a["w_conv_qkv_2"][0].reshape(TAPS, 48, P).transpose(2, 1, 0).reshape(P, -1),
        "w_long": a["w_dw_2"][0].reshape(LONG, 16, P).transpose(2, 1, 0).reshape(P, -1),
        "b_gate": a["b_gate_2"].reshape(8, 1, NB),
        "pT": a["p_2"][0, 0].reshape(SEQ, 2, P).transpose(2, 1, 0),
        "g_post": a["g_post_2"],
        "g_ple": a["g_ple_2"],
    }
    arrays.update(constants())
    return {k: np.ascontiguousarray(v) for k, v in arrays.items()}


def kernel(**inputs):
    import concourse.bacc as bacc
    from concourse.bass_utils import run_bass_kernel_spmd

    nc = bacc.Bacc("TRN2", target_bir_lowering=False, num_devices=1)
    arrays, dram = {}, {}
    for name, a in arrays_of(inputs).items():
        arrays[f"in_{name}"] = a
        dram[name] = nc.dram_tensor(f"in_{name}", a.shape, mybir.dt.from_np(a.dtype), kind="ExternalInput").ap()
    dram["out"] = nc.dram_tensor("out_0", (SEQ, DM), F32, kind="ExternalOutput").ap()
    build(nc, dram)
    r = run_bass_kernel_spmd(nc, [arrays], core_ids=[0])
    return r.results[0]["out_0"].reshape(1, SEQ, DM)
```

```python
from contextlib import ExitStack

import concourse.bass as bass
import numpy as np
from concourse import mybir

F32 = mybir.dt.float32
F32R = mybir.dt.float32r
ALU = mybir.AluOpType
ACT = mybir.ActivationFunctionType
AX = mybir.AxisListType

P = 128
SEQ = 256
NT = SEQ // P
DM = 2048
EPS = 1e-6
NB = 512
QT = NB // P
KPC = 2
RING = 4
K16 = DM // (KPC * P)
K32 = 2 * K16

RET_HEADS = 8
RET_QK = DM // RET_HEADS
HALF = RET_QK // 2
RET_V = 2 * DM
POOL_WINDOWS = (2, 4, 8, 16)
GROUPS = len(POOL_WINDOWS)
GDIM = 2 * DM // GROUPS
DN_HEADS = 16
HG = 4
TAPS = 4
LONG = 31
LEVELS = 7

R_PER, R_N = 3 * K16, RET_HEADS
RO_PER, RO_N = 2 * K32, 2
P_PER, P_N = 4 * K16 + 2 * (GDIM // (KPC * P)), GROUPS
D_PER, D_N = 4 * K16, 4
G_PER, G_N = 5 * K16, 4
Y_PER, Y_N = 2 * K16, 4
O_PER, O_N = 2 * K16, 2
E_PER = 4
R_AT = 0
RO_AT = R_AT + R_PER * R_N
P_AT = RO_AT + RO_PER * RO_N
PO_AT = P_AT + P_PER * P_N
D_AT = PO_AT + RO_PER * RO_N
G_AT = D_AT + D_PER * D_N
Y_AT = G_AT + G_PER * G_N
O_AT = Y_AT + Y_PER * Y_N
E_AT = O_AT + O_PER * O_N
PG_AT = E_AT + E_PER
CHUNKS = PG_AT + O_PER * O_N
LN_AT = 14

C_RN = 0
C_GN = C_RN + 16
C_PN = C_GN + 32
C_PS = C_PN + 16
C_PRE = C_PS + 32
C_DN = C_PRE + 16
C_LNG = C_DN + 1
C_LNB = C_LNG + 16
C_BDW = C_LNB + 16
C_WIN = C_BDW + 16
C_END = C_WIN + GROUPS * NT

T_N1, T_R, T_N2, T_P, T_N3, T_D, T_Y, T_X3 = 0, 4, 12, 16, 24, 28, 32, 36
M_N1, M_N2, M_FN, M_N3, M_POST, M_PLE = range(6)


def build(nc, dram):
    with ExitStack() as outer:
        sem_of = {}

        def sem(name):
            if name not in sem_of:
                sem_of[name] = outer.enter_context(nc.semaphore(name))
            return sem_of[name]

        def sb(stack, name, shape, dt=F32):
            return stack.enter_context(nc.sbuf_tensor(name, shape, dt))

        raw = sb(outer, "raw", [P, RING, KPC, NB])
        whi = sb(outer, "whi", [P, RING, KPC, NB], F32R)
        wlo = sb(outer, "wlo", [P, RING, KPC, NB], F32R)
        H = sb(outer, "H", [P, NT, DM])
        aH = sb(outer, "aH", [P, 16, SEQ], F32R)
        aL = sb(outer, "aL", [P, 16, SEQ], F32R)
        cols = sb(outer, "cols", [P, C_END])
        con = sb(outer, "con", [P, 4, P])
        ident, ones, upper, maskneg = (con[:, n, :] for n in range(4))
        part = sb(outer, "part", [P, 6, NT, 4])
        ssq = sb(outer, "ssq", [P, 6, NT])
        ms = sb(outer, "ms", [P, 6, NT])
        rstd = sb(outer, "rstd", [P, 6, NT])
        both = sb(outer, "both", [P, NT])
        mhalf = sb(outer, "mhalf", [P, 16])
        epsilon = sb(outer, "epsilon", [P, 16])
        carrier = sb(outer, "carrier", [P, 1])
        PS = outer.enter_context(nc.psum_tensor("PS", [P, 8, NB], F32))

        with ExitStack() as s:
            XS = sb(s, "XS", [P, NT, DM])
        with ExitStack() as s:
            oH = sb(s, "oH", [P, 32, SEQ], F32R)
            oL = sb(s, "oL", [P, 32, SEQ], F32R)
            with ExitStack() as r:
                dmask = sb(r, "dmask", [P, RET_HEADS, 3 * P])
                rot = sb(r, "rot", [P, 2, NT, HALF])
                with ExitStack() as b:
                    sTL = sb(b, "sTL", [P, 3 * P], F32R)
                roped = sb(r, "roped", [P, NT, 2, 2, HALF])
                rt = sb(r, "rt", [P, 2, NT, 2, HALF])
                sT = rt[:].rearrange("p a t h n -> p (a t h n)")[:, 0:3 * P]
                qkT = sb(r, "qkT", [P, 2, 2, SEQ])
                vH = sb(r, "vH", [P, NT, NB], F32R)
                vL = sb(r, "vL", [P, NT, NB], F32R)
                zR = sb(r, "zR", [P, NT, NB])
                sTH = sb(r, "sTH", [P, 3 * P], F32R)
                oR = sb(r, "oR", [P, NT, NB])
                bst = sb(r, "bst", [P, NT, 6])
                mv = sb(r, "mv", [P, NT, 2])
                rvar = sb(r, "rvar", [P, NT])
                rrs = sb(r, "rrs", [P, NT])
            with ExitStack() as r:
                with ExitStack() as b:
                    mz = sb(b, "mz", [P, NT, NB])
                    pB = sb(b, "pB", [P, GDIM])
                pUH = sb(r, "pUH", [P, NT, GDIM], F32R)
                pUL = sb(r, "pUL", [P, NT, GDIM], F32R)
                pZ = sb(r, "pZ", [P, NT, GDIM])
                mH = sb(r, "mH", [P, 8, SEQ], F32R)
                mL = sb(r, "mL", [P, 8, SEQ], F32R)
                pM = sb(r, "pM", [P, 3 * P])
                pMH = sb(r, "pMH", [P, 3 * P], F32R)
            with ExitStack() as r:
                row = sb(r, "row", [P, DM])
                junk = sb(r, "junk", [P, 2, NT, NB])
        with ExitStack() as s:
            oaH = sb(s, "oaH", [P, 16, SEQ], F32R)
            oaL = sb(s, "oaL", [P, 16, SEQ], F32R)
            with ExitStack() as r:
                beta = sb(r, "beta", [P, NT, DN_HEADS])
                cum = sb(r, "cum", [P, NT, DN_HEADS])
                ecum = sb(r, "ecum", [P, NT, DN_HEADS])
                becum = sb(r, "becum", [P, NT, DN_HEADS])
                gl = sb(r, "gl", [P, NT, DN_HEADS])
                wcv = sb(r, "wcv", [P, 3 * 16 * TAPS])
                lmask = sb(r, "lmask", [P, LEVELS, P])
                yD = sb(r, "yD", [P, HG, SEQ])
                kqv = sb(r, "kqv", [P, 3, HG, SEQ])
                zD = sb(r, "zD", [P, NT, NB])
                gm = sb(r, "gm", [P, NT, HG, P])
                dT = sb(r, "dT", [P, NT, HG, P])
                kn = sb(r, "kn", [P, NT, HG, P])
                kb = sb(r, "kb", [P, NT, HG, P])
                vb = sb(r, "vb", [P, NT, HG, P])
                knT = sb(r, "knT", [P, NT, HG, P])
                kbT = sb(r, "kbT", [P, NT, HG, P])
                aT = sb(r, "aT", [P, NT, HG, P])
                qk = sb(r, "qk", [P, NT, HG, P])
                iT = sb(r, "iT", [P, NT, HG, P])
                with ExitStack() as b:
                    wbr = sb(b, "wbr", [P, 16, 32])
                    wbh = sb(b, "wbh", [P, 16, 32], F32R)
                    wbl = sb(b, "wbl", [P, 16, 32], F32R)
                    dtb = sb(b, "dtb", [P, DN_HEADS])
                    alog = sb(b, "alog", [P, DN_HEADS])
                    ea = sb(b, "ea", [P, DN_HEADS])
                    ad = sb(b, "ad", [P, NT, DN_HEADS])
                    sp1 = sb(b, "sp1", [P, NT, DN_HEADS])
                    sp2 = sb(b, "sp2", [P, NT, DN_HEADS])
                iU = sb(r, "iU", [P, NT, HG, P])
                vn = sb(r, "vn", [P, NT, HG, P])
                ke = sb(r, "ke", [P, HG, P])
                sqn = sb(r, "sqn", [P, 2, NT, HG])
                rqk = sb(r, "rqk", [P, 2, NT, HG])
                oms = sb(r, "oms", [P, 3, NT, HG])
            st = kbT[:, 0]
            oD = yD[:].rearrange("p (t x) n -> p t (x n)", t=NT)
            with ExitStack() as r:
                uT = sb(r, "uT", [P, 16, SEQ])
                zbT = sb(r, "zbT", [P, 16, SEQ])
                mx = sb(r, "mx", [P, NT, DM])
                up = sb(r, "up", [P, QT, LONG - 1 + SEQ])
                sg = sb(r, "sg", [P, NT, NB])
                sg1 = sb(r, "sg1", [P, NT, NB])
                yl = sb(r, "yl", [P, QT, SEQ])
                yl2 = yl[:].rearrange("p (t x) n -> p t (x n)", t=NT)
                bg = sb(r, "bg", [P, NB])
                wdw = sb(r, "wdw", [P, 16 * LONG])
                wl = sb(r, "wl", [P, QT * LONG])
                mean = sb(r, "mean", [P, SEQ])
                rln = sb(r, "rln", [P, SEQ])
                ln_tmp = (up[:].rearrange("p c n -> p (c n)")[:, 0:QT * SEQ], yl[:].rearrange("p c n -> p (c n)"))
            with ExitStack() as r:
                ubH = sb(r, "ubH", [P, 16, SEQ], F32R)
                ubL = sb(r, "ubL", [P, 16, SEQ], F32R)
            with ExitStack() as r:
                mo = sb(r, "mo", [P, NT, DM])
                eb = sb(r, "eb", [P, NT, DM])
                rpost = sb(r, "rpost", [P, DM])
                rple = sb(r, "rple", [P, DM])
                pT = sb(r, "pT", [P, NT, SEQ])
                pTh = sb(r, "pTh", [P, NT, SEQ], F32R)
                pTl = sb(r, "pTl", [P, NT, SEQ], F32R)
                sgp = sb(r, "sgp", [P, NT, NB])
                junk2 = sb(r, "junk2", [P, 2, NT, NB])

        block = outer.enter_context(nc.Block())

        con_in, rot_in = sem("con_in"), sem("rot_in")
        x_in = [sem(f"x_in{n}") for n in range(4)]
        raw_in = [sem(f"raw_in{n}") for n in range(RING)]
        hi_done = sem("hi_done")
        lo_done = sem("lo_done")
        multiplied = sem("multiplied")
        t_ps, t_hi, t_lo = sem("t_ps"), sem("t_hi"), sem("t_lo")
        row_sq = [sem(f"row_sq{n}") for n in range(6)]
        row_sum, row_ms, row_rstd, rows_sb = sem("row_sum"), sem("row_ms"), sem("row_rstd"), sem("rows_sb")
        rot_scaled, fn_t, both_done = sem("rot_scaled"), sem("fn_t"), sem("both_done")
        const_set = sem("const_set")
        h_out = sem("h_out")
        stored = sem("stored")
        rope_t, rope_done, qkT_ps, qkT_sb, sT_ps, sT_sb, v_sb, o_ps = (
            sem(n) for n in "rope_t rope_done qkT_ps qkT_sb sT_ps sT_sb v_sb o_ps".split())
        bst_done, rrs_done, on_sb, z_sb, oz_sb = (
            sem(n) for n in "bst_done rrs_done on_sb z_sb oz_sb".split())
        pu_sb, pu_lo, pz_sb, mix_ps, mix_hi, mix_lo, pm_in, pb_in, mz_add, mz_sb, pb_used = (
            sem(n) for n in "pu_sb pu_lo pz_sb mix_ps mix_hi mix_lo pm_in pb_in mz_add mz_sb pb_used".split())
        row_in = sem("row_in")
        ba_in, small_hi, small_lo, ba_ps, beta_sb, ad_sb, ea_sb, sp_a, gl_sb, cum_ps, cum_sb, ecum_sb = (
            sem(n) for n in ("ba_in small_hi small_lo ba_ps beta_sb ad_sb ea_sb sp_a gl_sb cum_ps cum_sb "
                             "ecum_sb").split())
        dn_in, conv_tap, kqv_sb, gu_sb, gu_ps, dt_sub, dt_sb, sq_sb, sq_ps, sqn_sb, rqk_sb = (
            sem(n) for n in "dn_in conv_tap kqv_sb gu_sb gu_ps dt_sub dt_sb sq_sb sq_ps sqn_sb rqk_sb".split())
        k_ps, kn_sb, kb_sb, kt_ps, kt_sb, a_ps, a_sb, b0_sb, u0_sb, t0_ps, t0_sb, lv_sb, m1_ps, m1_sb, tu_ps, tu_sb = (
            sem(n) for n in ("k_ps kn_sb kb_sb kt_ps kt_sb a_ps a_sb b0_sb u0_sb t0_ps t0_sb lv_sb m1_ps m1_sb "
                             "tu_ps tu_sb").split())
        qk_ps, qk_sb, v_ps, vb_sb, ke_sb, vn0_ps, vn0_sb, st_ps, st_sb, r1_ps, r1_sb, vb1_sb, o1_sb, iu_ps, iu_sb = (
            sem(n) for n in ("qk_ps qk_sb v_ps vb_sb ke_sb vn0_ps vn0_sb st_ps st_sb r1_ps r1_sb vb1_sb o1_sb "
                             "iu_ps iu_sb").split())
        vn1_ps, vn1_sb, o1_ps, o1s_sb, oq_sb, osq_sb, omean_sb, ors_sb, onr_sb, zd_sb, od_sb = (
            sem(n) for n in ("vn1_ps vn1_sb o1_ps o1s_sb oq_sb osq_sb omean_sb ors_sb onr_sb zd_sb "
                             "od_sb").split())
        g_in, bg_in, sgb_sb, g_read, wl_set, zb_sb, gate_add, ga_sb, fn_t2 = (
            sem(n) for n in "g_in bg_in sgb_sb g_read wl_set zb_sb gate_add ga_sb fn_t2".split())
        long_tap = [sem(f"long_tap{c}") for c in range(QT)]
        mean_ps, mean_sb, uc_sb, usq_sb, usq_ps, std_sb, un_sb, us_sb, ub_sb, ub_hi, ub_lo = (
            sem(n) for n in ("mean_ps mean_sb uc_sb usq_sb usq_ps std_sb un_sb us_sb ub_sb ub_hi "
                             "ub_lo").split())
        gb_sb, yt_sb, ym_sb, mo_sb, tail_in, mp_sb, eb_sb, sp_sb, es_sb, ep_sb, out_sb = (
            sem(n) for n in ("gb_sb yt_sb ym_sb mo_sb tail_in mp_sb eb_sb sp_sb es_sb "
                             "ep_sb out_sb").split())

        def half(bank, c):
            return PS[:, bank + c // 2, (c % 2) * SEQ:(c % 2 + 1) * SEQ]

        def heads(bank):
            return PS[:, bank:bank + 2].rearrange("p t (h n) -> p t h n", h=HG)

        def blocks(v, lv, odd):
            return v.rearrange("p (b two m) -> p two b m", two=2, m=2 ** lv)[:, odd]

        def all_blocks(v, lv, odd):
            return v.rearrange("p t (b two m) -> p (t b) two m", two=2, m=2 ** lv)[:, :, odd]

        def flat(v):
            return v[:].rearrange("p t h n -> p t (h n)")

        def over(v, i):
            return v[:, :, bass.ds(i * HG, HG)][:, :, :, None].to_broadcast([P, NT, HG, P])

        def done(eng, q, j):
            eng.wait_ge(multiplied, q * RING + (RING + j + 1))

        @block.sync
        def _(sp):
            sp.dma_start(con[:], dram["con"]).then_inc(con_in, 16)
            x = dram["x"].rearrange("(t p) n -> p t n", p=P)

            def chunk(q, s):
                sp.wait_ge(lo_done, q * RING + (s + 1))
                sp.dma_start(raw[:, s].rearrange("p k n -> p (k n)"), dram["stream"][q * RING + s]).then_inc(raw_in[s], 16)

            for u in range(4):
                sp.dma_start(H[:, :, u * NB:(u + 1) * NB], x[:, :, u * NB:(u + 1) * NB]).then_inc(x_in[u], 16)
                if u == 0:
                    sp.dma_start(cols[:], dram["cols"]).then_inc(con_in, 16)
                chunk(0, u)
            with sp.Fori(1, CHUNKS // RING) as i:
                for s in range(RING):
                    chunk(i, s)
            out = dram["out"].rearrange("(t p) n -> p t n", p=P)
            for u in range(4):
                sp.wait_ge(out_sb, NT * (u + 1))
                sp.dma_start(out[:, :, u * NB:(u + 1) * NB], eb[:, :, u * NB:(u + 1) * NB]).then_inc(stored, 16)
            sp.wait_ge(stored, 4 * 16)

        @block.gpsimd
        def _(pool):
            nc.gpsimd.memset(mhalf[:], -0.5).then_inc(const_set, 1)
            nc.gpsimd.memset(epsilon[:], EPS).then_inc(const_set, 1)
            pool.wait_ge(const_set, 2)
            pool.wait_ge(hi_done, RING)
            pool.dma_start(rot[:], dram["rot"]).then_inc(rot_in, 16)
            pool.dma_start(dmask[:], dram["dmask"]).then_inc(rot_in, 16)

            def row_scale(use):
                pool.wait_ge(row_sum, use + 1)
                nc.gpsimd.tensor_scalar(ms[:, use], ssq[:, use], 1.0 / DM, EPS, ALU.mult, ALU.add).then_inc(row_ms, 1)
                pool.wait_ge(row_ms, use + 1)
                nc.gpsimd.tensor_tensor(rstd[:, use], ms[:, use], mhalf[:, 0:NT], ALU.pow).then_inc(row_rstd, 1)

            row_scale(M_N1)
            with pool.Fori(0, R_N) as i:
                pool.wait_ge(bst_done, i * (2 * NT) + 2 * NT)
                nc.gpsimd.tensor_tensor(rvar[:], mv[:, :, 1], epsilon[:, 0:NT], ALU.add).then_inc(rrs_done, 1)
                pool.wait_ge(rrs_done, i * 2 + 1)
                nc.gpsimd.tensor_tensor(rrs[:], rvar[:], mhalf[:, 0:NT], ALU.pow).then_inc(rrs_done, 1)
            pool.wait_ge(row_sq[M_N2], 8)
            pool.dma_start(pM[:], dram["pm"][0]).then_inc(pm_in, 16)
            row_scale(M_N2)

            def bias(i):
                pool.wait_ge(mix_hi, i * 4 + 4)
                pool.dma_start(pB[:], dram["pool_b"][i].to_broadcast([P, GDIM])).then_inc(pb_in, 16)

            bias(0)
            with pool.Fori(1, P_N) as i:
                pool.wait_ge(pb_used, i)
                pool.dma_start(pM[:], dram["pm"][i]).then_inc(pm_in, 16)
                bias(i)
            pool.wait_ge(t_ps, (T_P + 8) * 2)
            pool.dma_start(row[:], dram["final_norm"].to_broadcast([P, DM])).then_inc(row_in, 16)
            row_scale(M_FN)
            pool.wait_ge(row_sum, M_N3 + 1)
            pool.wait_ge(row_rstd, M_FN + 1)
            nc.gpsimd.tensor_tensor(ms[:, M_N3], ssq[:, M_N3], rstd[:, M_FN], ALU.mult).then_inc(fn_t, 1)
            pool.wait_ge(fn_t, 1)
            nc.gpsimd.tensor_tensor(ms[:, M_N3], ms[:, M_N3], rstd[:, M_FN], ALU.mult).then_inc(fn_t, 1)
            pool.wait_ge(fn_t, 2)
            nc.gpsimd.tensor_scalar(ms[:, M_N3], ms[:, M_N3], 1.0 / DM, EPS, ALU.mult, ALU.add).then_inc(row_ms, 1)
            pool.wait_ge(row_ms, M_N3 + 1)
            nc.gpsimd.tensor_tensor(rstd[:, M_N3], ms[:, M_N3], mhalf[:, 0:NT], ALU.pow).then_inc(row_rstd, 1)
            pool.wait_ge(row_rstd, M_N3 + 1)
            nc.gpsimd.tensor_tensor(both[:], rstd[:, M_N3], rstd[:, M_FN], ALU.mult).then_inc(both_done, 1)

            pool.dma_start(wbr[:], dram["w_ba"]).then_inc(ba_in, 16)
            pool.dma_start(dtb[:], dram["dt_bias"].to_broadcast([P, DN_HEADS])).then_inc(ba_in, 16)
            pool.dma_start(alog[:], dram["a_log"].to_broadcast([P, DN_HEADS])).then_inc(ba_in, 16)
            pool.dma_start(wcv[:], dram["w_conv"]).then_inc(dn_in, 16)
            pool.dma_start(lmask[:], dram["lm"]).then_inc(dn_in, 16)

            def delta_pool(i, first):
                if first:
                    pool.wait_ge(gl_sb, 1)
                else:
                    pool.wait_ge(omean_sb, i * 2)
                nc.gpsimd.tensor_tensor(gm[:], upper[:, None, None, :].to_broadcast([P, NT, HG, P]), over(gl, i),
                                        ALU.mult).then_inc(gu_sb, 1)
                pool.wait_ge(sqn_sb, i * 2 + 1)
                nc.gpsimd.tensor_tensor(rqk[:, 0].rearrange("p t h -> p (t h)"),
                                        sqn[:, 0].rearrange("p t h -> p (t h)"), mhalf[:, 0:8],
                                        ALU.pow).then_inc(rqk_sb, 1)
                pool.wait_ge(dn_in, 32)
                pool.wait_ge(dt_sb, i + 1)
                nc.gpsimd.tensor_tensor(iT[:], dT[:], lmask[:, 0][:, None, None, :].to_broadcast([P, NT, HG, P]),
                                        ALU.mult).then_inc(gu_sb, 1)
                for lv in range(1, LEVELS):
                    if lv == 1:
                        pool.wait_ge(a_sb, i + 1)
                    elif lv == 2:
                        pool.wait_ge(u0_sb, i + 1)
                    else:
                        pool.wait_ge(m1_ps, i * (LEVELS - 1) + (lv - 2))
                    to = kbT if lv % 2 else kb
                    nc.gpsimd.tensor_tensor(to[:], aT[:], lmask[:, lv][:, None, None, :].to_broadcast([P, NT, HG, P]),
                                            ALU.mult).then_inc(lv_sb, 1)
                pool.wait_ge(sqn_sb, i * 2 + 2)
                nc.gpsimd.tensor_tensor(rqk[:, 1].rearrange("p t h -> p (t h)"),
                                        sqn[:, 1].rearrange("p t h -> p (t h)"), mhalf[:, 0:8],
                                        ALU.pow).then_inc(rqk_sb, 1)
                pool.wait_ge(omean_sb, i * 2 + 2)
                nc.gpsimd.tensor_tensor(oms[:, 2].rearrange("p t h -> p (t h)"),
                                        oms[:, 1].rearrange("p t h -> p (t h)"), mhalf[:, 0:8],
                                        ALU.pow).then_inc(ors_sb, 1)

            delta_pool(0, True)
            with pool.Fori(1, D_N) as i:
                delta_pool(i, False)
            pool.wait_ge(t_ps, (T_D + D_N) * 2)
            pool.dma_start(wdw[:], dram["w_long"]).then_inc(g_in, 16)
            nc.gpsimd.memset(up[:, :, 0:LONG - 1], 0.0).then_inc(const_set, 1)
            pool.dma_start(bg[:], dram["b_gate"][0].to_broadcast([P, NB])).then_inc(bg_in, 16)
            with pool.Fori(1, 2 * G_N) as i:
                pool.wait_ge(gate_add, i)
                pool.dma_start(bg[:], dram["b_gate"][i].to_broadcast([P, NB])).then_inc(bg_in, 16)
            pool.wait_ge(t_ps, (T_Y + Y_N) * 2)
            pool.dma_start(pT[:], dram["pT"]).then_inc(tail_in, 16)
            pool.dma_start(rpost[:], dram["g_post"].to_broadcast([P, DM])).then_inc(tail_in, 16)
            pool.dma_start(rple[:], dram["g_ple"].to_broadcast([P, DM])).then_inc(tail_in, 16)
            row_scale(M_POST)
            row_scale(M_PLE)

        @block.scalar
        def _(act):
            def split_hi(q, j):
                s = j % RING
                act.wait_ge(raw_in[s], q * 16 + 16 * (j // RING + 1))
                act.wait_ge(multiplied, q * RING + (j + 1))
                nc.scalar.copy(whi[:, s], raw[:, s]).then_inc(hi_done, 1)

            def t_split_hi(use, dst, kt, scale, bank=6):
                for c in range(QT):
                    act.wait_ge(t_ps, use * 2 + (c // 2 + 1))
                    to = dst[:, bass.ds(kt + c, 1), :].rearrange("p a n -> p (a n)")
                    if scale is None:
                        nc.scalar.copy(to, half(bank, c)).then_inc(t_hi, 1)
                    else:
                        nc.scalar.activation(to, half(bank, c), ACT.Copy,
                                             scale=cols[:, bass.ds(scale(c), 1)]).then_inc(t_hi, 1)

            def squares(use, b, src, to):
                for t in range(NT):
                    if b:
                        act.wait_ge(row_sq[use], NT * (b - 1) + t + 1)
                    nc.scalar.activation(to[:, t], src[:, t], ACT.Square,
                                         accum_out=part[:, use, t, b:b + 1]).then_inc(row_sq[use], 1)

            def quarter(v, b):
                return v[:, :, b * NB:(b + 1) * NB]

            def by_token(to, bank, func, use, sem_to):
                for t in range(NT):
                    ins = nc.scalar.activation(to[:, t], PS[:, bank + t], func, scale=rstd[:, use, t:t + 1])
                ins.then_inc(sem_to, 1)

            nc.scalar.preload_act_table(ACT.Silu)
            act.wait_ge(con_in, 32)

            def norm1(u):
                t_split_hi(T_N1 + u, aH, 4 * u, lambda c: C_RN + 4 * u + c, 6 - 2 * (u % 2))

            norm1(0)
            split_hi(0, 0)
            norm1(1)
            for j in range(1, RING):
                split_hi(0, j)

            def head_tail(i):
                t_split_hi(i + T_R, oH, i * QT, lambda c: i * QT + (C_GN + c))

            def head(i, first):
                q = i * (R_PER // RING) + R_AT // RING
                for j in range(R_PER):
                    split_hi(q, j + RING)
                    if first and j in (1, 3):
                        norm1((j + 3) // 2)
                    if first and j == 4:
                        for b in range(4):
                            squares(M_N1, b, quarter(H, b), XS[:, :, b * NB:(b + 1) * NB])
                    if not first and j == 1:
                        head_tail(i - 1)
                    if j == 11:
                        act.wait_ge(qkT_ps, i + 1)
                        nc.scalar.copy(qkT[:].rearrange("p a h n -> p (a h n)"),
                                       PS[:, 6:8].rearrange("p b n -> p (b n)")).then_inc(qkT_sb, 1)
                    if j == 15:
                        done(act, q, j)
                        act.wait_ge(row_rstd, M_N1 + 1)
                        by_token(vH, 2, ACT.Copy, M_N1, v_sb)
                    if j == 16:
                        act.wait_ge(sT_sb, i * 3 + 1)
                        nc.scalar.copy(sTH[:], sT).then_inc(v_sb, 1)
                done(act, q, R_PER - 1)
                by_token(zR, 4, ACT.Silu, M_N1, z_sb)

            head(0, True)
            with act.Fori(1, R_N) as i:
                head(i, False)

            for b in range(4):
                q = (RO_AT + b * K32) // RING
                for j in range(K32):
                    split_hi(q, j + RING)
                    if b == 0 and j == 1:
                        head_tail(R_N - 1)
                    if b and j == 2:
                        t_split_hi(T_N2 + b - 1, aH, 4 * (b - 1), lambda c: C_PN + 4 * (b - 1) + c)
                act.wait_ge(h_out, 2 + b + 1)
                squares(M_N2, b, quarter(H, b), junk[:, 0])

            def group(i, first):
                q = i * (P_PER // RING) + P_AT // RING
                for j in range(P_PER):
                    split_hi(q, j + RING)
                    if j == 1:
                        if first:
                            t_split_hi(T_N2 + 3, aH, 12, lambda c: C_PN + 12 + c)
                        else:
                            group_tail(i - 1, 1)
                    if j in (7, 15):
                        done(act, q, j)
                        b = j // 8
                        act.wait_ge(row_rstd, M_N2 + 1)
                        by_token(pUH[:, :, b * NB:(b + 1) * NB], 2 * b, ACT.Copy, M_N2, pu_sb)
                    if j == 16:
                        act.wait_ge(pm_in, i * 16 + 16)
                        nc.scalar.copy(pMH[:], pM[:]).then_inc(pu_sb, 1)
                    if j == 19:
                        for b in range(4):
                            act.wait_ge(mix_ps, i * 4 + (b + 1))
                            nc.scalar.copy(mH[:, 2 * b:2 * b + 2].rearrange("p a n -> p (a n)"),
                                           PS[:, 4 + b]).then_inc(mix_hi, 1)
                    if j in (23, 31):
                        done(act, q, j)
                        b = j // 8 - 2
                        by_token(pZ[:, :, b * NB:(b + 1) * NB], 2 * b, ACT.Silu, M_N2, pz_sb)
                    if j == 38:
                        group_tail(i, 0)

            def group_tail(i, w):
                t_split_hi(i * 2 + (T_P + w), oH, i * 8 + 4 * w, lambda c: i * 8 + (C_PS + 4 * w + c))

            group(0, True)
            with act.Fori(1, P_N) as i:
                group(i, False)
            for b in range(4):
                q = (PO_AT + b * K32) // RING
                for j in range(K32 - 1):
                    split_hi(q, j + RING)
                    if b == 0 and j == 1:
                        group_tail(P_N - 1, 1)
                if b < 3:
                    split_hi(q, K32 - 1 + RING)
                act.wait_ge(h_out, 2 + 4 + b + 1)
                squares(M_FN, b, quarter(H, b), junk[:, 0])
                act.wait_ge(fn_t2, b + 1)
                squares(M_N3, b, quarter(H if b < 3 else XS, b), junk[:, 1])
            split_hi(q, K32 - 1 + RING)

            def norm3(u):
                t_split_hi(T_N3 + u, aH, 4 * u, lambda c: C_PRE + 4 * u + c, 6 - 2 * (u % 2))

            norm3(0)
            norm3(1)

            def decays():
                act.wait_ge(ad_sb, 1)
                nc.scalar.activation(beta[:], PS[:, 4, 0:64].rearrange("p (t n) -> p t n", t=NT)[:, :, 0:DN_HEADS],
                                     ACT.Sigmoid).then_inc(beta_sb, 1)
                nc.scalar.activation(sp1[:], ad[:], ACT.Abs).then_inc(sp_a, 1)
                act.wait_ge(sp_a, 1)
                nc.scalar.activation(sp1[:], sp1[:], ACT.Exp, scale=-1.0).then_inc(sp_a, 1)
                act.wait_ge(sp_a, 2)
                nc.scalar.activation(sp1[:], sp1[:], ACT.Ln, bias=1.0).then_inc(sp_a, 1)

            act.sem_inc(kqv_sb, 1)
            act.sem_inc(zb_sb, 1)

            def copy_heads(to, bank, wait, after, value):
                act.wait_ge(wait, value)
                nc.scalar.copy(to[:].rearrange("p t h n -> p t (h n)"), PS[:, bank:bank + 2]).then_inc(after, 1)

            def delta_tail(i, j):
                if j == 1:
                    act.wait_ge(vn1_ps, i + 1)
                    nc.scalar.copy(vn[:, 1].rearrange("p h n -> p (h n)"), PS[:, 4]).then_inc(vn1_sb, 1)
                if j == 3:
                    act.wait_ge(oq_sb, i + 1)
                    nc.scalar.activation(gm[:].rearrange("p t h n -> p t (h n)"), oD, ACT.Square).then_inc(osq_sb, 1)
                if j == 6:
                    t_split_hi(i + T_D, oaH, i * QT, lambda c: C_DN)

            def delta(i, first):
                q = i * (D_PER // RING) + D_AT // RING
                for j in range(D_PER):
                    split_hi(q, j + RING)
                    if first and j in (1, 3):
                        norm3((j + 3) // 2)
                    if first and j == 5:
                        act.wait_ge(ba_in, 48)
                        nc.scalar.copy(wbh[:], wbr[:]).then_inc(small_hi, 1)
                        nc.scalar.activation(ea[:], alog[:], ACT.Exp).then_inc(ea_sb, 1)
                    if first and j == 7:
                        decays()
                    if first and j == 8:
                        act.wait_ge(cum_ps, 1)
                        nc.scalar.copy(cum[:].rearrange("p t h -> p (t h)"), PS[:, 5, 0:NT * DN_HEADS]).then_inc(cum_sb, 1)
                        act.wait_ge(cum_sb, 1)
                        nc.scalar.activation(ecum[:], cum[:], ACT.Exp).then_inc(ecum_sb, 1)
                    if not first:
                        delta_tail(i - 1, j)
                    if j == 11:
                        act.wait_ge(dt_sub, i * 2 + 2)
                        nc.scalar.activation(dT[:], dT[:], ACT.Exp).then_inc(dt_sb, 1)
                    if j in (9, 20, 27):
                        y = (j - 9) // 9
                        act.wait_ge(conv_tap, i * 48 + 16 * (y + 1))
                        nc.scalar.activation(kqv[:, y], yD[:], ACT.Silu).then_inc(kqv_sb, 1)
                        if y < 2:
                            act.wait_ge(kqv_sb, i * 3 + (y + 2))
                            to = kb[:].rearrange("p t h n -> p (t h n)") if y == 0 else zD[:].rearrange("p t n -> p (t n)")
                            nc.scalar.activation(to, kqv[:, y].rearrange("p h n -> p (h n)"),
                                                 ACT.Square).then_inc(sq_sb, 1)
                    if j == 13:
                        copy_heads(knT, 4, kt_ps, kt_sb, i + 1)
                        copy_heads(kbT, 6, kt_ps, kt_sb, i + 1)
                    if j == 16:
                        copy_heads(iT, 4, t0_ps, t0_sb, i + 1)
                    if 17 <= j <= 27 and j % 2:
                        lv = (j - 15) // 2
                        act.wait_ge(m1_ps, i * (LEVELS - 1) + lv)
                        if lv < LEVELS - 1:
                            nc.scalar.copy(all_blocks(flat(gm), lv, 0), all_blocks(PS[:, 4:6], lv, 0)).then_inc(m1_sb, 1)
                        else:
                            nc.scalar.copy(flat(gm), PS[:, 4:6]).then_inc(m1_sb, 1)
                        if lv > 1:
                            copy_heads(iU, 6, iu_ps, iu_sb, i * (LEVELS - 2) + (lv - 1))
                    if j == 30:
                        act.wait_ge(vn0_ps, i + 1)
                        nc.scalar.copy(vn[:, 0].rearrange("p h n -> p (h n)"), PS[:, 7]).then_inc(vn0_sb, 1)
                    if j == 31:
                        act.wait_ge(st_ps, i + 1)
                        nc.scalar.copy(st.rearrange("p h n -> p (h n)"), PS[:, 4]).then_inc(st_sb, 1)
                done(act, q, D_PER - 1)
                act.wait_ge(sq_ps, i * 2 + 2)
                nc.scalar.activation(zD[:], PS[:, 2:4], ACT.Silu).then_inc(zd_sb, 1)

            delta(0, True)
            with act.Fori(1, D_N) as i:
                delta(i, False)

            def gated(i, first):
                q = i * (G_PER // RING) + G_AT // RING
                for j in range(G_PER):
                    split_hi(q, j + RING)
                    if first:
                        delta_tail(D_N - 1, j)
                    if j == 15:
                        done(act, q, j)
                        nc.scalar.activation(sg[:], PS[:, 2:4], ACT.Sigmoid).then_inc(sgb_sb, 1)
                    if j == 23:
                        done(act, q, j)
                        nc.scalar.activation(zbT[:, bass.ds(i * QT, QT)].rearrange("p c n -> p (c n)"),
                                             PS[:, 4:6].rearrange("p b n -> p (b n)"), ACT.Silu).then_inc(zb_sb, 1)
                    if j == 31:
                        act.wait_ge(gate_add, i + 1)
                        nc.scalar.activation(sg[:], sg[:], ACT.Sigmoid).then_inc(ga_sb, 1)

            gated(0, True)
            with act.Fori(1, G_N) as i:
                gated(i, False)

            def gate_b(b):
                act.wait_ge(gate_add, b + (G_N + 1))
                to = (sg, sg1)[b % 2]
                nc.scalar.activation(to[:], to[:], ACT.Sigmoid).then_inc(gb_sb, 1)

            def branch_tail(b):
                t_split_hi(b + T_Y, oaH, b * QT, None, 2 * b)

            for j in range(8 * K16):
                split_hi(Y_AT // RING, j + RING)
                if j == LN_AT:
                    for u in range(4):
                        act.wait_ge(uc_sb, u + 1)
                        if u > 1:
                            act.wait_ge(usq_ps, u - 1)
                        nc.scalar.activation(ln_tmp[u % 2], uT[:, 4 * u:4 * u + 4].rearrange("p c n -> p (c n)"),
                                             ACT.Square).then_inc(usq_sb, 1)
                if j == LN_AT + 4:
                    act.wait_ge(mean_sb, 2)
                    nc.scalar.activation(rln[:], rln[:], ACT.Sqrt).then_inc(std_sb, 1)
                if LN_AT + 6 <= j < LN_AT + 14 and j % 2 == 0:
                    u = (j - LN_AT) // 2 - 3
                    act.wait_ge(un_sb, u + 1)
                    for c in range(QT):
                        k = 4 * u + c
                        nc.scalar.activation(uT[:, k], uT[:, k], ACT.Silu, scale=cols[:, C_LNG + k:C_LNG + k + 1],
                                             bias=cols[:, C_LNB + k:C_LNB + k + 1]).then_inc(us_sb, 1)
                if LN_AT + 6 <= j < LN_AT + 14 and j % 2:
                    u = (j - LN_AT) // 2 - 3
                    act.wait_ge(ub_sb, u + 1)
                    nc.scalar.copy(ubH[:, 4 * u:4 * u + 4].rearrange("p c n -> p (c n)"), ln_tmp[u % 2]).then_inc(ub_hi, 1)
                if j in (LN_AT + 14, LN_AT + 15):
                    gate_b(j - LN_AT - 14)
                if j in (5 * K16 + 1, 6 * K16 + 1):
                    gate_b(j // K16 - 3)
                if j in (5 * K16 + 2, 6 * K16 + 2, 7 * K16 + 2):
                    branch_tail(j // K16 - 5)

            for b in range(4):
                q = (O_AT + b * K16) // RING
                for j in range(K16):
                    split_hi(q, j + RING)
                    if b == 0 and j == 2:
                        branch_tail(Y_N - 1)
                done(act, q, K16 - 1)
                nc.scalar.copy(quarter(mo, b), PS[:, 2 * (b % 2):2 * (b % 2) + 2]).then_inc(mo_sb, 1)
                squares(M_POST, b, PS[:, 2 * (b % 2):2 * (b % 2) + 2], junk2[:, 0])
                if b == 1:
                    act.wait_ge(tail_in, 48)
                    nc.scalar.copy(pTh[:], pT[:]).then_inc(small_hi, 1)

            def norm_x3(u):
                t_split_hi(T_X3 + u, aH, 4 * u, None, 6 - 2 * (u % 2))

            for j in range(E_PER):
                split_hi(E_AT // RING, j + RING)
                if j > 1:
                    norm_x3(j - 2)
                done(act, E_AT // RING, j)
                nc.scalar.copy(eb[:, :, j * NB:(j + 1) * NB], PS[:, 2 * (j % 2):2 * (j % 2) + 2]).then_inc(eb_sb, 1)

            for b in range(4):
                q = (PG_AT + b * K16) // RING
                for j in range(K16):
                    if b < 3 or j < K16 - RING:
                        split_hi(q, j + RING)
                    if b == 0 and j in (1, 3):
                        norm_x3((j + 3) // 2)
                done(act, q, K16 - 1)
                if b:
                    act.wait_ge(es_sb, b)
                nc.scalar.activation(sgp[:], PS[:, 2 * (b % 2):2 * (b % 2) + 2], ACT.Sigmoid).then_inc(sp_sb, 1)
                act.wait_ge(es_sb, b + 1)
                squares(M_PLE, b, quarter(eb, b), junk2[:, 1])

        @block.vector
        def _(dve):
            def split_lo(q, j):
                s = j % RING
                dve.wait_ge(hi_done, q * RING + (j + 1))
                nc.vector.tensor_tensor(wlo[:, s], raw[:, s], whi[:, s].bitcast(F32), ALU.subtract).then_inc(lo_done, 1)

            def t_split_lo(use, hi, lo, kt, scale, bank=6):
                for c in range(QT):
                    dve.wait_ge(t_hi, use * QT + (c // 2 * 2 + 2))
                    h = hi[:, bass.ds(kt + c, 1), :].rearrange("p a n -> p (a n)").bitcast(F32)
                    to = lo[:, bass.ds(kt + c, 1), :].rearrange("p a n -> p (a n)")
                    if scale is None:
                        nc.vector.tensor_tensor(to, half(bank, c), h, ALU.subtract).then_inc(t_lo, 1)
                    else:
                        nc.vector.scalar_tensor_tensor(out=to, in0=half(bank, c), scalar=cols[:, bass.ds(scale(c), 1)],
                                                       in1=h, op0=ALU.mult, op1=ALU.subtract).then_inc(t_lo, 1)

            def row_total(use):
                dve.wait_ge(row_sq[use], 8)
                nc.vector.tensor_reduce(ssq[:, use], part[:, use], AX.X, ALU.add).then_inc(row_sum, 1)

            def quarter(v, b):
                return v[:, :, b * NB:(b + 1) * NB]

            dve.sem_inc(lo_done, RING)
            dve.sem_inc(h_out, 2)
            dve.wait_ge(con_in, 32)

            def norm1(u):
                t_split_lo(T_N1 + u, aH, aL, 4 * u, lambda c: C_RN + 4 * u + c, 6 - 2 * (u % 2))

            norm1(0)
            split_lo(0, 0)
            norm1(1)
            for j in range(1, RING):
                split_lo(0, j)

            def head_tail(i):
                t_split_lo(i + T_R, oH, oL, i * QT, lambda c: i * QT + (C_GN + c))

            def rope(i):
                x = PS[:, 0:2].rearrange("p t (a h n) -> p t a h n", a=2, h=2)
                cos, sin = (rot[:, n][:, :, None, :].to_broadcast([P, NT, 2, HALF]) for n in range(2))
                steps = ((0, cos, 1, sin, ALU.subtract), (0, sin, 1, cos, ALU.add))
                for n, (ha, fa, hb, fb, op) in enumerate(steps):
                    if n:
                        dve.wait_ge(rope_done, i * 2 + 1)
                    nc.vector.tensor_tensor(rt[:, 0], x[:, :, :, ha], fa, ALU.mult).then_inc(rope_t, 1)
                    nc.vector.tensor_tensor(rt[:, 1], x[:, :, :, hb], fb, ALU.mult).then_inc(rope_t, 1)
                    dve.wait_ge(rope_t, i * 4 + 2 * (n + 1))
                    nc.vector.tensor_tensor(roped[:, :, :, n], rt[:, 0], rt[:, 1], op).then_inc(rope_done, 1)

            def head(i, first):
                q = i * (R_PER // RING) + R_AT // RING
                for j in range(R_PER):
                    split_lo(q, j + RING)
                    if first and j in (1, 3):
                        norm1((j + 3) // 2)
                    if first and j == 5:
                        row_total(M_N1)
                    if first and j == 6:
                        dve.wait_ge(row_rstd, M_N1 + 1)
                        dve.wait_ge(rot_in, 32)
                        for t in range(NT):
                            ins = nc.vector.tensor_scalar(rot[:, :, t], rot[:, :, t], rstd[:, M_N1, t:t + 1], None, ALU.mult)
                        ins.then_inc(rot_scaled, 1)
                    if not first and j == 1:
                        head_tail(i - 1)
                    if j == 7:
                        dve.wait_ge(rot_scaled, 1)
                        done(dve, q, j)
                        rope(i)
                    if j == 15:
                        dve.wait_ge(sT_ps, i + 1)
                        nc.vector.tensor_tensor(sT, PS[:, 6, 0:3 * P],
                                                dmask[:, bass.ds(i, 1)].rearrange("p a n -> p (a n)"),
                                                ALU.mult).then_inc(sT_sb, 1)
                        dve.wait_ge(v_sb, i * 2 + 1)
                        for t in range(NT):
                            ins = nc.vector.scalar_tensor_tensor(out=vL[:, t], in0=PS[:, 2 + t],
                                                                 scalar=rstd[:, M_N1, t:t + 1],
                                                                 in1=vH[:, t].bitcast(F32), op0=ALU.mult,
                                                                 op1=ALU.subtract)
                        ins.then_inc(sT_sb, 1)
                    if j == 16:
                        dve.wait_ge(v_sb, i * 2 + 2)
                        nc.vector.tensor_tensor(sTL[:], sT, sTH[:].bitcast(F32), ALU.subtract).then_inc(sT_sb, 1)
                    if j == 19:
                        dve.wait_ge(o_ps, i + 1)
                        for t in range(NT):
                            nc.vector.bn_stats(bst[:, t], PS[:, 6 + t]).then_inc(bst_done, 1)
                        dve.wait_ge(bst_done, i * (2 * NT) + NT)
                        nc.vector.memset(carrier[:], 0.0)
                        for t in range(NT):
                            nc.vector.bn_aggr(mv[:, t], bst[:, t]).then_inc(bst_done, 1)
                    if j == 20:
                        dve.wait_ge(rrs_done, i * 2 + 2)
                        dve.wait_ge(bst_done, i * (2 * NT) + 2 * NT)
                        for t in range(NT):
                            nc.vector.tensor_scalar(oR[:, t], PS[:, 6 + t], mv[:, t, 0:1], rrs[:, t:t + 1],
                                                    ALU.subtract, ALU.mult).then_inc(on_sb, 1)
                dve.wait_ge(z_sb, i + 1)
                dve.wait_ge(on_sb, i * NT + NT)
                nc.vector.tensor_tensor(oR[:], oR[:], zR[:], ALU.mult).then_inc(oz_sb, 1)

            head(0, True)
            with dve.Fori(1, R_N) as i:
                head(i, False)

            for b in range(4):
                q = (RO_AT + b * K32) // RING
                for j in range(K32):
                    split_lo(q, j + RING)
                    if b == 0 and j == 1:
                        head_tail(R_N - 1)
                    if b and j == 2:
                        t_split_lo(T_N2 + b - 1, aH, aL, 4 * (b - 1), lambda c: C_PN + 4 * (b - 1) + c)
                done(dve, q, K32 - 1)
                nc.vector.tensor_tensor(quarter(H, b), PS[:, 2 * (b % 2):2 * (b % 2) + 2], quarter(H, b),
                                        ALU.add).then_inc(h_out, 1)
            row_total(M_N2)

            def group_tail(i, w):
                t_split_lo(i * 2 + (T_P + w), oH, oL, i * 8 + 4 * w, lambda c: i * 8 + (C_PS + 4 * w + c))

            def group(i, first):
                q = i * (P_PER // RING) + P_AT // RING
                for j in range(P_PER):
                    split_lo(q, j + RING)
                    if j == 1:
                        if first:
                            t_split_lo(T_N2 + 3, aH, aL, 12, lambda c: C_PN + 12 + c)
                        else:
                            group_tail(i - 1, 1)
                    if j in (7, 15):
                        b = j // 8
                        dve.wait_ge(pu_sb, i * 3 + (b + 1))
                        for t in range(NT):
                            cut = pUH[:, t, b * NB:(b + 1) * NB].bitcast(F32)
                            ins = nc.vector.scalar_tensor_tensor(out=pUL[:, t, b * NB:(b + 1) * NB], in0=PS[:, 2 * b + t],
                                                                 scalar=rstd[:, M_N2, t:t + 1], in1=cut, op0=ALU.mult,
                                                                 op1=ALU.subtract)
                        ins.then_inc(pu_lo, 1)
                    if j == 19:
                        for b in range(4):
                            dve.wait_ge(mix_hi, i * 4 + (b + 1))
                            nc.vector.tensor_tensor(mL[:, 2 * b:2 * b + 2].rearrange("p a n -> p (a n)"), PS[:, 4 + b],
                                                    mH[:, 2 * b:2 * b + 2].rearrange("p a n -> p (a n)").bitcast(F32),
                                                    ALU.subtract).then_inc(mix_lo, 1)
                    if j in (35, 39):
                        w = (j - 35) // 4
                        done(dve, q, j)
                        if w == 0:
                            dve.wait_ge(pb_in, i * 16 + 16)
                        dve.wait_ge(t_ps, i * 4 + (T_P + w) * 2)
                        for t in range(NT):
                            ins = nc.vector.scalar_tensor_tensor(out=mz[:, t], in0=PS[:, 2 * w + t],
                                                                 scalar=cols[:, bass.ds(i * NT + (C_WIN + t), 1)],
                                                                 in1=pB[:, w * NB:(w + 1) * NB], op0=ALU.mult,
                                                                 op1=ALU.add)
                        ins.then_inc(mz_add, 1)
                        dve.wait_ge(pz_sb, i * 2 + (w + 1))
                        dve.wait_ge(mz_add, i * 2 + (w + 1))
                        nc.vector.tensor_tensor(mz[:], mz[:], pZ[:, :, w * NB:(w + 1) * NB], ALU.mult).then_inc(mz_sb, 1)
                    if j == 38:
                        group_tail(i, 0)
                dve.sem_inc(pb_used, 1)

            group(0, True)
            with dve.Fori(1, P_N) as i:
                group(i, False)
            for b in range(4):
                q = (PO_AT + b * K32) // RING
                for j in range(K32 - 1):
                    split_lo(q, j + RING)
                    if b == 0 and j == 1:
                        group_tail(P_N - 1, 1)
                if b < 3:
                    split_lo(q, K32 - 1 + RING)
                done(dve, q, K32 - 1)
                nc.vector.tensor_tensor(quarter(H, b), PS[:, 2 * (b % 2):2 * (b % 2) + 2], quarter(H, b),
                                        ALU.add).then_inc(h_out, 1)
                dve.wait_ge(row_in, 16)
                if b < 3:
                    dve.wait_ge(row_sq[M_FN], NT * (b + 1))
                else:
                    dve.wait_ge(h_out, 2 + 4 + 4)
                nc.vector.tensor_tensor(quarter(H if b < 3 else XS, b), quarter(H, b),
                                        row[:, b * NB:(b + 1) * NB][:, None, :].to_broadcast([P, NT, NB]),
                                        ALU.mult).then_inc(fn_t2, 1)
            row_total(M_FN)
            row_total(M_N3)
            dve.wait_ge(fn_t2, 4)
            nc.vector.tensor_copy(quarter(H, 3), quarter(XS, 3)).then_inc(fn_t2, 1)
            split_lo(q, K32 - 1 + RING)
            dve.wait_ge(both_done, 1)

            def scaled(u):
                for t in range(NT):
                    nc.vector.tensor_scalar(XS[:, t, u * NB:(u + 1) * NB], H[:, t, u * NB:(u + 1) * NB], both[:, t:t + 1],
                                            None, ALU.mult).then_inc(rows_sb, 1)

            def norm3(u):
                t_split_lo(T_N3 + u, aH, aL, 4 * u, lambda c: C_PRE + 4 * u + c, 6 - 2 * (u % 2))

            scaled(0)
            scaled(1)
            norm3(0)
            scaled(2)
            norm3(1)
            dve.wait_ge(fn_t2, 5)
            scaled(3)

            def add_bias(bank, to, n):
                dve.wait_ge(bg_in, n * 16 + 16)
                nc.vector.tensor_tensor(to[:], PS[:, bank:bank + 2], bg[:, None, :].to_broadcast([P, NT, NB]),
                                        ALU.add).then_inc(gate_add, 1)

            def decays():
                dve.wait_ge(ba_ps, 1)
                nc.vector.tensor_tensor(ad[:], PS[:, 4, 0:64].rearrange("p (t n) -> p t n", t=NT)[:, :, DN_HEADS:],
                                        dtb[:, None, :].to_broadcast([P, NT, DN_HEADS]), ALU.add).then_inc(ad_sb, 1)
                dve.wait_ge(ad_sb, 1)
                dve.wait_ge(sp_a, 3)
                nc.vector.scalar_tensor_tensor(out=sp2[:], in0=ad[:], scalar=0.0, in1=sp1[:], op0=ALU.max,
                                               op1=ALU.add).then_inc(ad_sb, 1)
                dve.wait_ge(ea_sb, 1)
                dve.wait_ge(ad_sb, 2)
                nc.vector.scalar_tensor_tensor(out=gl[:], in0=sp2[:], scalar=-1.0,
                                               in1=ea[:, None, :].to_broadcast([P, NT, DN_HEADS]), op0=ALU.mult,
                                               op1=ALU.mult).then_inc(gl_sb, 1)

            o = oD.rearrange("p t (h n) -> p t h n", h=HG)

            def delta_tail(i, j):
                def second(v):
                    return v[:, 1, bass.ds(i * HG, HG)][:, :, None].to_broadcast([P, HG, P])

                if j == 0:
                    dve.wait_ge(r1_ps, i + 1)
                    nc.vector.tensor_tensor(ke[:], heads(4)[:, 1], second(becum), ALU.mult).then_inc(r1_sb, 1)
                    dve.wait_ge(r1_sb, i + 1)
                    nc.vector.tensor_tensor(vb[:, 1], vb[:, 1], ke[:], ALU.subtract).then_inc(vb1_sb, 1)
                    nc.vector.tensor_tensor(o[:, 1], heads(6)[:, 0], second(ecum), ALU.mult).then_inc(o1_sb, 1)
                    nc.vector.tensor_copy(o[:, 0], heads(6)[:, 1]).then_inc(o1_sb, 1)
                if j == 2:
                    dve.wait_ge(o1_ps, i + 1)
                    dve.wait_ge(o1_sb, i * 2 + 2)
                    nc.vector.tensor_tensor(o[:, 1], heads(4)[:, 1], o[:, 1], ALU.add).then_inc(o1s_sb, 1)
                    dve.wait_ge(o1s_sb, i + 1)
                    dve.wait_ge(rqk_sb, i * 2 + 2)
                    nc.vector.tensor_tensor(o, o, rqk[:, 1][:, :, :, None].to_broadcast([P, NT, HG, P]),
                                            ALU.mult).then_inc(oq_sb, 1)
                if j == 3:
                    dve.wait_ge(osq_sb, i + 1)
                    nc.vector.tensor_reduce(oms[:, 0], gm[:], AX.X, ALU.add).then_inc(omean_sb, 1)
                    dve.wait_ge(omean_sb, i * 2 + 1)
                    nc.vector.tensor_scalar(oms[:, 1], oms[:, 0], 1.0 / P, EPS, ALU.mult, ALU.add).then_inc(omean_sb, 1)
                if j == 4:
                    dve.wait_ge(ors_sb, i + 1)
                    nc.vector.tensor_tensor(o, o, oms[:, 2][:, :, :, None].to_broadcast([P, NT, HG, P]),
                                            ALU.mult).then_inc(onr_sb, 1)
                    dve.wait_ge(onr_sb, i + 1)
                    dve.wait_ge(zd_sb, i + 1)
                    nc.vector.tensor_tensor(oD, oD, zD[:], ALU.mult).then_inc(od_sb, 1)
                if j == 6:
                    t_split_lo(i + T_D, oaH, oaL, i * QT, lambda c: C_DN)

            def conv(i, y, taps=range(TAPS)):
                at = (1, 0, 2)[y] * 16 * TAPS
                for k in taps:
                    for c in range(HG):
                        src = half(2 * (y % 2), c)
                        w = wcv[:, bass.ds(i * (HG * TAPS) + (at + c * TAPS + TAPS - 1 - k), 1)]
                        if k == 0:
                            if c == 0:
                                dve.wait_ge(kqv_sb, i * 3 + (y + 1))
                                if y == 0:
                                    dve.wait_ge(t_ps, i * 2 + T_D * 2)
                            nc.vector.tensor_scalar(yD[:, c], src, w, None, ALU.mult).then_inc(conv_tap, 1)
                        else:
                            dve.wait_ge(conv_tap, i * 48 + (16 * y + HG * (k - 1) + c + 1))
                            nc.vector.scalar_tensor_tensor(out=yD[:, c, k:], in0=src[:, 0:SEQ - k], scalar=w,
                                                           in1=yD[:, c, k:], op0=ALU.mult,
                                                           op1=ALU.add).then_inc(conv_tap, 1)

            def norms(i, n, bank):
                dve.wait_ge(sq_ps, i * 2 + (n + 1))
                nc.vector.tensor_scalar(sqn[:, n].rearrange("p t h -> p (t h)"), PS[:, bank, 0:8], EPS,
                                        (1.0, float(P))[n], ALU.add, ALU.mult).then_inc(sqn_sb, 1)

            def log_decays(i):
                dve.wait_ge(gu_ps, i + 1)
                nc.vector.tensor_tensor(dT[:], heads(4), over(cum, i), ALU.subtract).then_inc(dt_sub, 1)
                dve.wait_ge(dt_sub, i * 2 + 1)
                nc.vector.tensor_tensor(dT[:], dT[:], maskneg[:, None, None, :].to_broadcast([P, NT, HG, P]),
                                        ALU.min).then_inc(dt_sub, 1)

            def delta(i, first):
                q = i * (D_PER // RING) + D_AT // RING
                for j in range(D_PER):
                    split_lo(q, j + RING)
                    if first and j in (1, 3):
                        norm3((j + 3) // 2)
                    if first and j == 4:
                        for t in range(NT):
                            nc.vector.tensor_scalar(H[:, t], H[:, t], rstd[:, M_FN, t:t + 1], None,
                                                    ALU.mult)
                    if first and j == 5:
                        dve.wait_ge(small_hi, 1)
                        nc.vector.tensor_tensor(wbl[:], wbr[:], wbh[:].bitcast(F32), ALU.subtract).then_inc(small_lo, 1)
                    if not first:
                        delta_tail(i - 1, j)
                    if first and j == 7:
                        decays()
                        dve.wait_ge(dn_in, 32)
                    if j == 7:
                        done(dve, q, j)
                        conv(i, 0)
                        if not first:
                            log_decays(i)
                    if j in (15, 23):
                        done(dve, q, j)
                    if first and j == 9:
                        dve.wait_ge(ecum_sb, 1)
                        dve.wait_ge(beta_sb, 1)
                        nc.vector.tensor_tensor(becum[:], ecum[:], beta[:], ALU.mult)
                    if j == 9 and first:
                        log_decays(i)
                    if j == 11:
                        norms(i, 0, 4)
                    if j == 11:
                        dve.wait_ge(k_ps, i + 1)
                        dve.wait_ge(rqk_sb, i * 2 + 1)
                        nc.vector.tensor_tensor(kn[:], heads(6), rqk[:, 0][:, :, :, None].to_broadcast([P, NT, HG, P]),
                                                ALU.mult).then_inc(kn_sb, 1)
                        dve.wait_ge(kn_sb, i + 1)
                        nc.vector.tensor_tensor(kb[:], kn[:], over(beta, i), ALU.mult).then_inc(kb_sb, 1)
                    if j == 14:
                        dve.wait_ge(gu_sb, i * 2 + 2)
                        dve.wait_ge(a_ps, i + 1)
                        nc.vector.tensor_tensor(kb[:], heads(4), iT[:], ALU.mult).then_inc(b0_sb, 1)
                        dve.wait_ge(b0_sb, i + 1)
                        nc.vector.tensor_tensor(iU[:], ident[:, None, None, :].to_broadcast([P, NT, HG, P]), kb[:],
                                                ALU.subtract).then_inc(u0_sb, 1)
                        nc.vector.tensor_tensor(aT[:], heads(4), dT[:], ALU.mult).then_inc(a_sb, 1)
                    if 18 <= j <= 28 and j % 2 == 0:
                        lv = (j - 16) // 2
                        dve.wait_ge(tu_ps, i * (LEVELS - 1) + lv)
                        if lv == 1:
                            dve.wait_ge(t0_sb, i + 1)
                        else:
                            dve.wait_ge(tu_sb, i * (LEVELS - 1) + (lv - 1))
                        if lv < LEVELS - 1:
                            nc.vector.tensor_tensor(all_blocks(flat(iT), lv, 0), all_blocks(flat(iT), lv, 0),
                                                    all_blocks(PS[:, 4:6], lv, 0), ALU.subtract).then_inc(tu_sb, 1)
                        else:
                            nc.vector.tensor_tensor(all_blocks(flat(iU), lv, 1), all_blocks(flat(iU), lv, 1),
                                                    all_blocks(PS[:, 6:8], lv, 1), ALU.subtract).then_inc(tu_sb, 1)
                    if 15 <= j <= 18:
                        conv(i, 1, [j - 15])
                    if 23 <= j <= 26:
                        conv(i, 2, [j - 23])
                    if j == 28:
                        dve.wait_ge(v_ps, i + 1)
                        nc.vector.tensor_tensor(vb[:], heads(4), over(beta, i), ALU.mult).then_inc(vb_sb, 1)
                        nc.vector.tensor_tensor(ke[:], kn[:, 0], dT[:, 0, :, P - 1:P].to_broadcast([P, HG, P]),
                                                ALU.mult).then_inc(ke_sb, 1)
                    if j == 29:
                        dve.wait_ge(qk_ps, i + 1)
                        nc.vector.tensor_tensor(qk[:], heads(6), dT[:], ALU.mult).then_inc(qk_sb, 1)
                    if j == 30:
                        norms(i, 1, 6)

            delta(0, True)
            with dve.Fori(1, D_N) as i:
                delta(i, False)

            dve.sem_inc(g_read, 3)

            def tap(i, k):
                for c in range(QT):
                    w = wl[:, c * LONG + k:c * LONG + k + 1]
                    if k == 0:
                        nc.vector.tensor_scalar(yl[:, c], up[:, c, 0:SEQ], w,
                                                cols[:, bass.ds(i * QT + (C_BDW + c), 1)], ALU.mult,
                                                ALU.add).then_inc(long_tap[c], 1)
                        continue
                    dve.wait_ge(long_tap[c], i * LONG + k)
                    to = yl[:, c] if k < LONG - 1 else uT[:, bass.ds(i * QT + c, 1)].rearrange("p a n -> p (a n)")
                    nc.vector.scalar_tensor_tensor(out=to, in0=up[:, c, k:k + SEQ], scalar=w, in1=yl[:, c],
                                                   op0=ALU.mult, op1=ALU.add).then_inc(long_tap[c], 1)

            OWN = 20

            def gated(i, first):
                q = i * (G_PER // RING) + G_AT // RING
                k = OWN
                for j in range(2 * K16):
                    split_lo(q, j + RING)
                    if first:
                        delta_tail(D_N - 1, j)
                    while not first and k < LONG and (k - OWN) * 14 < (j + 1) * (LONG - OWN):
                        tap(i - 1, k)
                        k += 1
                done(dve, q, 2 * K16 - 1)
                dve.wait_ge(sgb_sb, i + 1)
                if not first:
                    dve.wait_ge(long_tap[QT - 1], i * LONG)
                nc.vector.tensor_tensor(up[:, :, LONG - 1:], PS[:, 0:2].rearrange("p b (c n) -> p (b c) n", c=2),
                                        sg[:].rearrange("p t (x n) -> p (t x) n", x=2), ALU.mult).then_inc(g_read, 1)
                dve.wait_ge(g_in, 16)
                nc.vector.tensor_copy(wl[:], wdw[:, bass.ds(i * (QT * LONG), QT * LONG)]).then_inc(wl_set, 1)
                dve.wait_ge(g_read, i * 3 + 4)
                dve.wait_ge(const_set, 3)
                dve.wait_ge(wl_set, i + 1)
                k = 0
                for j in range(2 * K16, G_PER):
                    split_lo(q, j + RING)
                    if j == 31:
                        done(dve, q, j)
                        add_bias(0, sg, i)
                        dve.sem_inc(g_read, 1)
                    while k < OWN and k * (G_PER - 2 * K16) < (j - 2 * K16 + 1) * OWN:
                        tap(i, k)
                        k += 1
                done(dve, q, G_PER - 1)
                dve.wait_ge(ga_sb, i + 1)
                nc.vector.tensor_tensor(mx[:, :, bass.ds(i * NB, NB)], PS[:, 2:4], sg[:], ALU.mult).then_inc(g_read, 1)

            gated(0, True)
            with dve.Fori(1, G_N) as i:
                gated(i, False)

            def join(b, bank, gate):
                dve.wait_ge(gb_sb, b + 1)
                dve.wait_ge(t_ps, b * 2 + T_Y * 2)
                nc.vector.tensor_tensor(yl2, PS[:, bank:bank + 2], gate[:], ALU.mult).then_inc(yt_sb, 1)
                dve.wait_ge(yt_sb, b + 1)
                nc.vector.tensor_tensor(yl2, yl2, mx[:, :, bass.ds(b * NB, NB)], ALU.add).then_inc(ym_sb, 1)

            def branch_tail(b):
                t_split_lo(b + T_Y, oaH, oaL, b * QT, None, 2 * b)

            k = OWN
            for j in range(8 * K16):
                split_lo(Y_AT // RING, j + RING)
                while k < LONG and (k - OWN) * (LN_AT - 1) < (j + 1) * (LONG - OWN):
                    tap(G_N - 1, k)
                    k += 1
                if j == LN_AT:
                    dve.wait_ge(mean_ps, 1)
                    nc.vector.tensor_scalar(mean[:], PS[:, 6, 0:SEQ], 1.0 / DM, None, ALU.mult).then_inc(mean_sb, 1)
                    dve.wait_ge(mean_sb, 1)
                    for u in range(4):
                        nc.vector.tensor_tensor(uT[:, 4 * u:4 * u + 4], uT[:, 4 * u:4 * u + 4],
                                                mean[:, None, :].to_broadcast([P, 4, SEQ]), ALU.subtract).then_inc(uc_sb, 1)
                if j == LN_AT + 3:
                    dve.wait_ge(usq_ps, 4)
                    nc.vector.tensor_scalar(rln[:], PS[:, 7, 0:SEQ], 1.0 / DM, EPS, ALU.mult, ALU.add).then_inc(mean_sb, 1)
                if j == LN_AT + 5:
                    dve.wait_ge(std_sb, 1)
                    nc.vector.reciprocal(rln[:], rln[:]).then_inc(mean_sb, 1)
                    dve.wait_ge(mean_sb, 3)
                    dve.wait_ge(uc_sb, 4)
                if LN_AT + 5 <= j <= LN_AT + 7:
                    for u in ((0, 1), (2,), (3,))[j - LN_AT - 5]:
                        nc.vector.tensor_tensor(uT[:, 4 * u:4 * u + 4], uT[:, 4 * u:4 * u + 4],
                                                rln[:, None, :].to_broadcast([P, 4, SEQ]), ALU.mult).then_inc(un_sb, 1)
                if LN_AT + 6 <= j < LN_AT + 14 and j % 2 == 0:
                    u = (j - LN_AT) // 2 - 3
                    dve.wait_ge(us_sb, 4 * u + 4)
                    if u > 1:
                        dve.wait_ge(ub_hi, u - 1)
                        dve.wait_ge(ub_lo, u - 1)
                    nc.vector.tensor_tensor(ln_tmp[u % 2], uT[:, 4 * u:4 * u + 4].rearrange("p c n -> p (c n)"),
                                            zbT[:, 4 * u:4 * u + 4].rearrange("p c n -> p (c n)"),
                                            ALU.mult).then_inc(ub_sb, 1)
                if LN_AT + 6 <= j < LN_AT + 14 and j % 2:
                    u = (j - LN_AT) // 2 - 3
                    dve.wait_ge(ub_hi, u + 1)
                    nc.vector.tensor_tensor(ubL[:, 4 * u:4 * u + 4].rearrange("p c n -> p (c n)"), ln_tmp[u % 2],
                                            ubH[:, 4 * u:4 * u + 4].rearrange("p c n -> p (c n)").bitcast(F32),
                                            ALU.subtract).then_inc(ub_lo, 1)
                if j in (LN_AT + 1, LN_AT + 2):
                    b = j - LN_AT - 1
                    done(dve, Y_AT // RING, b * K16 + K16 - 1)
                    add_bias(2 * b, (sg, sg1)[b], G_N + b)
                if j > 4 * K16 and j % K16 == 0:
                    b = j // K16 - 5
                    done(dve, Y_AT // RING, j - 1)
                    join(b, 2 * b, (sg, sg1)[b % 2])
                    if b < 2:
                        add_bias(2 * b + 4, (sg, sg1)[b], G_N + 2 + b)
                if j in (5 * K16 + 2, 6 * K16 + 2, 7 * K16 + 2):
                    branch_tail(j // K16 - 5)
            done(dve, Y_AT // RING, 8 * K16 - 1)
            join(3, 6, sg1)

            for b in range(4):
                q = (O_AT + b * K16) // RING
                for j in range(K16):
                    split_lo(q, j + RING)
                    if b == 0 and j == 2:
                        branch_tail(Y_N - 1)
                dve.wait_ge(mo_sb, b + 1)
                dve.wait_ge(tail_in, 48)
                nc.vector.tensor_tensor(quarter(mo, b), quarter(mo, b),
                                        rpost[:, b * NB:(b + 1) * NB][:, None, :].to_broadcast([P, NT, NB]),
                                        ALU.mult).then_inc(mp_sb, 1)
                if b == 1:
                    dve.wait_ge(small_hi, 2)
                    nc.vector.tensor_tensor(pTl[:], pT[:], pTh[:].bitcast(F32), ALU.subtract).then_inc(small_lo, 1)
            row_total(M_POST)

            def x3(u):
                for t in range(NT):
                    nc.vector.scalar_tensor_tensor(out=quarter(H, u)[:, t], in0=quarter(mo, u)[:, t],
                                                   scalar=rstd[:, M_POST, t:t + 1], in1=quarter(H, u)[:, t],
                                                   op0=ALU.mult, op1=ALU.add).then_inc(rows_sb, 1)

            def norm_x3(u):
                t_split_lo(T_X3 + u, aH, aL, 4 * u, None, 6 - 2 * (u % 2))

            for j in range(E_PER):
                split_lo(E_AT // RING, j + RING)
                if j == 0:
                    dve.wait_ge(mp_sb, 4)
                    dve.wait_ge(row_rstd, M_POST + 1)
                x3(j)
                if j > 1:
                    norm_x3(j - 2)
            for b in range(4):
                q = (PG_AT + b * K16) // RING
                for j in range(K16):
                    if b < 3 or j < K16 - RING:
                        split_lo(q, j + RING)
                    if b == 0 and j in (1, 3):
                        norm_x3((j + 3) // 2)
                dve.wait_ge(sp_sb, b + 1)
                dve.wait_ge(eb_sb, 4)
                nc.vector.tensor_tensor(quarter(eb, b), quarter(eb, b), sgp[:], ALU.mult).then_inc(es_sb, 1)
                if b < 3:
                    dve.wait_ge(row_sq[M_PLE], NT * (b + 1))
                    nc.vector.tensor_tensor(quarter(eb, b), quarter(eb, b),
                                            rple[:, b * NB:(b + 1) * NB][:, None, :].to_broadcast([P, NT, NB]),
                                            ALU.mult).then_inc(ep_sb, 1)
            row_total(M_PLE)
            nc.vector.tensor_tensor(quarter(eb, 3), quarter(eb, 3),
                                    rple[:, 3 * NB:][:, None, :].to_broadcast([P, NT, NB]), ALU.mult).then_inc(ep_sb, 1)
            dve.wait_ge(row_rstd, M_PLE + 1)
            dve.wait_ge(ep_sb, 4)
            for u in range(4):
                for t in range(NT):
                    nc.vector.scalar_tensor_tensor(out=quarter(eb, u)[:, t], in0=quarter(eb, u)[:, t],
                                                   scalar=rstd[:, M_PLE, t:t + 1], in1=quarter(H, u)[:, t],
                                                   op0=ALU.mult, op1=ALU.add).then_inc(out_sb, 1)

        @block.tensor
        def _(pe):
            mm = nc.tensor.matmul

            def chunk_a(q, j, kt, hi, lo, bank, last):
                s = j % RING
                pe.wait_ge(lo_done, q * RING + (RING + j + 1))
                for k in range(KPC):
                    for t in range(NT):
                        out, tok = PS[:, bank + t], slice(t * P, (t + 1) * P)
                        mm(out, hi[:, kt + k, tok], whi[:, s, k], start=kt + k == 0, stop=False)
                        mm(out, hi[:, kt + k, tok], wlo[:, s, k], start=False, stop=False)
                        ins = mm(out, lo[:, kt + k, tok], whi[:, s, k], start=False, stop=last and k == KPC - 1)
                ins.then_inc(multiplied, 1)

            def chunk_b(q, j, kt, bank, last):
                s = j % RING
                pe.wait_ge(lo_done, q * RING + (RING + j + 1))
                for k in range(KPC):
                    for c in range(QT):
                        w = slice(c * P, (c + 1) * P)
                        end = last and k == KPC - 1
                        mm(half(bank, c), whi[:, s, k, w], aH[:, kt + k], start=kt + k == 0 and c % 2 == 0, stop=False,
                           skip_group_check=True)
                        mm(half(bank, c), whi[:, s, k, w], aL[:, kt + k], start=False, stop=False, skip_group_check=True)
                        ins = mm(half(bank, c), wlo[:, s, k, w], aH[:, kt + k], start=False, stop=end,
                                 skip_group_check=True)
                ins.then_inc(multiplied, 1)

            def transpose_tiles(src, bank=6):
                for c in range(QT):
                    for t in range(NT):
                        ins = nc.tensor.transpose(half(bank, c)[:, t * P:(t + 1) * P], src[:, t, c * P:(c + 1) * P], ident)
                    if c % 2:
                        ins.then_inc(t_ps, 1)

            def quarter(v, b):
                return v[:, :, b * NB:(b + 1) * NB]

            def spread(use, u, src, ready, value):
                pe.wait_ge(ready, value)
                if use + u > 1:
                    pe.wait_ge(t_lo, (use + u - (1 if u else 0)) * QT)
                transpose_tiles(quarter(src, u), 6 - 2 * (u % 2))

            pe.sem_inc(multiplied, RING)
            pe.wait_ge(con_in, 32)
            spread(T_N1, 0, H, x_in[0], 16)
            spread(T_N1, 1, H, x_in[1], 16)

            def head_tail(i):
                pe.wait_ge(oz_sb, i + 1)
                transpose_tiles(oR)

            def head(i, first):
                q = i * (R_PER // RING) + R_AT // RING
                for j in range(R_PER):
                    if first and j in (0, 2, 4, 6):
                        if j in (2, 4):
                            spread(T_N1, j // 2 + 1, H, x_in[j // 2 + 1], 16)
                        pe.wait_ge(t_lo, (T_N1 + j // 2 + 1) * QT)
                    chunk_a(q, j, (j % K16) * KPC, aH, aL, 2 * (j // K16), j % K16 == K16 - 1)
                    if not first and j == 1:
                        head_tail(i - 1)
                    if j == 11:
                        pe.wait_ge(rope_done, i * 2 + 2)
                        if first:
                            pe.wait_ge(t_lo, T_R * QT)
                        else:
                            pe.wait_ge(t_lo, i * QT + T_R * QT)
                        for e in range(4):
                            for t in range(NT):
                                at = (e % 2) * SEQ + t * P
                                ins = nc.tensor.transpose(PS[:, 6 + e // 2, at:at + P], roped[:, t, e // 2, e % 2], ident)
                        ins.then_inc(qkT_ps, 1)
                    if j == 15:
                        pe.wait_ge(qkT_sb, i + 1)
                        for h in range(2):
                            mm(PS[:, 6, 0:SEQ], qkT[:, 1, h, 0:P], qkT[:, 0, h, :], start=h == 0, stop=h == 1,
                               skip_group_check=True)
                            ins = mm(PS[:, 6, SEQ:3 * P], qkT[:, 1, h, P:SEQ], qkT[:, 0, h, P:SEQ], start=False,
                                     stop=h == 1, skip_group_check=True)
                        ins.then_inc(sT_ps, 1)
                    if j == 19:
                        pe.wait_ge(sT_sb, i * 3 + 3)
                        for bank, at, t, first_t in ((6, 0, 0, True), (7, P, 0, True), (7, SEQ, 1, False)):
                            key = slice(at, at + P)
                            mm(PS[:, bank], sTH[:, key], vH[:, t], start=first_t, stop=False)
                            mm(PS[:, bank], sTH[:, key], vL[:, t], start=False, stop=False)
                            ins = mm(PS[:, bank], sTL[:, key], vH[:, t], start=False, stop=bank == 6 or t == 1)
                        ins.then_inc(o_ps, 1)

            head(0, True)
            with pe.Fori(1, R_N) as i:
                head(i, False)
            for b in range(4):
                q = (RO_AT + b * K32) // RING
                pe.wait_ge(h_out, b + 1)
                for j in range(K32):
                    if b == 0 and j == K32 - 2:
                        pe.wait_ge(t_lo, (T_R + R_N) * QT)
                    chunk_a(q, j, j * KPC, oH, oL, 2 * (b % 2), j == K32 - 1)
                    if b == 0 and j == 1:
                        head_tail(R_N - 1)
                    if b and j == 2:
                        pe.wait_ge(h_out, 2 + b)
                        pe.wait_ge(t_lo, (T_N2 + b - 1) * QT)
                        transpose_tiles(quarter(H, b - 1))

            def group(i, first):
                q = i * (P_PER // RING) + P_AT // RING
                for j in range(4 * K16):
                    b = j // K16
                    if j == 16 or j == 24:
                        pe.wait_ge(pu_lo, i * 2 + (b - 1))
                    if first and j == 6:
                        pe.wait_ge(t_lo, (T_N2 + 4) * QT)
                    chunk_a(q, j, (j % K16) * KPC, aH, aL, 2 * (b % 2), j % K16 == K16 - 1)
                    if j == 1:
                        if first:
                            pe.wait_ge(h_out, 2 + 4)
                            pe.wait_ge(t_lo, (T_N2 + 3) * QT)
                            transpose_tiles(quarter(H, 3))
                        else:
                            group_tail(i - 1, 1)
                    if j == 19:
                        pe.wait_ge(pu_lo, i * 2 + 2)
                        pe.wait_ge(pu_sb, i * 3 + 3)
                        for c in range(8):
                            out, ch = half(4, c), slice(c * P, (c + 1) * P)
                            mm(out, pUH[:, 0, ch], pMH[:, 0:SEQ], start=c % 2 == 0, stop=False, skip_group_check=True)
                            mm(out, pUL[:, 0, ch], pMH[:, 0:SEQ], start=False, stop=False, skip_group_check=True)
                            mm(out[:, P:], pUH[:, 1, ch], pMH[:, SEQ:], start=False, stop=False, skip_group_check=True)
                            ins = mm(out[:, P:], pUL[:, 1, ch], pMH[:, SEQ:], start=False, stop=True,
                                     skip_group_check=True)
                            if c % 2:
                                ins.then_inc(mix_ps, 1)
                pe.wait_ge(mix_lo, i * 4 + 4)
                for w in range(2):
                    pe.wait_ge(pz_sb, i * 2 + (w + 1))
                    for k in range(4):
                        chunk_a(q, 4 * K16 + 4 * w + k, k * KPC, mH, mL, 2 * w, k == 3)
                        if w == 1 and k == 2:
                            group_tail(i, 0)

            def group_tail(i, w):
                pe.wait_ge(mz_sb, i * 2 + (w + 1))
                pe.wait_ge(t_lo, i * (2 * QT) + (T_P + w) * QT)
                transpose_tiles(mz)

            group(0, True)
            with pe.Fori(1, P_N) as i:
                group(i, False)
            for b in range(4):
                q = (PO_AT + b * K32) // RING
                pe.wait_ge(h_out, 4 + b + 1)
                for j in range(K32):
                    if b == 0 and j == K32 - 2:
                        pe.wait_ge(t_lo, (T_P + 8) * QT)
                    chunk_a(q, j, j * KPC, oH, oL, 2 * (b % 2), j == K32 - 1)
                    if b == 0 and j == 1:
                        group_tail(P_N - 1, 1)

            def norm3(u):
                spread(T_N3, u, XS, rows_sb, NT * (u + 1))

            norm3(0)
            norm3(1)

            def by_head(bank, lhsT, rhs, tiles=range(NT), part=None):
                for n, t in enumerate(tiles):
                    for h in range(HG):
                        out, moving = PS[:, bank + n, h * P:(h + 1) * P], rhs(t, h)
                        if part:
                            out, moving = blocks(out, *part), blocks(moving, *part)
                        ins = mm(out, lhsT(t, h), moving, start=h == 0, stop=True, skip_group_check=True)
                return ins

            def turn(bank, src):
                for t in range(NT):
                    for h in range(HG):
                        ins = nc.tensor.transpose(PS[:, bank + t, h * P:(h + 1) * P], src(t, h), ident)
                return ins

            def squares(src, bank):
                for t in range(NT):
                    for h in range(HG):
                        ins = mm(PS[:, bank, t * HG + h:t * HG + h + 1], src[:, h * SEQ + t * P:h * SEQ + (t + 1) * P],
                                 ones[:, 0:1], start=t + h == 0, stop=True, skip_group_check=True)
                ins.then_inc(sq_ps, 1)

            def delta_tail(i, j):
                if j == 0:
                    pe.wait_ge(st_sb, i + 1)
                    pe.wait_ge(sqn_sb, i * 2 + 2)
                    by_head(5, lambda t, h: knT[:, t, h], lambda t, h: st[:, h], [1])
                    by_head(6, lambda t, h: kqv[:, 1, h, t * P:(t + 1) * P], lambda t, h: st[:, h], [1])
                    by_head(7, lambda t, h: qk[:, t, h], lambda t, h: vn[:, t, h], [0]).then_inc(r1_ps, 1)
                if j == 1:
                    pe.wait_ge(vb1_sb, i + 1)
                    by_head(4, lambda t, h: iU[:, t, h], lambda t, h: vb[:, t, h], [1]).then_inc(vn1_ps, 1)
                if j == 2:
                    pe.wait_ge(vn1_sb, i + 1)
                    by_head(5, lambda t, h: qk[:, t, h], lambda t, h: vn[:, t, h], [1]).then_inc(o1_ps, 1)
                if j == 6:
                    pe.wait_ge(od_sb, i + 1)
                    transpose_tiles(oD)

            def delta(i, first):
                q = i * (D_PER // RING) + D_AT // RING
                for j in range(D_PER):
                    b = j // K16
                    if j == 2 * K16 or j == 3 * K16:
                        pe.wait_ge(conv_tap, i * 48 + 16 * (b - 1))
                    if first and j in (0, 2, 4, 6):
                        if j in (2, 4):
                            norm3(j // 2 + 1)
                        pe.wait_ge(t_lo, (T_N3 + j // 2 + 1) * QT)
                    if b < 3:
                        chunk_b(q, j, (j % K16) * KPC, 2 * (b % 2), j % K16 == K16 - 1)
                    else:
                        chunk_a(q, j, (j % K16) * KPC, aH, aL, 2 * (b % 2), j % K16 == K16 - 1)
                    if not first:
                        delta_tail(i - 1, j)
                    if first and j == 7:
                        pe.wait_ge(small_lo, 1)
                        for t in range(NT):
                            for k in range(16):
                                out, tok = PS[:, 4, t * 32:(t + 1) * 32], slice(t * P, (t + 1) * P)
                                mm(out, aH[:, k, tok], wbh[:, k], start=k == 0, stop=False)
                                mm(out, aH[:, k, tok], wbl[:, k], start=False, stop=False)
                                ins = mm(out, aL[:, k, tok], wbh[:, k], start=False, stop=k == 15)
                        ins.then_inc(ba_ps, 1)
                    if first and j == 8:
                        pe.wait_ge(gl_sb, 1)
                        for t in range(NT):
                            ins = mm(PS[:, 5, t * DN_HEADS:(t + 1) * DN_HEADS], upper, gl[:, t], start=True, stop=True)
                        ins.then_inc(cum_ps, 1)
                    if j == (9 if first else 6):
                        if first:
                            pe.wait_ge(cum_sb, 1)
                        pe.wait_ge(gu_sb, i * 2 + 1)
                        for t in range(NT):
                            ins = mm(PS[:, 4 + t], ones, gm[:, t].rearrange("p h n -> p (h n)"), start=True, stop=True)
                        ins.then_inc(gu_ps, 1)
                    if j == 11:
                        pe.wait_ge(kqv_sb, i * 3 + 2)
                        turn(6, lambda t, h: kqv[:, 0, h, t * P:(t + 1) * P]).then_inc(k_ps, 1)
                        pe.wait_ge(sq_sb, i * 2 + 1)
                        pe.wait_ge(dt_sub, i * 2 + 1)
                        squares(kb[:].rearrange("p t h n -> p (t h n)"), 4)
                    if j == 13:
                        pe.wait_ge(kn_sb, i + 1)
                        turn(4, lambda t, h: kn[:, t, h])
                        pe.wait_ge(kb_sb, i + 1)
                        turn(6, lambda t, h: kb[:, t, h]).then_inc(kt_ps, 1)
                    if j == 14:
                        pe.wait_ge(kt_sb, i * 2 + 2)
                        by_head(4, lambda t, h: knT[:, t, h], lambda t, h: kbT[:, t, h]).then_inc(a_ps, 1)
                    if j == 16:
                        pe.wait_ge(a_sb, i + 1)
                        turn(4, lambda t, h: iU[:, t, h]).then_inc(t0_ps, 1)
                    if 17 <= j <= 28:
                        lv = (j - 15) // 2
                        even, odd, final = (lv, 0), (lv, 1), lv == LEVELS - 1
                        if j % 2:
                            if lv == 1:
                                pe.wait_ge(t0_sb, i + 1)
                            else:
                                pe.wait_ge(tu_sb, i * (LEVELS - 1) + (lv - 1))
                            pe.wait_ge(lv_sb, i * (LEVELS - 1) + lv)
                            below = kbT if lv % 2 else kb
                            by_head(4, lambda t, h: below[:, t, h], lambda t, h: iT[:, t, h],
                                    part=None if final else even).then_inc(m1_ps, 1)
                            if lv > 1:
                                turn(6, lambda t, h: iT[:, t, h]).then_inc(iu_ps, 1)
                        else:
                            pe.wait_ge(m1_sb, i * (LEVELS - 1) + lv)
                            if lv > 1:
                                pe.wait_ge(iu_sb, i * (LEVELS - 2) + (lv - 1))
                            if final:
                                by_head(6, lambda t, h: gm[:, t, h], lambda t, h: iU[:, t, h], part=odd).then_inc(tu_ps, 1)
                            else:
                                by_head(4, lambda t, h: iU[:, t, h], lambda t, h: gm[:, t, h], part=even).then_inc(tu_ps, 1)
                    if j == 28:
                        pe.wait_ge(kqv_sb, i * 3 + 4)
                        turn(4, lambda t, h: kqv[:, 2, h, t * P:(t + 1) * P]).then_inc(v_ps, 1)
                    if j == 29:
                        pe.wait_ge(tu_sb, i * (LEVELS - 1) + (LEVELS - 1))
                        pe.wait_ge(kqv_sb, i * 3 + 3)
                        by_head(6, lambda t, h: knT[:, t, h],
                                lambda t, h: kqv[:, 1, h, t * P:(t + 1) * P]).then_inc(qk_ps, 1)
                    if j == 30:
                        pe.wait_ge(qk_sb, i + 1)
                        pe.wait_ge(sq_sb, i * 2 + 2)
                        squares(zD[:].rearrange("p t n -> p (t n)"), 6)
                        pe.wait_ge(vb_sb, i + 1)
                        by_head(7, lambda t, h: iU[:, t, h], lambda t, h: vb[:, t, h], [0]).then_inc(vn0_ps, 1)
                    if j == 31:
                        pe.wait_ge(vn0_sb, i + 1)
                        pe.wait_ge(ke_sb, i + 1)
                        by_head(4, lambda t, h: ke[:, h], lambda t, h: vn[:, t, h], [0]).then_inc(st_ps, 1)

            delta(0, True)
            with pe.Fori(1, D_N) as i:
                delta(i, False)

            def gated(i, first):
                q = i * (G_PER // RING) + G_AT // RING
                for j in range(G_PER):
                    b, k, last = j // K16, (j % K16) * KPC, j % K16 == K16 - 1
                    if k == 0:
                        if b < 2:
                            pe.wait_ge(g_read, i * 3 + (2 + b))
                            if b and first:
                                pe.wait_ge(zd_sb, D_N)
                        if b == 2:
                            pe.wait_ge(zb_sb, i + 1)
                        if b == 3:
                            pe.wait_ge(g_read, i * 3 + 4)
                            if first:
                                pe.wait_ge(t_lo, (T_D + D_N) * QT)
                    if b < 3:
                        chunk_b(q, j, k, 2 * b, last)
                    elif b == 3:
                        chunk_a(q, j, k, aH, aL, 0, last)
                    else:
                        chunk_a(q, j, k, oaH, oaL, 2, last)
                    if first:
                        delta_tail(D_N - 1, j)

            gated(0, True)
            with pe.Fori(1, G_N) as i:
                gated(i, False)

            def branch_tail(b):
                pe.wait_ge(ym_sb, b + 1)
                transpose_tiles(yl2, 2 * b)

            q = Y_AT // RING
            for j in range(8 * K16):
                b, k, last = j // K16, (j % K16) * KPC, j % K16 == K16 - 1
                if k == 0:
                    if b < 2:
                        pe.wait_ge(g_read, G_N * 3 + (2 + b))
                    elif b == 2:
                        pe.wait_ge(zb_sb, G_N + 1)
                    elif b == 3:
                        pe.wait_ge(mean_sb, 2)
                    else:
                        pe.wait_ge(gate_add, G_N + (b - 3))
                    if b == 4:
                        pe.wait_ge(ub_lo, 4)
                if b < 4:
                    chunk_a(q, j, k, aH, aL, 2 * b, last)
                else:
                    chunk_a(q, j, k, ubH, ubL, 2 * (b - 4), last)
                if j == LN_AT - 1:
                    for c in range(QT):
                        pe.wait_ge(long_tap[c], G_N * LONG)
                    for n in range(16):
                        ins = mm(PS[:, 6, 0:SEQ], ones, uT[:, n], start=n == 0, stop=n == 15)
                    ins.then_inc(mean_ps, 1)
                if j == LN_AT + 3:
                    for u in range(4):
                        pe.wait_ge(usq_sb, u + 1)
                        for c in range(QT):
                            ins = mm(PS[:, 7, 0:SEQ], ones, ln_tmp[u % 2][:, c * SEQ:(c + 1) * SEQ],
                                     start=u + c == 0, stop=u + c == 6)
                        ins.then_inc(usq_ps, 1)
                if j in (5 * K16 + 2, 6 * K16 + 2, 7 * K16 + 2):
                    branch_tail(b - 5)

            for b in range(4):
                q = (O_AT + b * K16) // RING
                if b < 2:
                    pe.wait_ge(t_lo, (T_Y + b + 1) * QT)
                else:
                    pe.wait_ge(row_sq[M_POST], NT * (b - 1))
                for j in range(K16):
                    if b == 0 and j == K16 - 2:
                        pe.wait_ge(t_lo, (T_Y + Y_N) * QT)
                    chunk_a(q, j, j * KPC, oaH, oaL, 2 * (b % 2), j == K16 - 1)
                    if b == 0 and j == 2:
                        branch_tail(Y_N - 1)
            def norm_x3(u):
                spread(T_X3, u, H, rows_sb, NT * (u + 5))

            pe.wait_ge(small_lo, 2)
            for j in range(E_PER):
                if j > 1:
                    pe.wait_ge(eb_sb, j - 1)
                else:
                    pe.wait_ge(row_sq[M_POST], NT * (3 + j))
                chunk_a(E_AT // RING, j, 0, pTh, pTl, 2 * (j % 2), True)
                if j > 1:
                    norm_x3(j - 2)
            for b in range(4):
                q = (PG_AT + b * K16) // RING
                if b < 2:
                    pe.wait_ge(eb_sb, 3 + b)
                else:
                    pe.wait_ge(sp_sb, b - 1)
                for j in range(K16):
                    if b == 0 and j in (0, 2, 4, 6):
                        if j in (2, 4):
                            norm_x3(j // 2 + 1)
                        pe.wait_ge(t_lo, (T_X3 + j // 2 + 1) * QT)
                    chunk_a(q, j, j * KPC, aH, aL, 2 * (b % 2), j == K16 - 1)


def constants():
    f8, f4 = np.float64, np.float32
    i, t = np.arange(P), np.arange(SEQ)
    con = np.zeros((P, 4, P), f4)
    con[:, 0] = np.eye(P)
    con[:, 1] = 1
    con[:, 2] = i[:, None] <= i[None, :]
    con[:, 3] = np.where(i[:, None] <= i[None, :], 0, -30000.0)

    inverse = np.power(f4(10000.0), -np.arange(HALF, dtype=f4) / f4(HALF)).astype(f4)
    angle = (t.astype(f4)[:, None] * inverse[None, :]).astype(f8)
    rot = np.stack([np.cos(angle), np.sin(angle)]).astype(f4)
    rot = rot.reshape(2, NT, P, HALF).transpose(2, 0, 1, 3)

    later = t[None, :] - t[:, None]
    log_decay = np.log1p(-np.exp2(-5.0 - np.arange(RET_HEADS, dtype=f8)))
    decay = np.where(later >= 0, np.exp(np.maximum(later, 0) * log_decay[:, None, None]), 0) * RET_QK ** -0.5
    dmask = np.concatenate([decay[:, :P], decay[:, P:, P:]], axis=2).transpose(1, 0, 2)

    pm, window = [], []
    for w in POOL_WINDOWS:
        size = np.minimum(t + 1, w)
        m = np.where((later >= 0) & (later < w), 1, 0) - np.eye(SEQ) * size[None, :]
        pm.append(np.concatenate([m[:P], m[P:, P:]], axis=1))
        window.append((1 / size).astype(f4).reshape(NT, P).T)

    lm = np.zeros((P, LEVELS, P), f4)
    for lv in range(LEVELS):
        b = i >> lv
        lm[:, lv] = (b[:, None] // 2 == b[None, :] // 2) & (b[:, None] % 2 == 0) & (b[None, :] % 2 == 1)
    return {"con": con, "rot": rot, "dmask": dmask.astype(f4), "pm": np.stack(pm).astype(f4), "lm": lm,
            "window": np.concatenate(window, axis=1)}


def chunks(w, columns):
    out = []
    for c in columns:
        block = np.concatenate([w[:, a:b] for a, b in c], axis=1) if isinstance(c, tuple) else w[:, c:c + NB]
        out.append(block.reshape(-1, KPC, P, NB).transpose(0, 2, 1, 3).reshape(-1, P, KPC * NB))
    return out


def stream(a):
    qk, v = RET_QK, 2 * DM
    w, out = a["ret_w_in"][0], []
    for h in range(RET_HEADS):
        out += chunks(w, [((h * qk, (h + 1) * qk), (DM + h * qk, DM + (h + 1) * qk)), v + h * NB, v + RET_V + h * NB])
    whole = range(0, DM, NB)
    out += chunks(a["ret_w_out"][0], whole)
    w = a["pool_w_in"][0]
    for g in range(GROUPS):
        u, z = g * GDIM, 2 * DM + g * GDIM
        out += chunks(w, [u, u + NB, z, z + NB]) + chunks(a["pool_w_grp"][0][g], [0, NB])
    out += chunks(a["pool_w_out"][0], whole)
    w = a["w_in_2"][0]
    z_a, glu = 3 * DM, 4 * DM + 2 * DN_HEADS
    z_b, gate = glu + 2 * DM, glu + 3 * DM
    for n in whole:
        out += chunks(w, [DM + n, n, 2 * DM + n, z_a + n])
    for n in whole:
        out += chunks(w, [glu + n, glu + DM + n, z_b + n, gate + n]) + chunks(a["w_br_a_2"][0], [n])
    out += chunks(w, [gate + DM + n for n in whole]) + chunks(a["w_br_b_2"][0], whole)
    for name in ("w_out_2", "w_ple_proj_2", "w_ple_gate_2"):
        out += chunks(a[name][0], whole)
    return np.concatenate(out)


def arrays_of(inputs):
    a = {k: np.asarray(v) for k, v in inputs.items()}

    def by_partition(v):
        return v.reshape(-1, P).T

    gates, shapes_only = 4 * DM, constants()
    arrays = {
        "x": a["x"][0],
        "stream": stream(a),
        "cols": np.concatenate([by_partition(a[k]) for k in (
            "ret_norm", "ret_gn", "pool_norm", "pool_scale", "g_pre_2", "g_dn_out_2", "ln_g_2", "ln_b_2",
            "b_dw_2")] + [shapes_only.pop("window")], axis=1),
        "pool_b": a["pool_b_grp"].reshape(GROUPS, 1, GDIM),
        "final_norm": a["final_norm"].reshape(1, DM),
        "w_ba": a["w_in_2"][0][:, gates:gates + 2 * DN_HEADS].reshape(16, P, 2 * DN_HEADS).transpose(1, 0, 2),
        "dt_bias": a["dt_bias_2"],
        "a_log": a["a_log_2"],
        "w_conv": a["w_conv_qkv_2"][0].reshape(TAPS, 48, P).transpose(2, 1, 0).reshape(P, -1),
        "w_long": a["w_dw_2"][0].reshape(LONG, 16, P).transpose(2, 1, 0).reshape(P, -1),
        "b_gate": a["b_gate_2"].reshape(8, 1, NB),
        "pT": a["p_2"][0, 0].reshape(SEQ, 2, P).transpose(2, 1, 0),
        "g_post": a["g_post_2"],
        "g_ple": a["g_ple_2"],
    }
    arrays.update(shapes_only)
    return {k: np.ascontiguousarray(v) for k, v in arrays.items()}


def kernel(**inputs):
    import concourse.bacc as bacc
    from concourse.bass_utils import run_bass_kernel_spmd

    nc = bacc.Bacc("TRN2", target_bir_lowering=False, num_devices=1)
    arrays, dram = {}, {}
    for name, a in arrays_of(inputs).items():
        arrays[f"in_{name}"] = a
        dram[name] = nc.dram_tensor(f"in_{name}", a.shape, mybir.dt.from_np(a.dtype), kind="ExternalInput").ap()
    dram["out"] = nc.dram_tensor("out_0", (SEQ, DM), F32, kind="ExternalOutput").ap()
    build(nc, dram)
    r = run_bass_kernel_spmd(nc, [arrays], core_ids=[0])
    return r.results[0]["out_0"].reshape(1, SEQ, DM)
```
